# Optimizing a Trainium2 kernel written in Bass

```python
import math
import jax, jax.numpy as jnp
from jax import lax
import numpy as np

D_MODEL = 1024
BATCH = 1
SEQ = 256
DEPTH = 2
DEC_BATCH = 8
DEC_SEQ = 1
PAST_LEN = 2048
PAGE_SIZE = 128

MIX_WIDTH = D_MODEL
HG_WIDTH = 3 * D_MODEL // 8
HG_DK = 64
HG_DV = 64
HG_HEADS = HG_WIDTH // HG_DV
RET_WIDTH = 3 * D_MODEL // 8
RET_DV = 64
RET_HEADS = RET_WIDTH // RET_DV
RET_DK = RET_DV // 2
RET_QK = RET_HEADS * RET_DK
S5_WIDTH = MIX_WIDTH - HG_WIDTH - RET_WIDTH
S5_GROUP = 16
S5_GROUPS = S5_WIDTH // S5_GROUP
S5_STATE = 64
D_FF = 4 * D_MODEL
IN_WIDTH = 4 * HG_WIDTH + 2 * RET_QK + 2 * RET_WIDTH + S5_WIDTH
CHUNK = 16
ROPE_BASE = 10000.0
EPS = 1e-5
ALPHA = (2.0 * DEPTH) ** 0.25
BETA = (8.0 * DEPTH) ** -0.25

kernel_name = "hymba_hgrn2_retnet_s5_deepnorm_step"

def _layer_norm(x, w, b):
    xf = x.astype(jnp.float32)
    mu = jnp.mean(xf, -1, keepdims=True)
    var = jnp.mean(jnp.square(xf - mu), -1, keepdims=True)
    return ((xf - mu) * lax.rsqrt(var + EPS) * w + b).astype(x.dtype)

def _rotary(x, pos):
    half = x.shape[-1] // 2
    inv = ROPE_BASE ** (-jnp.arange(half, dtype=jnp.float32) / half)
    ang = pos[:, None] * inv[None, :]
    cos = jnp.cos(ang)[:, None, :]
    sin = jnp.sin(ang)[:, None, :]
    x1, x2 = x[..., :half], x[..., half:]
    return jnp.concatenate([x1 * cos - x2 * sin, x1 * sin + x2 * cos], axis=-1)

def _chunked_gated_linear(q, k, v, log_f, s0):
    bsz, t, h, _ = q.shape
    dv = v.shape[-1]
    q, k, v, log_f = [a.astype(jnp.float32) for a in (q, k, v, log_f)]
    pad = (-t) % CHUNK
    if pad:
        cfg = ((0, 0), (0, pad), (0, 0), (0, 0))
        q, k, v, log_f = [jnp.pad(a, cfg) for a in (q, k, v, log_f)]
    n = (t + pad) // CHUNK

    def chunks(a):
        return a.reshape(bsz, n, CHUNK, h, a.shape[-1])

    q, k, v, log_f = chunks(q), chunks(k), chunks(v), chunks(log_f)
    b = jnp.cumsum(log_f, axis=2)
    causal = jnp.tril(jnp.ones((CHUNK, CHUNK), dtype=bool))[None, None, :, :, None, None]
    diff = b[:, :, :, None] - b[:, :, None, :]
    rel = jnp.where(causal, jnp.exp(jnp.where(causal, diff, 0.0)), 0.0)
    scores = jnp.einsum('bntshk,bnthk,bnshk->bnhts', rel, q, k)
    o_intra = jnp.einsum('bnhts,bnshv->bnthv', scores, v)
    q_dec = q * jnp.exp(b)
    k_dec = k * jnp.exp(b[:, :, -1:] - b)
    chunk_decay = jnp.exp(b[:, :, -1])

    def step(state, inp):
        qd, kd, vc, cd = inp
        o = jnp.einsum('bthk,bhkv->bthv', qd, state)
        state = cd[..., None] * state + jnp.einsum('bshk,bshv->bhkv', kd, vc)
        return state, o

    xs = tuple(jnp.moveaxis(a, 1, 0) for a in (q_dec, k_dec, v, chunk_decay))
    s_final, o_inter = lax.scan(step, s0.astype(jnp.float32), xs)
    o = o_intra + jnp.moveaxis(o_inter, 0, 1)
    o = o.reshape(bsz, n * CHUNK, h, dv)[:, :t]
    return o, s_final.astype(s0.dtype)

def _s5_combine(e1, e2):
    a1r, a1i, b1r, b1i = e1
    a2r, a2i, b2r, b2i = e2
    return (a2r * a1r - a2i * a1i,
            a2r * a1i + a2i * a1r,
            a2r * b1r - a2i * b1i + b2r,
            a2r * b1i + a2i * b1r + b2i)

def _s5_scan(u, log_dt, a_re, a_im, b_re, b_im, c_re, c_im, d, x0_re, x0_im):
    bsz, t, _ = u.shape
    f32 = jnp.float32
    uf = u.astype(f32).reshape(bsz, t, S5_GROUPS, S5_GROUP)
    a_re, a_im = a_re.astype(f32), a_im.astype(f32)
    dt = jnp.exp(log_dt.astype(f32))[:, None]
    mag = jnp.exp(dt * a_re)
    ab_re = mag * jnp.cos(dt * a_im)
    ab_im = mag * jnp.sin(dt * a_im)
    den = a_re * a_re + a_im * a_im
    nr = ab_re - 1.0
    g_re = (nr * a_re + ab_im * a_im) / den
    g_im = (ab_im * a_re - nr * a_im) / den
    b_re, b_im = b_re.astype(f32), b_im.astype(f32)
    bb_re = g_re[..., None] * b_re - g_im[..., None] * b_im
    bb_im = g_re[..., None] * b_im + g_im[..., None] * b_re
    bu_re = jnp.einsum('btgc,gnc->btgn', uf, bb_re)
    bu_im = jnp.einsum('btgc,gnc->btgn', uf, bb_im)
    x0r, x0i = x0_re.astype(f32), x0_im.astype(f32)
    bu_re = bu_re.at[:, 0].add(ab_re * x0r - ab_im * x0i)
    bu_im = bu_im.at[:, 0].add(ab_re * x0i + ab_im * x0r)
    ar = jnp.broadcast_to(ab_re, bu_re.shape)
    ai = jnp.broadcast_to(ab_im, bu_re.shape)
    _, _, xr, xi = lax.associative_scan(_s5_combine, (ar, ai, bu_re, bu_im), axis=1)
    y = (jnp.einsum('gcn,btgn->btgc', c_re.astype(f32), xr)
         - jnp.einsum('gcn,btgn->btgc', c_im.astype(f32), xi))
    y = y.reshape(bsz, t, S5_WIDTH) + d * uf.reshape(bsz, t, S5_WIDTH)
    return y, xr[:, -1].astype(x0_re.dtype), xi[:, -1].astype(x0_im.dtype)

def _layer(x, pos, s_hg, s_rt, s_re, s_im, w_in, lb, hg_norm_w, ret_norm_w,
           s5_log_dt, s5_a_re, s5_a_im, s5_b_re, s5_b_im, s5_c_re, s5_c_im, s5_d,
           s5_glu_w, s5_glu_b, w_out, ln1_w, ln1_b, w_up, w_down, ln2_w, ln2_b):
    f32 = jnp.float32
    bsz, t, _ = x.shape
    proj = jnp.einsum('btd,de->bte', x, w_in)
    sizes = [HG_WIDTH] * 4 + [RET_QK] * 2 + [RET_WIDTH] * 2 + [S5_WIDTH]
    cuts = [int(c) for c in np.cumsum(sizes)[:-1]]
    hq, hf, hi, hg, rq, rk, rv, rg, su = jnp.split(proj, cuts, axis=-1)

    def heads(a, nh):
        return a.reshape(bsz, t, nh, -1)

    lbf = lb.astype(f32)
    zf = hf.astype(f32)
    f_gate = lbf + (1.0 - lbf) * jax.nn.sigmoid(zf)
    log_f = jnp.log(f_gate)
    k_hg = (1.0 - lbf) * jax.nn.sigmoid(-zf)
    o_hg, s_hg_new = _chunked_gated_linear(heads(jax.nn.silu(hq), HG_HEADS), heads(k_hg, HG_HEADS),
                                           heads(hi, HG_HEADS), heads(log_f, HG_HEADS), s_hg)
    o_hg = o_hg * lax.rsqrt(jnp.mean(jnp.square(o_hg), -1, keepdims=True) + EPS)
    o_hg = o_hg * hg_norm_w * jax.nn.silu(heads(hg, HG_HEADS).astype(f32))
    o_hg = o_hg.reshape(bsz, t, HG_WIDTH)

    q_r = _rotary(heads(rq, RET_HEADS).astype(f32), pos)
    k_r = _rotary(heads(rk, RET_HEADS).astype(f32), pos) * (RET_DK ** -0.5)
    log_gamma = jnp.log1p(-jnp.exp2(-5.0 - jnp.arange(RET_HEADS, dtype=f32)))
    log_f_r = jnp.broadcast_to(log_gamma[:, None], (bsz, t, RET_HEADS, RET_DK))
    o_rt, s_rt_new = _chunked_gated_linear(q_r, k_r, heads(rv, RET_HEADS), log_f_r, s_rt)
    mu = jnp.mean(o_rt, -1, keepdims=True)
    var = jnp.mean(jnp.square(o_rt - mu), -1, keepdims=True)
    o_rt = (o_rt - mu) * lax.rsqrt(var + EPS) * ret_norm_w.reshape(RET_HEADS, RET_DV)
    o_rt = o_rt * jax.nn.silu(heads(rg, RET_HEADS).astype(f32))
    o_rt = o_rt.reshape(bsz, t, RET_WIDTH)

    y5, s_re_new, s_im_new = _s5_scan(su, s5_log_dt, s5_a_re, s5_a_im, s5_b_re, s5_b_im,
                                      s5_c_re, s5_c_im, s5_d, s_re, s_im)
    y5 = jax.nn.gelu(y5)
    y5 = y5 * jax.nn.sigmoid(y5 @ s5_glu_w + s5_glu_b)

    mixed = jnp.concatenate([o_hg, o_rt, y5], axis=-1).astype(x.dtype) @ w_out
    x = _layer_norm(ALPHA * x + mixed, ln1_w, ln1_b)
    ff = jnp.square(jax.nn.relu(x @ w_up)) @ w_down
    x = _layer_norm(ALPHA * x + ff, ln2_w, ln2_b)
    return x, s_hg_new, s_rt_new, s_re_new, s_im_new

def setup_inputs(seed: int = 0) -> dict:
    key = jax.random.key(seed)
    ks = jax.random.split(key, 32)
    f32 = jnp.float32

    def nrm(k, shape, scale):
        return scale * jax.random.normal(k, shape, f32)

    n_idx = jnp.arange(S5_STATE, dtype=f32)
    return {
        "x_prompt": nrm(ks[0], (BATCH, SEQ, D_MODEL), 1.0),
        "x_sample": nrm(ks[1], (DEC_BATCH, DEC_SEQ, D_MODEL), 1.0),
        "state_hgrn": nrm(ks[2], (DEPTH, DEC_BATCH, HG_HEADS, HG_DK, HG_DV), 0.3),
        "state_ret": nrm(ks[3], (DEPTH, DEC_BATCH, RET_HEADS, RET_DK, RET_DV), 1.0),
        "state_s5_re": nrm(ks[4], (DEPTH, DEC_BATCH, S5_GROUPS, S5_STATE), 0.3),
        "state_s5_im": nrm(ks[5], (DEPTH, DEC_BATCH, S5_GROUPS, S5_STATE), 0.3),
        "w_in": nrm(ks[6], (DEPTH, D_MODEL, IN_WIDTH), D_MODEL ** -0.5),
        "hgrn_lb_logits": nrm(ks[7], (DEPTH, HG_WIDTH), 0.1),
        "hgrn_norm_w": 1.0 + nrm(ks[8], (DEPTH, HG_DV), 0.02),
        "ret_norm_w": 1.0 + nrm(ks[9], (DEPTH, RET_WIDTH), 0.02),
        "s5_log_dt": jax.random.uniform(ks[10], (DEPTH, S5_GROUPS), f32, math.log(1e-3), math.log(1e-1)),
        "s5_a_re": -0.5 + nrm(ks[11], (DEPTH, S5_GROUPS, S5_STATE), 0.01),
        "s5_a_im": math.pi * n_idx + nrm(ks[12], (DEPTH, S5_GROUPS, S5_STATE), 0.01),
        "s5_b_re": nrm(ks[13], (DEPTH, S5_GROUPS, S5_STATE, S5_GROUP), (2 * S5_GROUP) ** -0.5),
        "s5_b_im": nrm(ks[14], (DEPTH, S5_GROUPS, S5_STATE, S5_GROUP), (2 * S5_GROUP) ** -0.5),
        "s5_c_re": nrm(ks[15], (DEPTH, S5_GROUPS, S5_GROUP, S5_STATE), (2 * S5_STATE) ** -0.5),
        "s5_c_im": nrm(ks[16], (DEPTH, S5_GROUPS, S5_GROUP, S5_STATE), (2 * S5_STATE) ** -0.5),
        "s5_d": nrm(ks[17], (DEPTH, S5_WIDTH), 0.5),
        "s5_glu_w": nrm(ks[18], (DEPTH, S5_WIDTH, S5_WIDTH), S5_WIDTH ** -0.5),
        "s5_glu_b": nrm(ks[19], (DEPTH, S5_WIDTH), 0.01),
        "w_out": nrm(ks[20], (DEPTH, MIX_WIDTH, D_MODEL), BETA * MIX_WIDTH ** -0.5),
        "ln1_w": 1.0 + nrm(ks[21], (DEPTH, D_MODEL), 0.02),
        "ln1_b": nrm(ks[22], (DEPTH, D_MODEL), 0.02),
        "w_up": nrm(ks[23], (DEPTH, D_MODEL, D_FF), D_MODEL ** -0.5),
        "w_down": nrm(ks[24], (DEPTH, D_FF, D_MODEL), BETA * D_FF ** -0.5),
        "ln2_w": 1.0 + nrm(ks[25], (DEPTH, D_MODEL), 0.02),
        "ln2_b": nrm(ks[26], (DEPTH, D_MODEL), 0.02),
    }

def reference(x_prompt, x_sample, state_hgrn, state_ret, state_s5_re, state_s5_im,
              w_in, hgrn_lb_logits, hgrn_norm_w, ret_norm_w, s5_log_dt, s5_a_re, s5_a_im,
              s5_b_re, s5_b_im, s5_c_re, s5_c_im, s5_d, s5_glu_w, s5_glu_b, w_out,
              ln1_w, ln1_b, w_up, w_down, ln2_w, ln2_b):
    f32 = jnp.float32
    lb_prob = jax.nn.softmax(hgrn_lb_logits.astype(f32), axis=0)
    lower_bounds = jnp.cumsum(lb_prob, axis=0) - lb_prob[0:1]

    bp, tp, _ = x_prompt.shape
    pos_p = jnp.arange(tp, dtype=f32)
    pos_s = PAST_LEN + jnp.arange(x_sample.shape[1], dtype=f32)
    zero_hg = jnp.zeros((bp, HG_HEADS, HG_DK, HG_DV), f32)
    zero_rt = jnp.zeros((bp, RET_HEADS, RET_DK, RET_DV), f32)
    zero_s5 = jnp.zeros((bp, S5_GROUPS, S5_STATE), f32)

    yp, ys = x_prompt, x_sample
    hg_p, rt_p, re_p, im_p = [], [], [], []
    hg_s, rt_s, re_s, im_s = [], [], [], []
    for l in range(DEPTH):
        params = (w_in[l], lower_bounds[l], hgrn_norm_w[l], ret_norm_w[l], s5_log_dt[l],
                  s5_a_re[l], s5_a_im[l], s5_b_re[l], s5_b_im[l], s5_c_re[l], s5_c_im[l],
                  s5_d[l], s5_glu_w[l], s5_glu_b[l], w_out[l], ln1_w[l], ln1_b[l],
                  w_up[l], w_down[l], ln2_w[l], ln2_b[l])
        yp, a, b, c, d = _layer(yp, pos_p, zero_hg, zero_rt, zero_s5, zero_s5, *params)
        ys, e, f, g, h = _layer(ys, pos_s, state_hgrn[l], state_ret[l], state_s5_re[l],
                                state_s5_im[l], *params)
        hg_p.append(a); rt_p.append(b); re_p.append(c); im_p.append(d)
        hg_s.append(e); rt_s.append(f); re_s.append(g); im_s.append(h)

    new_hgrn_prompt = jnp.stack(hg_p)
    new_ret_prompt = jnp.stack(rt_p)
    new_s5_re_prompt = jnp.stack(re_p)
    new_s5_im_prompt = jnp.stack(im_p)
    new_hgrn_sample = jnp.stack(hg_s)
    new_ret_sample = jnp.stack(rt_s)
    new_s5_re_sample = jnp.stack(re_s)
    new_s5_im_sample = jnp.stack(im_s)
    return (yp, ys, new_hgrn_prompt, new_ret_prompt, new_s5_re_prompt, new_s5_im_prompt,
            new_hgrn_sample, new_ret_sample, new_s5_re_sample, new_s5_im_sample)


_drawn_inputs = setup_inputs


def setup_inputs(seed=0):
    import zlib

    import numpy as np

    out = dict(_drawn_inputs(seed))
    spreads = {}
    factors = {'hgrn_norm_w': 8.0,
     'ret_norm_w': 8.0,
     's5_a_re': 4.826,
     's5_c_re': 3.554,
     's5_c_im': 3.551,
     's5_glu_w': 7.285,
     's5_glu_b': 8.0}
    for name, (base, spread) in spreads.items():
        noise = np.random.default_rng([zlib.crc32(name.encode()), seed]).standard_normal(out[name].shape)
        drawn = base * np.exp(spread * noise) if base else spread * noise
        out[name] = __import__('jax').numpy.asarray(drawn.astype(out[name].dtype))
    for name, factor in factors.items():
        out[name] = (out[name] * factor).astype(out[name].dtype)
    return out
```

```python
from contextlib import ExitStack

import numpy as np

import concourse.bass as bass
from concourse import mybir

ALU = mybir.AluOpType
ACT = mybir.ActivationFunctionType
F32 = mybir.dt.float32
U8 = mybir.dt.uint8

DEPTH = 2
D_MODEL = 1024
SEQ = 256
NSAMP = 8
PAST_LEN = 2048
T = SEQ + NSAMP
KT = D_MODEL // 128
HEADS = 6
DV = 64
HG_FT = HEADS * DV // 128
RET_DK = 32
S5_TILES = 8
FF_TILES = 32
EPS = 1e-5
ALPHA = (2.0 * DEPTH) ** 0.25
LEVELS = 8
ROPE_BASE = 10000.0
GELU_C0 = 2.0 * (2.0 / np.pi) ** 0.5
GELU_C1 = GELU_C0 * 0.044715

SU, HF, HQ, HI, RQ, RK, RV, HGT, RG = 0, 2, 5, 8, 11, 13, 15, 18, 21
N_IN, N_OUT, N_UP, N_DOWN = 24, KT, FF_TILES, KT
OUT0 = N_IN
UP0 = OUT0 + N_OUT
DOWN0 = UP0 + N_UP
N_STREAM = DOWN0 + N_DOWN
STREAM_BANKS = 4
CHUNK = 16 * 128
RING = 5
N_CHUNKS = DOWN0 // 2 + 2 * N_DOWN

PV = {}
_at = 0
for _name, _n in (("log_dt", 8), ("a_re", 8), ("a_im", 8), ("d", 2), ("glu_b", 2), ("hg_norm", 1), ("ret_norm", 3),
                  ("ln1_w", 8), ("ln1_b", 8), ("ln2_w", 8), ("ln2_b", 8), ("logits", 3)):
    PV[_name] = (_at, _n)
    _at += _n
N_PV = _at
CV = {}
_at = 0
for _name, _n in (("ident", 128), ("head_mean", 128), ("model_mean", 128), ("cos_q", T), ("sin_q", T), ("cos_k", T),
                  ("sin_k", T), ("decay", HEADS * 256), ("k_decay", 512), ("gamma", 2), ("eps", 1), ("sample_row", 1)):
    CV[_name] = (_at, _n)
    _at += _n
N_CV = _at
MATS = 512 + 512 + 512

UNIT_ORDER = []
PLAN = {i: [] for i in range(-1, N_STREAM)}


def _plan(after, *names):
    for n in names:
        PLAN[after].append(n)


for _j, _a in enumerate((1, 1, 3, 4, 5, 7, 8, 9)):
    _plan(_a, ("s5_in", _j))
_plan(9, ("s5_in_sample",))
for _j, _a in enumerate((4, 6, 7, 8, 9, 11, 12, 13)):
    _plan(_a, ("s5_out", _j))
_plan(11, ("tr_hi", 0), ("tr_hi", 1), ("tr_hi_sample",))
_plan(13, ("tr_hk_sample",))
for _L in range(-1, 7):
    _plan(14 + _L, *[("hg_level", _L, ft) for ft in range(3)])
_plan(21, *[("hg_far", h) for h in range(2)], ("s5_out_sample",))
_plan(22, ("tr_hkd", 0), ("tr_hkd", 1), ("hg_state",), *[("hg_kv", ft) for ft in range(3)])
_plan(23, *[("ret_score", h) for h in range(HEADS)], ("tr_rv", 0), ("tr_rv", 1), ("tr_rv_sample",), ("tr_rk", 0), ("tr_rk", 1), ("tr_rk_sample",),
      ("ret_state",), ("ret_kv", 0), ("ret_kv", 1),
      *[("hg_o", ft) for ft in range(3)], *[("ret_o", ft) for ft in range(3)],
      ("glu", 0), ("glu", 1),
      *[("hg_ms", ft) for ft in range(3)], *[("ret_mu", ft) for ft in range(3)], *[("ret_var", ft) for ft in range(3)])
_plan(OUT0 + N_OUT - 1, ("ln1_mu",), ("ln1_var",))
_plan(DOWN0 + N_DOWN - 1, ("ln2_mu",), ("ln2_var",))
for _i in range(-1, N_STREAM):
    UNIT_ORDER += [u for u in PLAN[_i] if u[0] != "s5_out"]
UNIT_AT = {u: n for n, u in enumerate(UNIT_ORDER)}
N_UNITS = len(UNIT_ORDER)
MIX_BANKS = 3
NEAR_PARTS = [[(0, f, t) for f in (0, 1) for t in (0, 1)], [(1, f, t) for f in (0, 1) for t in (0, 1)],
              [(h, 2, t) for h in (0, 1) for t in (0, 1)]]


def chunk_of(tile):
    return tile // 2 if tile < DOWN0 else DOWN0 // 2 + 2 * (tile - DOWN0)


def last_tile(chunk):
    return 2 * chunk + 1 if chunk < DOWN0 // 2 else DOWN0 + (chunk - DOWN0 // 2) // 2


def build(nc, xT, weights, vectors, matrices, constants, level_masks, state_hg, state_rt, state_s5,
          y_out, hg_p_out, rt_p_out, s5_p_out, hg_s_out, rt_s_out, s5_s_out):
    with ExitStack() as ctx:
        def sb(name, shape, dt=F32):
            return ctx.enter_context(nc.sbuf_tensor(name, shape, dt))

        def sem(name):
            return ctx.enter_context(nc.semaphore(name))

        ring = sb("ring", [128, RING, CHUNK])
        X = sb("X", [128, KT, T])
        X1 = sb("X1", [128, KT, T])
        SQ = sb("SQ", [128, KT, T])
        MIX = sb("MIX", [128, KT, T])
        H = sb("H", [128, FF_TILES, T])
        rot = sb("rot", [128, 2, S5_TILES, SEQ])
        U = sb("U", [128, 2, T])
        Kg = sb("Kg", [128, HG_FT, T])
        Qg = sb("Qg", [128, HG_FT, T])
        Fg = sb("Fg", [128, HG_FT, SEQ])
        Fs = sb("Fs", [128, HG_FT, NSAMP])
        V_tok = sb("V_tok", [128, 2, 2, 384])
        near = sb("near", [128, 2, HG_FT, 2, 128])
        gates = sb("gates", [128, 6, T])
        QR = sb("QR", [128, 2, T])
        KR = sb("KR", [128, 2, T])
        S_hg = sb("S_hg", [128, HG_FT, NSAMP, DV])
        S_rt = sb("S_rt", [128, 2, NSAMP, DV])
        v_own = sb("v_own", [NSAMP, 2, NSAMP, 128])
        vs_tok = sb("vs_tok", [NSAMP, 2, 384])
        ks_tok = sb("ks_tok", [NSAMP, 640])
        consts = sb("consts", [128, N_CV])
        masks = sb("masks", [128, LEVELS, 128], U8)
        vecs = sb("vecs", [128, DEPTH, N_PV])
        mats = sb("mats", [128, MATS])
        s5x0 = sb("s5x0", [128, DEPTH, 2, S5_TILES, NSAMP])
        Cg = sb("Cg", [128, S5_TILES, 2, 32])
        Cs = sb("Cs", [128, S5_TILES, 32])
        s5xs = sb("s5xs", [128, 2, S5_TILES, NSAMP])
        s5tmp = sb("s5tmp", [128, 2, S5_TILES, NSAMP])
        s5fin = sb("s5fin", [128, 2, S5_TILES])
        s5last = sb("s5last", [128, 2, S5_TILES])
        par = sb("par", [128, 24, S5_TILES])
        low = sb("low", [128, 8, HG_FT])
        st_p = sb("st_p", [128, 5, DV])

        Hf = H[:, :, :].rearrange("p a b -> p (a b)")
        P1, P2, W5, Z5 = (Hf[:, 512 * i:512 * i + 512] for i in range(4))
        XS = [Hf[:, 2048 + 512 * i:2560 + 512 * i] for i in range(2)]
        kt_hg = Hf[:, 0:768].rearrange("p (a b) -> p a b", a=2)
        far = Hf[:, 768:1536].rearrange("p (a b c) -> p a b c", a=2, b=3)
        kt_rt = Hf[:, 1536:2048].rearrange("p (a b) -> p a b", a=2)
        qdec = [Hf[:, 3072 + 1536 * i:3840 + 1536 * i].rearrange("p (a b) -> p a b", a=3) for i in range(2)]
        kdec = [Hf[:, 3840 + 1536 * i:4608 + 1536 * i].rearrange("p (a b) -> p a b", a=3) for i in range(2)]
        masks_f32 = Hf[:, 6144:7168].rearrange("p (a b) -> p a b", a=LEVELS)
        RS = Hf[:, 6144:8448].rearrange("p (a b) -> p a b", a=HEADS)
        sig_f, sig_n = X1[:, 0:3, :], X1[:, 3:6, :]
        gel = X1[:, 6:8, :]
        Gg = X1[:, 3:6, :].rearrange("p a b -> p (a b)")[:, 0:3 * SEQ].rearrange("p (a b) -> p a b", a=3)
        RQraw, RKraw = SQ[:, 0:2, :], SQ[:, 2:4, :]
        swq, swk = SQ[:, 4:6, :], SQ[:, 6:8, :]
        Vf = MIX[:, 0:6, :]
        Y = MIX[:, 6:8, :]

        def cv(name):
            a, n = CV[name]
            return consts[:, a:a + n]

        def pv(l, name):
            a, n = PV[name]
            return vecs[:, l, a:a + n]

        ident = cv("ident")
        decay = cv("decay").rearrange("p (h t) -> p h t", h=HEADS)
        k_decay = cv("k_decay").rearrange("p (a b) -> p a b", a=2)
        B_s5 = mats[:, 0:512].rearrange("p (s r n) -> p s r n", s=2, r=2)
        C_s5 = mats[:, 512:1024].rearrange("p (j r c) -> p j r c", j=8, r=2)
        glu_w = mats[:, 1024:1536].rearrange("p (k m) -> p k m", k=2)

        stream_bank = [ctx.enter_context(nc.psum_tensor(f"stream{i}", [128, 512], F32)) for i in range(STREAM_BANKS)]
        mix_bank = [ctx.enter_context(nc.psum_tensor(f"mix{i}", [128, 512], F32)) for i in range(MIX_BANKS)]
        y5_bank = ctx.enter_context(nc.psum_tensor("y5_bank", [128, 2, 256], F32))

        w_loaded = [sem(f"w_loaded{i}") for i in range(RING)]
        x_loaded, const_loaded, mats_loaded, states_loaded = sem("x_loaded"), sem("const_loaded"), sem("mats_loaded"), sem("states_loaded")
        tile_done = sem("tile_done")
        tile_free = [sem(f"tile_free{i}") for i in range(STREAM_BANKS)]
        unit_done = sem("unit_done")
        unit_free = [sem(f"unit_free{i}") for i in range(MIX_BANKS)]
        row_tile_done = sem("row_tile_done")
        y5_done, y5_free = sem("y5_done"), sem("y5_free")
        u_ready = sem("u_ready")
        sig_ready = sem("sig_ready")
        qsig_ready = sem("qsig_ready")
        gsig_ready = sem("gsig_ready")
        v_ready = sem("v_ready")
        rqk_ready = sem("rqk_ready")
        vtok_ready = sem("vtok_ready")
        vs_ready = sem("vs_ready")
        ks_ready = sem("ks_ready")
        vown_ready = sem("vown_ready")
        kt_ready = sem("kt_ready")
        ktr_ready = sem("ktr_ready")
        far_ready = sem("far_ready")
        o_ready = sem("o_ready")
        oret_ready = sem("oret_ready")
        var_ready = sem("var_ready")
        hrms_ready = sem("hrms_ready")
        rrms_ready = sem("rrms_ready")
        gel_ready = sem("gel_ready")
        act_params = sem("act_params")
        softmax_exp = sem("softmax_exp")
        lnsq_ready = sem("lnsq_ready")
        lnsd_ready = sem("lnsd_ready")
        relu_ready = sem("relu_ready")
        act_step = sem("act_step")
        stp_ready = sem("stp_ready")

        dve_step = sem("dve_step")
        par_ready = sem("par_ready")
        table_ready = sem("table_ready")
        xs_ready = sem("xs_ready")
        xss_ready = sem("xss_ready")
        hq_ready = sem("hq_ready")
        dec_ready = sem("dec_ready")
        near_ready = sem("near_ready")
        ret_ready = sem("ret_ready")
        rs_ready = sem("rs_ready")
        shg_ready = sem("shg_ready")
        srt_ready = sem("srt_ready")
        gelarg_ready = sem("gelarg_ready")
        gelu_done = sem("gelu_done")
        orc_ready = sem("orc_ready")
        mixed_ready = sem("mixed_ready")
        res_ready = sem("res_ready")
        lnc_ready = sem("lnc_ready")
        ln_ready = sem("ln_ready")
        h_ready = sem("h_ready")
        s5fin_ready = sem("s5fin_ready")
        pool_step = sem("pool_step")
        outs = {n: sem("stored_" + n) for n in ("y", "hg_p", "rt_p", "s5_p", "hg_s", "rt_s", "s5_s")}

        def unit_index(l, name):
            return l * N_UNITS + UNIT_AT[name]

        def bank(l, name):
            return mix_bank[unit_index(l, name) % MIX_BANKS]

        def unit_freed(l, name):
            return unit_free[unit_index(l, name) % MIX_BANKS]

        def need(eng, s, n):
            if n > 0:
                eng.wait_ge(s, n)

        block = ctx.enter_context(nc.Block())

        @block.sync
        def _(sp):
            sp.dma_start(X[:, :, :], xT).then_inc(x_loaded, 16)
            for l in range(DEPTH):
                for c in range(N_CHUNKS):
                    n = l * N_CHUNKS + c
                    if n >= RING:
                        ol, oc = divmod(n - RING, N_CHUNKS)
                        sp.wait_ge(tile_done, ol * N_STREAM + last_tile(oc) + 1)
                    sp.dma_start(ring[:, n % RING, :], weights[l, c]).then_inc(w_loaded[n % RING], 16)
            sp.wait_ge(ln_ready, 2 * DEPTH)
            sp.dma_start(y_out, X[:, :, :]).then_inc(outs["y"], 16)
            sp.wait_ge(outs["y"], 16)

        @block.gpsimd
        def _(pool):
            pool.dma_start(vecs[:, :, :], vectors).then_inc(const_loaded, 16)
            pool.dma_start(consts[:, :], constants).then_inc(const_loaded, 16)
            pool.dma_start(masks_f32, level_masks).then_inc(const_loaded, 16)
            pool.dma_start(s5x0[:, :, :, :, :], state_s5).then_inc(const_loaded, 16)
            for l in range(DEPTH):
                if l:
                    pool.wait_ge(unit_done, unit_index(l - 1, ("glu", 1)) + 1)
                    pool.wait_ge(table_ready, l)
                pool.dma_start(mats[:, :], matrices[l]).then_inc(mats_loaded, 16)
                if l:
                    pool.wait_ge(outs["hg_s"], 16 * l)
                    pool.wait_ge(outs["rt_s"], 16 * l)
                    pool.wait_ge(unit_done, unit_index(l - 1, ("ret_o", 2)) + 1)
                pool.dma_start(S_hg[:, :, :, :], state_hg[l]).then_inc(states_loaded, 16)
                pool.dma_start(S_rt[:, :, :, :], state_rt[l]).then_inc(states_loaded, 16)
                for i in range(6):
                    pool.wait_ge(vs_ready, 2 * l + i // 3 + 1)
                    if i >= 2 or l:
                        who = ("hg_kv", i - 2) if 2 <= i < 5 else ("ret_kv", 0)
                        ll = l if i >= 2 else l - 1
                        if i < 2:
                            who = ("ret_kv", 1)
                        pool.wait_ge(unit_done, unit_index(ll, who) + 1)
                    src = vs_tok[:, i // 3, 128 * (i % 3):128 * (i % 3) + 128]
                    pool.affine_select(out=v_own[:, i % 2, :, :], in_=src.unsqueeze(1).broadcast_to([NSAMP, NSAMP, 128]),
                                       compare_op=ALU.is_equal, fill=0.0, base=0, pattern=[[-1, NSAMP], [0, 128]],
                                       channel_multiplier=1).then_inc(vown_ready, 1)
                pool.wait_ge(shg_ready, 3 * l + 3)
                pool.dma_start(hg_s_out[l], S_hg[:, :, :, :]).then_inc(outs["hg_s"], 16)
                pool.wait_ge(srt_ready, 2 * l + 2)
                pool.dma_start(rt_s_out[l], S_rt[:, :, :, :]).then_inc(outs["rt_s"], 16)
                pool.wait_ge(s5fin_ready, 2 * l + 2)
                pool.dma_start(s5_p_out[l], s5fin[:, :, :]).then_inc(outs["s5_p"], 16)
                pool.dma_start(s5_s_out[l], s5xs[:, :, :, :]).then_inc(outs["s5_s"], 16)
                pool.wait_ge(stp_ready, 3 * l + 3)
                pool.dma_start(hg_p_out[l], st_p[:, 0:3, :]).then_inc(outs["hg_p"], 16)
                pool.dma_start(rt_p_out[l], st_p[:, 3:5, :]).then_inc(outs["rt_p"], 16)
            for n in ("hg_p", "rt_p", "s5_p", "hg_s", "rt_s", "s5_s"):
                pool.wait_ge(outs[n], 16 * DEPTH)

        @block.tensor
        def _(pe):
            def unit(l, name):
                g = unit_index(l, name)
                need(pe, unit_free[g % MIX_BANKS], g // MIX_BANKS)
                return mix_bank[g % MIX_BANKS]

            fences = [0]

            def row_tile_fence(mm):
                fences[0] += 1
                mm.then_inc(row_tile_done, 1)
                pe.wait_ge(row_tile_done, fences[0])

            def run_unit(l, u):
                kind = u[0]
                if kind == "s5_in":
                    j = u[1]
                    if j == 0:
                        pe.wait_ge(u_ready, 2 * l + 2)
                        pe.wait_ge(mats_loaded, 16 * (l + 1))
                    b = unit(l, u)
                    q = 32 * (j % 4)
                    for r in range(2):
                        mm = pe.matmul(b[:, 256 * r:256 * r + 256], B_s5[q:q + 32, j // 4, r, :], U[q:q + 32, j // 4, 0:256], start=True, stop=True, tile_position=(q, 0))
                    mm.then_inc(unit_done, 1)
                elif kind == "s5_in_sample":
                    b = unit(l, u)
                    bv = b[:, 0:128].rearrange("p (r j t) -> p r j t", r=2, j=8)
                    for q in range(0, 128, 32):
                        for s in range(2):
                            for r in range(2):
                                mm = pe.matmul(bv[:, r, 4 * s + q // 32, :], B_s5[q:q + 32, s, r, :], U[q:q + 32, s, 256:T], start=True, stop=True, tile_position=(q, 0))
                        if q < 96:
                            row_tile_fence(mm)
                    mm.then_inc(unit_done, 1)
                elif kind == "s5_out":
                    j = u[1]
                    if j == 0:
                        need(pe, y5_free, l)
                        pe.wait_ge(table_ready, l + 1)
                    pe.wait_ge(xs_ready, 8 * l + j + 1)
                    q = 32 * (j % 4)
                    o = y5_bank[q:q + 32, j // 4, :]
                    pe.matmul(o, Cg[:, j, 0, :], XS[j % 2][:, 0:256], start=True, stop=False, tile_position=(0, q))
                    pe.matmul(o, Cg[:, j, 1, :], XS[j % 2][:, 256:512], start=False, stop=True, tile_position=(0, q)).then_inc(y5_done, 1)
                elif kind == "s5_out_sample":
                    pe.wait_ge(xss_ready, l + 1)
                    b = unit(l, u)
                    for j in range(8):
                        q = 32 * (j % 4)
                        o = b[q:q + 32, 8 * (j // 4):8 * (j // 4) + 8]
                        pe.matmul(o, C_s5[:, j, 0, :], s5xs[:, 0, j, :], start=True, stop=False, tile_position=(0, q))
                        mm = pe.matmul(o, Cs[:, j, :], s5xs[:, 1, j, :], start=False, stop=True, tile_position=(0, q))
                    mm.then_inc(unit_done, 1)
                elif kind in ("tr_hi", "tr_rv"):
                    f0 = 0 if kind == "tr_hi" else 3
                    pe.wait_ge(v_ready, 6 * l + f0 + 3)
                    b = unit(l, u)
                    for i in range(3):
                        mm = pe.transpose(b[:, 128 * i:128 * i + 128], Vf[:, f0 + i, 128 * u[1]:128 * u[1] + 128], ident)
                    mm.then_inc(unit_done, 1)
                elif kind in ("tr_hi_sample", "tr_rv_sample"):
                    f0 = 0 if kind == "tr_hi_sample" else 3
                    b = unit(l, u)
                    for i in range(3):
                        mm = pe.transpose(b[0:NSAMP, 128 * i:128 * i + 128], Vf[:, f0 + i, 256:T], ident)
                    mm.then_inc(unit_done, 1)
                elif kind == "tr_hk_sample":
                    pe.wait_ge(hq_ready, l + 1)
                    b = unit(l, u)
                    for i in range(3):
                        mm = pe.transpose(b[0:NSAMP, 128 * i:128 * i + 128], Kg[:, i, 256:T], ident)
                    mm.then_inc(unit_done, 1)
                elif kind == "tr_rk_sample":
                    b = unit(l, u)
                    for i in range(2):
                        mm = pe.transpose(b[0:NSAMP, 128 * i:128 * i + 128], KR[:, i, 256:T], ident)
                    mm.then_inc(unit_done, 1)
                elif kind == "tr_hkd":
                    pe.wait_ge(dec_ready, 9 * l + 9)
                    b = unit(l, u)
                    for i in range(3):
                        mm = pe.transpose(b[:, 128 * i:128 * i + 128], kdec[0][:, i, 128 * u[1]:128 * u[1] + 128], ident)
                    mm.then_inc(unit_done, 1)
                elif kind == "tr_rk":
                    b = unit(l, u)
                    for i in range(2):
                        mm = pe.transpose(b[:, 128 * i:128 * i + 128], KR[:, i, 128 * u[1]:128 * u[1] + 128], ident)
                    mm.then_inc(unit_done, 1)
                elif kind == "hg_level":
                    L, ft = u[1:]
                    if L < 0:
                        pe.wait_ge(hq_ready, l + 1)
                        k, q = Kg, Qg
                    else:
                        pe.wait_ge(dec_ready, 9 * l + L + 1)
                        k, q = kdec[L % 2], qdec[L % 2]
                    b = unit(l, u)
                    for c, (h, f, t) in enumerate(NEAR_PARTS[ft]):
                        if c == 2 and ft == 2:
                            row_tile_fence(mm)
                        mm = pe.matmul(b[:, 128 * c:128 * c + 128], k[64 * h:64 * h + 64, f, 128 * t:128 * t + 128],
                                       q[64 * h:64 * h + 64, f, 128 * t:128 * t + 128], start=True, stop=True, tile_position=(64 * h, 0))
                    mm.then_inc(unit_done, 1)
                elif kind == "hg_far":
                    pe.wait_ge(dec_ready, 9 * l + 8)
                    b = unit(l, u)
                    h = u[1]
                    for f in range(3):
                        mm = pe.matmul(b[:, 128 * f:128 * f + 128], kdec[1][64 * h:64 * h + 64, f, 0:128],
                                       qdec[1][64 * h:64 * h + 64, f, 128:256], start=True, stop=True, tile_position=(64 * h, 0))
                    mm.then_inc(unit_done, 1)
                elif kind == "hg_state":
                    pe.wait_ge(kt_ready, 2 * l + 2)
                    pe.wait_ge(vtok_ready, 4 * l + 2)
                    b = unit(l, u)
                    for h in range(HEADS):
                        o = b[64 * (h % 2):64 * (h % 2) + 64, 64 * (h // 2):64 * (h // 2) + 64]
                        for t in range(2):
                            mm = pe.matmul(o, kt_hg[:, t, 64 * h:64 * h + 64], V_tok[:, t, 0, 64 * h:64 * h + 64], start=(t == 0), stop=(t == 1),
                                           tile_position=(0, 64 * (h % 2)))
                    mm.then_inc(unit_done, 1)
                elif kind == "hg_kv":
                    ft = u[1]
                    pe.wait_ge(ks_ready, 2 * l + 1)
                    pe.wait_ge(vown_ready, 6 * l + ft + 1)
                    b = unit(l, u)
                    for h in range(2):
                        mm = pe.matmul(b[64 * h:64 * h + 64, :].rearrange("p (b v) -> p b v", b=8), ks_tok[:, 128 * ft + 64 * h:128 * ft + 64 * h + 64],
                                       v_own[:, ft % 2, :, 64 * h:64 * h + 64], start=True, stop=True, tile_position=(0, 64 * h))
                    mm.then_inc(unit_done, 1)
                elif kind == "ret_kv":
                    i = u[1]
                    pe.wait_ge(ks_ready, 2 * l + 2)
                    b = unit(l, u)
                    for h in range(4 * i, min(4 * i + 4, HEADS)):
                        pe.wait_ge(vown_ready, 6 * l + 3 + h // 2 + 1)
                        o = b[32 * (h % 4):32 * (h % 4) + 32, :].rearrange("p (b v) -> p b v", b=8)
                        mm = pe.matmul(o, ks_tok[:, 384 + 32 * h:384 + 32 * h + 32], v_own[:, (3 + h // 2) % 2, :, 64 * (h % 2):64 * (h % 2) + 64],
                                       start=True, stop=True, tile_position=(0, 32 * (h % 4)))
                    mm.then_inc(unit_done, 1)
                elif kind == "hg_o":
                    ft = u[1]
                    if ft == 0:
                        pe.wait_ge(near_ready, l + 1)
                    pe.wait_ge(far_ready, 2 * l + 2)
                    pe.wait_ge(shg_ready, 3 * l + ft + 1)
                    b = unit(l, u)
                    for h in range(2):
                        o = b[64 * h:64 * h + 64, :]
                        hc = slice(128 * ft + 64 * h, 128 * ft + 64 * h + 64)
                        pos = (0, 64 * h)
                        pe.matmul(o[:, 0:128], V_tok[:, 0, 0, hc], near[:, h, ft, 0, :], start=True, stop=True, tile_position=pos)
                        pe.matmul(o[:, 128:256], V_tok[:, 0, 0, hc], far[:, h, ft, :], start=True, stop=False, tile_position=pos)
                        pe.matmul(o[:, 128:256], V_tok[:, 1, 0, hc], near[:, h, ft, 1, :], start=False, stop=True, tile_position=pos)
                        for s in range(NSAMP):
                            mm = pe.matmul(o[:, 256 + s:257 + s], S_hg[64 * h:64 * h + 64, ft, s, :], Qg[64 * h:64 * h + 64, ft, 256 + s:257 + s],
                                           start=True, stop=True, tile_position=(64 * h, 64 * h))
                    mm.then_inc(unit_done, 1)
                elif kind == "ret_score":
                    h = u[1]
                    if h == 0:
                        pe.wait_ge(ret_ready, l + 1)
                    b = unit(l, u)
                    q, i = 32 * (h % 4), h // 4
                    pe.matmul(b[:, 0:256], KR[q:q + 32, i, 0:128], QR[q:q + 32, i, 0:256], start=True, stop=True, tile_position=(q, 0))
                    pe.matmul(b[:, 256:384], KR[q:q + 32, i, 128:256], QR[q:q + 32, i, 128:256], start=True, stop=True, tile_position=(q, 0)).then_inc(unit_done, 1)
                elif kind == "ret_state":
                    pe.wait_ge(ktr_ready, 2 * l + 2)
                    pe.wait_ge(vtok_ready, 4 * l + 4)
                    b = unit(l, u)
                    for h in range(HEADS):
                        q, i = 32 * (h % 4), h // 4
                        for t in range(2):
                            mm = pe.matmul(b[q:q + 32, 64 * i:64 * i + 64], kt_rt[:, t, 32 * h:32 * h + 32], V_tok[:, t, 1, 64 * h:64 * h + 64],
                                           start=(t == 0), stop=(t == 1), tile_position=(0, q))
                    mm.then_inc(unit_done, 1)
                elif kind == "ret_o":
                    ft = u[1]
                    pe.wait_ge(rs_ready, 6 * l + 2 * ft + 2)
                    pe.wait_ge(srt_ready, 2 * l + 1 + ft // 2)
                    b = unit(l, u)
                    for hh in range(2):
                        h = 2 * ft + hh
                        o = b[64 * hh:64 * hh + 64, :]
                        hc = slice(64 * h, 64 * h + 64)
                        pos = (0, 64 * hh)
                        q, i = 32 * (h % 4), h // 4
                        pe.matmul(o[:, 0:128], V_tok[:, 0, 1, hc], RS[:, h, 0:128], start=True, stop=True, tile_position=pos)
                        pe.matmul(o[:, 128:256], V_tok[:, 0, 1, hc], RS[:, h, 128:256], start=True, stop=False, tile_position=pos)
                        pe.matmul(o[:, 128:256], V_tok[:, 1, 1, hc], RS[:, h, 256:384], start=False, stop=True, tile_position=pos)
                        for s in range(NSAMP):
                            mm = pe.matmul(o[:, 256 + s:257 + s], S_rt[q:q + 32, i, s, :], QR[q:q + 32, i, 256 + s:257 + s],
                                           start=True, stop=True, tile_position=(q, 64 * hh))
                    mm.then_inc(unit_done, 1)
                elif kind == "glu":
                    if u[1] == 0:
                        pe.wait_ge(gelu_done, l + 1)
                    b = unit(l, u)
                    for k in range(2):
                        mm = pe.matmul(b[:, 0:T], glu_w[:, k, 128 * u[1]:128 * u[1] + 128], Y[:, k, :], start=(k == 0), stop=(k == 1))
                    mm.then_inc(unit_done, 1)
                elif kind in ("hg_ms", "ret_mu", "ret_var"):
                    ft = u[1]
                    if kind == "hg_ms":
                        pe.wait_ge(o_ready, 3 * l + ft + 1)
                        src = SQ[:, ft, :]
                    elif kind == "ret_mu":
                        pe.wait_ge(oret_ready, 3 * l + ft + 1)
                        src = MIX[:, 3 + ft, :]
                    else:
                        pe.wait_ge(var_ready, 3 * l + ft + 1)
                        src = SQ[:, 3 + ft, :]
                    b = unit(l, u)
                    pe.matmul(b[:, 0:T], cv("head_mean"), src, start=True, stop=True).then_inc(unit_done, 1)
                elif kind in ("ln1_mu", "ln2_mu", "ln1_var", "ln2_var"):
                    w = int(kind[2]) - 1
                    b = unit(l, u)
                    x = X1 if w == 0 else X
                    for k in range(KT):
                        if kind.endswith("mu"):
                            pe.wait_ge(res_ready, 16 * l + 8 * w + k + 1)
                            src = x[:, k, :]
                        else:
                            if k == 0:
                                pe.wait_ge(lnsq_ready, 2 * l + w + 1)
                            src = SQ[:, k, :]
                        mm = pe.matmul(b[:, 0:T], cv("model_mean"), src, start=(k == 0), stop=(k == KT - 1))
                    mm.then_inc(unit_done, 1)
                else:
                    raise AssertionError(kind)

            pe.wait_ge(x_loaded, 16)
            pe.wait_ge(const_loaded, 64)
            for l in range(DEPTH):
                if l:
                    pe.wait_ge(ln_ready, 2 * l)
                for i in range(N_STREAM):
                    if i == OUT0:
                        pe.wait_ge(mixed_ready, l + 1)
                    if i == UP0:
                        pe.wait_ge(ln_ready, 2 * l + 1)
                    g = l * N_STREAM + i
                    bnk = stream_bank[g % STREAM_BANKS]
                    need(pe, tile_free[g % STREAM_BANKS], g // STREAM_BANKS)
                    ks = KT if i < DOWN0 else FF_TILES
                    for k in range(ks):
                        c = l * N_CHUNKS + chunk_of(i) + (k // 16 if i >= DOWN0 else 0)
                        blk = (i % 2) * 8 + k if i < DOWN0 else k % 16
                        if k % 16 == 0:
                            pe.wait_ge(w_loaded[c % RING], 16 * (c // RING + 1))
                        if i < OUT0:
                            src = X[:, k, :]
                        elif i < UP0:
                            src = MIX[:, k, :]
                        elif i < DOWN0:
                            src = X1[:, k, :]
                        else:
                            src = H[:, k, :]
                            if i == DOWN0:
                                pe.wait_ge(h_ready, 32 * l + k + 1)
                        mm = pe.matmul(bnk[:, 0:T], ring[:, c % RING, 128 * blk:128 * blk + 128], src, start=(k == 0), stop=(k == ks - 1))
                    mm.then_inc(tile_done, 1)
                    for u in PLAN[i]:
                        run_unit(l, u)

        @block.scalar
        def _(act):
            def tile(l, i):
                g = l * N_STREAM + i
                act.wait_ge(tile_done, g + 1)
                return stream_bank[g % STREAM_BANKS][:, 0:T], tile_free[g % STREAM_BANKS]

            def got(l, name):
                act.wait_ge(unit_done, unit_index(l, name) + 1)
                return bank(l, name), unit_freed(l, name)

            freed = {}

            def s5_params(l):
                if l == 0:
                    act.wait_ge(const_loaded, 64)
                act.activation(par[:, 0, :], pv(l, "log_dt"), ACT.Exp).then_inc(act_params, 1)
                act.wait_ge(par_ready, l + 1)
                act.activation(par[:, 3:5, :], par[:, 1:3, :], ACT.Sin).then_inc(act_params, 1)

            s5_params(0)
            act.wait_ge(par_ready, 1)
            act.wait_ge(dve_step, 3)
            act.activation(low[:, 0:2, :], low[:, 2:4, :], ACT.Exp).then_inc(softmax_exp, 1)
            for l in range(DEPTH):
                for i in range(2):
                    p, fr = tile(l, SU + i)
                    act.activation(U[:, i, :], p, ACT.Copy).then_inc(u_ready, 1)
                    act.wait_ge(u_ready, 2 * l + i + 1)
                    act.sem_inc(fr, 1)
                for i in range(3):
                    p, fr = tile(l, HF + i)
                    act.activation(sig_f[:, i, :], p, ACT.Sigmoid).then_inc(sig_ready, 1)
                    act.activation(sig_n[:, i, :], p, ACT.Sigmoid, scale=-1.0).then_inc(sig_ready, 1)
                    act.wait_ge(sig_ready, 6 * l + 2 * i + 2)
                    act.sem_inc(fr, 1)
                for i in range(3):
                    p, fr = tile(l, HQ + i)
                    act.activation(Qg[:, i, :], p, ACT.Sigmoid).then_inc(qsig_ready, 1)
                for i in range(3):
                    p, fr = tile(l, HI + i)
                    act.activation(Vf[:, i, :], p, ACT.Copy).then_inc(v_ready, 1)
                    act.wait_ge(v_ready, 6 * l + i + 1)
                    act.sem_inc(fr, 1)
                for i in range(4):
                    p, fr = tile(l, RQ + i)
                    dst = RQraw[:, i, :] if i < 2 else RKraw[:, i - 2, :]
                    act.activation(dst, p, ACT.Copy).then_inc(rqk_ready, 1)
                    act.wait_ge(rqk_ready, 4 * l + i + 1)
                    act.sem_inc(fr, 1)
                    if i == 0:
                        for t in range(2):
                            b, fu = got(l, ("tr_hi", t))
                            act.activation(V_tok[:, t, 0, :], b[:, 0:384], ACT.Copy).then_inc(vtok_ready, 1)
                            act.wait_ge(vtok_ready, 4 * l + t + 1)
                            act.sem_inc(fu, 1)
                        b, fu = got(l, ("tr_hi_sample",))
                        act.activation(vs_tok[:, 0, :], b[0:NSAMP, 0:384], ACT.Copy).then_inc(vs_ready, 1)
                        act.wait_ge(vs_ready, 2 * l + 1)
                        act.sem_inc(fu, 1)
                    if i == 2:
                        b, fu = got(l, ("tr_hk_sample",))
                        act.activation(ks_tok[:, 0:384], b[0:NSAMP, 0:384], ACT.Copy).then_inc(ks_ready, 1)
                        act.wait_ge(ks_ready, 2 * l + 1)
                        act.sem_inc(fu, 1)
                for i in range(3):
                    p, fr = tile(l, RV + i)
                    act.activation(Vf[:, 3 + i, :], p, ACT.Copy).then_inc(v_ready, 1)
                    act.wait_ge(v_ready, 6 * l + 3 + i + 1)
                    act.sem_inc(fr, 1)
                for i in range(6):
                    if i == 4:
                        for h in range(2):
                            b, fu = got(l, ("hg_far", h))
                            act.activation(far[:, h, :, :], b[:, 0:384].rearrange("p (a b) -> p a b", a=3), ACT.Copy).then_inc(far_ready, 1)
                            act.wait_ge(far_ready, 2 * l + h + 1)
                            act.sem_inc(fu, 1)
                    if i == 5:
                        for t in range(2):
                            b, fu = got(l, ("tr_hkd", t))
                            act.activation(kt_hg[:, t, :], b[:, 0:384], ACT.Copy).then_inc(kt_ready, 1)
                            act.wait_ge(kt_ready, 2 * l + t + 1)
                            act.sem_inc(fu, 1)
                        b, fu = got(l, ("hg_state",))
                        if l:
                            act.wait_ge(outs["hg_p"], 16 * l)
                            act.wait_ge(outs["rt_p"], 16 * l)
                        act.activation(st_p[:, 0:3, :], b[:, 0:192].rearrange("p (a b) -> p a b", a=3), ACT.Copy).then_inc(stp_ready, 1)
                        act.wait_ge(stp_ready, 3 * l + 1)
                        act.sem_inc(fu, 1)
                    p, fr = tile(l, HGT + i)
                    act.activation(gates[:, i, :], p, ACT.Sigmoid).then_inc(gsig_ready, 1)
                act.wait_ge(gelarg_ready, l + 1)
                act.activation(gel, gel, ACT.Sigmoid).then_inc(gel_ready, 1)
                for t in range(2):
                    b, fu = got(l, ("tr_rv", t))
                    act.activation(V_tok[:, t, 1, :], b[:, 0:384], ACT.Copy).then_inc(vtok_ready, 1)
                    act.wait_ge(vtok_ready, 4 * l + 2 + t + 1)
                    act.sem_inc(fu, 1)
                b, fu = got(l, ("tr_rv_sample",))
                act.activation(vs_tok[:, 1, :], b[0:NSAMP, 0:384], ACT.Copy).then_inc(vs_ready, 1)
                act.wait_ge(vs_ready, 2 * l + 2)
                act.sem_inc(fu, 1)
                b, fu = got(l, ("tr_rk_sample",))
                act.activation(ks_tok[:, 384:640], b[0:NSAMP, 0:256], ACT.Copy).then_inc(ks_ready, 1)
                act.wait_ge(ks_ready, 2 * l + 2)
                act.sem_inc(fu, 1)
                b, fu = got(l, ("ret_state",))
                act.activation(st_p[:, 3, :], b[:, 0:64], ACT.Copy).then_inc(stp_ready, 1)
                act.activation(st_p[0:64, 4, :], b[0:64, 64:128], ACT.Copy).then_inc(stp_ready, 1)
                act.wait_ge(stp_ready, 3 * l + 3)
                act.sem_inc(fu, 1)
                for ft in range(3):
                    b, fu = got(l, ("hg_o", ft))
                    act.activation(MIX[:, ft, :], b[:, 0:T], ACT.Copy).then_inc(act_step, 1)
                    act.activation(SQ[:, ft, :], b[:, 0:T], ACT.Square).then_inc(o_ready, 1)
                    act.wait_ge(o_ready, 3 * l + ft + 1)
                    act.sem_inc(fu, 1)
                for ft in range(3):
                    b, fu = got(l, ("ret_o", ft))
                    act.activation(MIX[:, 3 + ft, :], b[:, 0:T], ACT.Copy).then_inc(oret_ready, 1)
                    act.wait_ge(oret_ready, 3 * l + ft + 1)
                    act.sem_inc(fu, 1)
                for m in range(2):
                    b, fu = got(l, ("glu", m))
                    act.activation(gel[:, m, :], b[:, 0:T], ACT.Sigmoid, bias=pv(l, "glu_b")[:, m:m + 1]).then_inc(gel_ready, 1)
                    act.wait_ge(gel_ready, 3 * l + m + 2)
                    act.sem_inc(fu, 1)
                for ft in range(3):
                    b, fu = got(l, ("hg_ms", ft))
                    act.activation(SQ[:, ft, :], b[:, 0:T], ACT.Sqrt, bias=cv("eps")).then_inc(hrms_ready, 1)
                    act.wait_ge(hrms_ready, 3 * l + ft + 1)
                    act.sem_inc(fu, 1)
                for ft in range(3):
                    act.wait_ge(orc_ready, 3 * l + ft + 1)
                    act.activation(SQ[:, 3 + ft, :], MIX[:, 3 + ft, :], ACT.Square).then_inc(var_ready, 1)
                for ft in range(3):
                    b, fu = got(l, ("ret_var", ft))
                    act.activation(SQ[:, 3 + ft, :], b[:, 0:T], ACT.Sqrt, bias=cv("eps")).then_inc(rrms_ready, 1)
                    act.wait_ge(rrms_ready, 3 * l + ft + 1)
                    act.sem_inc(fu, 1)

                def norm(w):
                    x = X1 if w == 0 else X
                    act.wait_ge(lnc_ready, 2 * l + w + 1)
                    act.activation(SQ[:, :, :], x[:, :, :], ACT.Square).then_inc(lnsq_ready, 1)
                    b, fu = got(l, (f"ln{w + 1}_var",))
                    act.activation(SQ[:, 0, :], b[:, 0:T], ACT.Sqrt, bias=cv("eps")).then_inc(lnsd_ready, 1)
                    act.wait_ge(lnsd_ready, 2 * l + w + 1)
                    act.sem_inc(fu, 1)

                norm(0)
                if l + 1 < DEPTH:
                    act.wait_ge(table_ready, l + 1)
                    s5_params(l + 1)
                for m in range(N_UP):
                    p, fr = tile(l, UP0 + m)
                    act.activation(H[:, m, :], p, ACT.Relu).then_inc(relu_ready, 1)
                    act.wait_ge(relu_ready, 32 * l + m + 1)
                    act.sem_inc(fr, 1)
                norm(1)

        @block.vector
        def _(dve):
            last = {"sem": None, "n": 0}
            count = {}

            def put(ins, s=None):
                s = dve_step if s is None else s
                count[s.name] = count.get(s.name, 0) + 1
                ins.then_inc(s, 1)
                last["sem"], last["n"] = s, count[s.name]

            def settle():
                dve.wait_ge(last["sem"], last["n"])

            def chain(ins, s=None):
                put(ins, s)
                settle()

            def free(s):
                settle()
                dve.sem_inc(s, 1)

            def got(l, name):
                dve.wait_ge(unit_done, unit_index(l, name) + 1)
                return bank(l, name), unit_freed(l, name)

            def tile(l, i):
                g = l * N_STREAM + i
                return stream_bank[g % STREAM_BANKS][:, 0:T], tile_free[g % STREAM_BANKS]

            tt, ts, stt, cp = dve.tensor_tensor, dve.tensor_scalar, dve.scalar_tensor_tensor, dve.tensor_copy
            DT, RC, RS_, SN, CS = 0, 1, 2, 3, 4
            TH, ZR, EX, MAG, ABR, ABI, DEN, GR, GI, T0, T1, T2, PC, PS, NR = range(5, 20)

            def row(i):
                return par[:, i, :]

            def s5_tables(l):
                are, aim = pv(l, "a_re"), pv(l, "a_im")
                dve.wait_ge(act_params, 2 * l + 1)
                chain(tt(row(TH), row(DT), aim, ALU.mult))
                two_pi_hi, two_pi_lo = 6.28125, float(2 * np.pi - 6.28125)
                magic = 12582912.0
                for dst, shift in ((RS_, 0.0), (RC, 0.25)):
                    chain(ts(row(T0), row(TH), float(1 / (2 * np.pi)), shift, ALU.mult, ALU.add))
                    chain(ts(row(T0), row(T0), magic, None, ALU.add))
                    chain(ts(row(T0), row(T0), -magic, None, ALU.add))
                    chain(stt(row(T1), row(T0), -two_pi_hi, row(TH), ALU.mult, ALU.add))
                    chain(stt(row(T1), row(T0), -two_pi_lo, row(T1), ALU.mult, ALU.add))
                    chain(ts(row(T1), row(T1), float(shift * 2 * np.pi), None, ALU.add))
                    chain(ts(row(dst), row(T1), 3.1415925, -3.1415925, ALU.min, ALU.max), par_ready if dst == RC else None)
                chain(tt(row(ZR), row(DT), are, ALU.mult))
                chain(ts(row(ZR), row(ZR), 1.0 / 16, None, ALU.mult))
                chain(ts(row(EX), row(ZR), 1.0 / 8, 1.0, ALU.mult, ALU.add))
                for n in range(7, 0, -1):
                    chain(tt(row(EX), row(EX), row(ZR), ALU.mult))
                    chain(ts(row(EX), row(EX), 1.0 / n, 1.0, ALU.mult, ALU.add))
                for n in range(4):
                    chain(tt(row(MAG if n == 3 else EX), row(EX), row(EX), ALU.mult))
                dve.wait_ge(act_params, 2 * l + 2)
                cos1, sin1 = row(3), row(4)
                chain(tt(row(ABR), row(MAG), cos1, ALU.mult))
                chain(tt(row(ABI), row(MAG), sin1, ALU.mult))
                chain(ts(row(NR), row(ABR), -1.0, None, ALU.add))
                chain(tt(row(T0), are, are, ALU.mult))
                chain(tt(row(T1), aim, aim, ALU.mult))
                chain(tt(row(DEN), row(T0), row(T1), ALU.add))
                chain(dve.reciprocal(row(DEN), row(DEN)))
                chain(tt(row(T0), row(NR), are, ALU.mult))
                chain(tt(row(T1), row(ABI), aim, ALU.mult))
                chain(tt(row(T0), row(T0), row(T1), ALU.add))
                chain(tt(row(GR), row(T0), row(DEN), ALU.mult))
                chain(tt(row(T0), row(ABI), are, ALU.mult))
                chain(tt(row(T1), row(NR), aim, ALU.mult))
                chain(tt(row(T0), row(T0), row(T1), ALU.subtract))
                chain(tt(row(GI), row(T0), row(DEN), ALU.mult))
                C, S = rot[:, 0, :, :], rot[:, 1, :, :]
                chain(dve.memset(rot[:, 0, :, 0:1], 1.0))
                chain(dve.memset(rot[:, 1, :, 0:1], 0.0))
                put(cp(row(PC), cos1))
                chain(cp(row(PS), sin1))
                n = 1
                while n < SEQ:
                    pc = row(PC).unsqueeze(2).broadcast_to([128, 8, n])
                    ps = row(PS).unsqueeze(2).broadcast_to([128, 8, n])
                    scratch = rot_tmp[:, 0:8 * n].rearrange("p (a b) -> p a b", a=8)
                    put(tt(scratch, S[:, :, 0:n], ps, ALU.mult))
                    chain(tt(C[:, :, n:2 * n], C[:, :, 0:n], pc, ALU.mult))
                    put(tt(C[:, :, n:2 * n], C[:, :, n:2 * n], scratch, ALU.subtract))
                    chain(tt(S[:, :, n:2 * n], S[:, :, 0:n], pc, ALU.mult))
                    chain(tt(scratch, C[:, :, 0:n], ps, ALU.mult))
                    chain(tt(S[:, :, n:2 * n], S[:, :, n:2 * n], scratch, ALU.add))
                    n *= 2
                    if n < SEQ:
                        chain(tt(row(T0), row(PC), row(PC), ALU.mult))
                        chain(tt(row(T1), row(PS), row(PS), ALU.mult))
                        chain(tt(row(T2), row(PC), row(PS), ALU.mult))
                        chain(tt(row(PC), row(T0), row(T1), ALU.subtract))
                        chain(ts(row(PS), row(T2), 2.0, None, ALU.mult))
                dve.wait_ge(mats_loaded, 16 * (l + 1))
                gr = row(GR).unsqueeze(2).broadcast_to([128, 8, 32])
                gi = row(GI).unsqueeze(2).broadcast_to([128, 8, 32])
                scratch = rot_tmp[:, 0:256].rearrange("p (a b) -> p a b", a=8)
                chain(tt(Cg[:, :, 0, :], C_s5[:, :, 0, :], gr, ALU.mult))
                chain(tt(scratch, C_s5[:, :, 1, :], gi, ALU.mult))
                chain(tt(Cg[:, :, 0, :], Cg[:, :, 0, :], scratch, ALU.subtract))
                chain(tt(Cg[:, :, 1, :], C_s5[:, :, 1, :], gr, ALU.mult))
                chain(tt(scratch, C_s5[:, :, 0, :], gi, ALU.mult))
                chain(stt(Cg[:, :, 1, :], Cg[:, :, 1, :], -1.0, scratch, ALU.mult, ALU.subtract))
                chain(ts(Cs[:, :, :], C_s5[:, :, 1, :], -1.0, None, ALU.mult), table_ready)

            rot_tmp = MIX[:, :, :].rearrange("p a b -> p (a b)")

            dve.wait_ge(const_loaded, 64)
            lg = [pv(l, "logits") for l in range(DEPTH)]
            chain(tt(low[:, 4, :], lg[0], lg[1], ALU.max))
            chain(tt(low[:, 2, :], lg[0], low[:, 4, :], ALU.subtract))
            chain(tt(low[:, 3, :], lg[1], low[:, 4, :], ALU.subtract))
            put(dve.memset(near[:, :, :, :, :], 0.0))
            put(dve.memset(st_p[:, :, :], 0.0))
            put(cp(masks[:, :, :], masks_f32))
            for b in (*qdec, *kdec):
                put(dve.memset(b, 0.0))
            settle()
            s5_tables(0)
            dve.wait_ge(softmax_exp, 1)
            chain(tt(low[:, 4, :], low[:, 0, :], low[:, 1, :], ALU.add))
            chain(dve.reciprocal(low[:, 4, :], low[:, 4, :]))
            chain(tt(low[:, 2, :], low[:, 0, :], low[:, 4, :], ALU.mult))
            chain(tt(low[:, 3, :], low[:, 1, :], low[:, 4, :], ALU.mult))
            chain(tt(low[:, 0, :], low[:, 2, :], low[:, 2, :], ALU.subtract))
            chain(tt(low[:, 3, :], low[:, 2, :], low[:, 3, :], ALU.add))
            chain(tt(low[:, 1, :], low[:, 3, :], low[:, 2, :], ALU.subtract))
            for l in range(DEPTH):
                chain(ts(low[:, 6 + l, :], low[:, l, :], -1.0, 1.0, ALU.mult, ALU.add))

            for l in range(DEPTH):
                lb, one_lb = low[:, l, :], low[:, 6 + l, :]

                def s5_tile(j):
                    b, fu = got(l, ("s5_in", j))
                    bb = b[:, :].rearrange("p (r t) -> p r t", r=2)
                    c = rot[:, 0, j, :].unsqueeze(1).broadcast_to([128, 2, SEQ])
                    s = rot[:, 1, j, :].unsqueeze(1).broadcast_to([128, 2, SEQ])
                    p1, p2 = (p.rearrange("p (r t) -> p r t", r=2) for p in (P1, P2))
                    put(tt(p1, bb, c, ALU.mult))
                    chain(tt(p2, bb, s, ALU.mult))
                    dve.sem_inc(fu, 1)
                    put(tt(W5[:, 0:256], P1[:, 0:256], P2[:, 256:512], ALU.add))
                    chain(tt(W5[:, 256:512], P1[:, 256:512], P2[:, 0:256], ALU.subtract))
                    mag = row(MAG)[:, j:j + 1].broadcast_to([128, SEQ])
                    for r in range(2):
                        put(dve.tensor_tensor_scan(Z5[:, 256 * r:256 * r + 256], mag, W5[:, 256 * r:256 * r + 256], 0.0, ALU.mult, ALU.add))
                    settle()
                    z = Z5.rearrange("p (r t) -> p r t", r=2)
                    put(tt(p1, z, c, ALU.mult))
                    chain(tt(p2, z, s, ALU.mult))
                    if j >= 2:
                        dve.wait_ge(y5_done, 8 * l + j - 1)
                    x = XS[j % 2]
                    put(tt(x[:, 0:256], P1[:, 0:256], P2[:, 256:512], ALU.subtract))
                    chain(tt(x[:, 256:512], P1[:, 256:512], P2[:, 0:256], ALU.add), xs_ready)
                    put(cp(s5last[:, :, j], x.rearrange("p (r t) -> p r t", r=2)[:, :, 255]))

                for j in range(S5_TILES):
                    s5_tile(j)
                    if j < 3:
                        dve.wait_ge(sig_ready, 6 * l + 2 * j + 2)
                        put(ts(Fg[:, j, :], sig_f[:, j, 0:256], one_lb[:, j:j + 1], lb[:, j:j + 1], ALU.mult, ALU.add))
                        put(ts(Fs[:, j, :], sig_f[:, j, 256:T], one_lb[:, j:j + 1], lb[:, j:j + 1], ALU.mult, ALU.add))
                        put(ts(Kg[:, j, :], sig_n[:, j, :], one_lb[:, j:j + 1], None, ALU.mult))
                    if 3 <= j < 6:
                        dve.wait_ge(qsig_ready, 3 * l + j - 2)
                        p, fr = tile(l, HQ + j - 3)
                        put(tt(Qg[:, j - 3, :], Qg[:, j - 3, :], p, ALU.mult))
                        free(fr)
                settle()
                gr2 = row(GR)
                gi2 = row(GI)
                if l:
                    dve.wait_ge(outs["s5_p"], 16 * l)
                    dve.wait_ge(outs["s5_s"], 16 * l)
                chain(tt(s5fin[:, 0, :], s5last[:, 0, :], gr2, ALU.mult))
                chain(tt(row(T0), s5last[:, 1, :], gi2, ALU.mult))
                chain(tt(s5fin[:, 0, :], s5fin[:, 0, :], row(T0), ALU.subtract))
                chain(tt(s5fin[:, 1, :], s5last[:, 0, :], gi2, ALU.mult))
                chain(tt(row(T0), s5last[:, 1, :], gr2, ALU.mult))
                chain(tt(s5fin[:, 1, :], s5fin[:, 1, :], row(T0), ALU.add), s5fin_ready)
                b, fu = got(l, ("s5_in_sample",))
                bv = b[:, 0:128].rearrange("p (r j t) -> p r j t", r=2, j=8)

                def wide(i):
                    return row(i).unsqueeze(2).broadcast_to([128, 8, NSAMP])

                x0 = s5x0[:, l, :, :, :]
                first = True
                for cr, ci, src in ((ABR, ABI, x0), (GR, GI, bv)):
                    for r, (ca, op1, cb) in enumerate(((cr, ALU.subtract, ci), (cr, ALU.add, ci))):
                        chain(tt(s5tmp[:, 0, :, :], src[:, r, :, :], wide(ca), ALU.mult))
                        chain(tt(s5tmp[:, 1, :, :], src[:, 1 - r, :, :], wide(cb), ALU.mult))
                        if first:
                            chain(tt(s5xs[:, r, :, :], s5tmp[:, 0, :, :], s5tmp[:, 1, :, :], op1))
                        else:
                            chain(tt(s5tmp[:, 0, :, :], s5tmp[:, 0, :, :], s5tmp[:, 1, :, :], op1))
                            chain(tt(s5xs[:, r, :, :], s5xs[:, r, :, :], s5tmp[:, 0, :, :], ALU.add), s5fin_ready if r == 1 else None)
                    first = False
                dve.sem_inc(fu, 1)
                dve.sem_inc(xss_ready, 1)
                dve.sem_inc(hq_ready, 1)

                def halves(x, half):
                    v = x.rearrange("p f (n c) -> p f n c", c=2 * half)
                    return v[:, :, :, 0:half], v[:, :, :, half:2 * half]

                put(dve.memset(Gg[:, :, :], 1.0))

                def near_level(L):
                    for ft in range(3):
                        b, fu = got(l, ("hg_level", L, ft))
                        m = masks[:, L + 1, :].unsqueeze(1).unsqueeze(1).broadcast_to([128, 2, 2, 128])
                        dst = near[:, ft, 0:2, :, :] if ft < 2 else near[:, :, 2, :, :]
                        put(dve.copy_predicated(dst, m, b[:, :].rearrange("p (a c t) -> p a c t", a=2, c=2)))
                        free(fu)

                for L in range(LEVELS):
                    half = 1 << L
                    if L >= 2:
                        dve.wait_ge(unit_done, unit_index(l, ("hg_level", L - 2, 2)) + 1)
                    F2 = Fg[:, :, :].rearrange("p f (n c) -> p (f n) c", c=2 * half)
                    G2 = Gg[:, :, :].rearrange("p f (n c) -> p (f n) c", c=2 * half)
                    _, q_r = halves(Qg[:, :, 0:256], half)
                    k_l, _ = halves(Kg[:, :, 0:256], half)
                    _, F_r = halves(Fg[:, :, :], half)
                    G_l, _ = halves(Gg[:, :, :], half)
                    settle()
                    put(tt(halves(qdec[L % 2], half)[1], q_r, F_r, ALU.mult))
                    chain(tt(halves(kdec[L % 2], half)[0], k_l, G_l, ALU.mult), dec_ready)
                    nb = 3 * SEQ // (2 * half)
                    chain(tt(G2[:, :, 0:half], G2[:, :, 0:half], F2[:, :, 2 * half - 1:2 * half].broadcast_to([128, nb, half]), ALU.mult))
                    if L < 7:
                        chain(tt(F2[:, :, half:2 * half], F2[:, :, half:2 * half], F2[:, :, half - 1:half].broadcast_to([128, nb, half]), ALU.mult))
                    near_level(L - 1)
                settle()
                chain(tt(kdec[0][:, :, :], Kg[:, :, 0:256], Gg[:, :, :], ALU.mult), dec_ready)
                dve.sem_inc(near_ready, 1)

                dve.wait_ge(y5_done, 8 * l + 8)
                for m in range(2):
                    put(stt(Y[:, m, 0:256], U[:, m, 0:256], pv(l, "d")[:, m:m + 1], y5_bank[:, m, :], ALU.mult, ALU.add))
                free(y5_free)
                b, fu = got(l, ("s5_out_sample",))
                for m in range(2):
                    put(stt(Y[:, m, 256:T], U[:, m, 256:T], pv(l, "d")[:, m:m + 1], b[:, 8 * m:8 * m + 8], ALU.mult, ALU.add))
                free(fu)
                chain(tt(gel, Y, Y, ALU.mult))
                chain(ts(gel, gel, GELU_C1, GELU_C0, ALU.mult, ALU.add))
                chain(tt(gel, gel, Y, ALU.mult), gelarg_ready)

                dve.wait_ge(rqk_ready, 4 * l + 4)
                swap = [i ^ 16 for i in range(32)]
                put(dve.stream_shuffle(swq, RQraw, swap))
                put(dve.stream_shuffle(swk, RKraw, swap))
                settle()
                for raw, sw, dst, c, s in ((RQraw, swq, QR, "cos_q", "sin_q"), (RKraw, swk, KR, "cos_k", "sin_k")):
                    put(tt(raw, raw, cv(c).unsqueeze(1).broadcast_to([128, 2, T]), ALU.mult))
                    chain(tt(sw, sw, cv(s).unsqueeze(1).broadcast_to([128, 2, T]), ALU.mult))
                    put(tt(dst[:, :, :], raw, sw, ALU.add))
                settle()
                dve.sem_inc(ret_ready, 1)

                for i in range(6):
                    dve.wait_ge(gsig_ready, 6 * l + i + 1)
                    p, fr = tile(l, HGT + i)
                    w = pv(l, "hg_norm")[:, 0:1] if i < 3 else pv(l, "ret_norm")[:, i - 3:i - 2]
                    put(stt(gates[:, i, :], gates[:, i, :], w, p, ALU.mult, ALU.mult))
                    free(fr)

                dve.wait_ge(states_loaded, 32 * (l + 1))
                chain(tt(S_hg[:, :, :, :].rearrange("p a b v -> p (a b) v"), S_hg[:, :, :, :].rearrange("p a b v -> p (a b) v"),
                         Fs[:, :, :].rearrange("p a b -> p (a b)").unsqueeze(2).broadcast_to([128, 24, DV]), ALU.mult))
                for ft in range(3):
                    b, fu = got(l, ("hg_kv", ft))
                    S = S_hg[:, ft, :, :].rearrange("p b v -> p (b v)")
                    put(tt(S, S, b[:, :], ALU.add), shg_ready)
                    free(fu)

                for h in range(HEADS):
                    b, fu = got(l, ("ret_score", h))
                    put(tt(RS[:, h, 0:256], b[:, 0:256], decay[:, h, :], ALU.mult))
                    put(tt(RS[:, h, 256:384], b[:, 256:384], decay[:, h, 0:128], ALU.mult), rs_ready)
                    free(fu)
                for t in range(2):
                    b, fu = got(l, ("tr_rk", t))
                    put(tt(kt_rt[:, t, :], b[:, 0:256], k_decay[:, t, :], ALU.mult), ktr_ready)
                    free(fu)
                for i in range(2):
                    b, fu = got(l, ("ret_kv", i))
                    n = 128 if i == 0 else 64
                    S = S_rt[0:n, i, :, :].rearrange("p b v -> p (b v)")
                    put(stt(S, S, cv("gamma")[0:n, i:i + 1], b[0:n, :], ALU.mult, ALU.add), srt_ready)
                    free(fu)

                dve.wait_ge(gel_ready, 3 * l + 1)
                chain(tt(Y, Y, gel, ALU.mult), gelu_done)
                dve.wait_ge(gel_ready, 3 * l + 3)
                put(tt(Y, Y, gel, ALU.mult))

                dve.wait_ge(hrms_ready, 3 * l + 3)
                chain(dve.reciprocal(SQ[:, 0:3, :], SQ[:, 0:3, :]))
                chain(tt(MIX[:, 0:3, :], MIX[:, 0:3, :], SQ[:, 0:3, :], ALU.mult))
                chain(tt(MIX[:, 0:3, :], MIX[:, 0:3, :], gates[:, 0:3, :], ALU.mult))
                for ft in range(3):
                    b, fu = got(l, ("ret_mu", ft))
                    put(tt(MIX[:, 3 + ft, :], MIX[:, 3 + ft, :], b[:, 0:T], ALU.subtract), orc_ready)
                    free(fu)
                dve.wait_ge(rrms_ready, 3 * l + 3)
                chain(dve.reciprocal(SQ[:, 3:6, :], SQ[:, 3:6, :]))
                chain(tt(MIX[:, 3:6, :], MIX[:, 3:6, :], SQ[:, 3:6, :], ALU.mult))
                chain(tt(MIX[:, 3:6, :], MIX[:, 3:6, :], gates[:, 3:6, :], ALU.mult), mixed_ready)

                def residual_and_norm(w):
                    old, x = (X, X1) if w == 0 else (X1, X)
                    for m in range(KT):
                        i = (OUT0 if w == 0 else DOWN0) + m
                        dve.wait_ge(tile_done, l * N_STREAM + i + 1)
                        p, fr = tile(l, i)
                        put(stt(x[:, m, :], old[:, m, :], ALPHA, p, ALU.mult, ALU.add), res_ready)
                        free(fr)
                    b, fu = got(l, (f"ln{w + 1}_mu",))
                    put(tt(x[:, :, :], x[:, :, :], b[:, 0:T].unsqueeze(1).broadcast_to([128, KT, T]), ALU.subtract), lnc_ready)
                    free(fu)
                    dve.wait_ge(lnsd_ready, 2 * l + w + 1)
                    chain(dve.reciprocal(SQ[:, 0, :], SQ[:, 0, :]))
                    chain(tt(x[:, :, :], x[:, :, :], SQ[:, 0, :].unsqueeze(1).broadcast_to([128, KT, T]), ALU.mult))
                    for m in range(KT):
                        put(ts(x[:, m, :], x[:, m, :], pv(l, f"ln{w + 1}_w")[:, m:m + 1], pv(l, f"ln{w + 1}_b")[:, m:m + 1], ALU.mult, ALU.add),
                            ln_ready if m == KT - 1 else None)

                residual_and_norm(0)

                def square(m):
                    dve.wait_ge(relu_ready, 32 * l + m + 1)
                    put(tt(H[:, m, :], H[:, m, :], H[:, m, :], ALU.mult), h_ready)

                if l + 1 < DEPTH:
                    settle()
                    s5_tables(l + 1)
                for m in range(N_UP):
                    square(m)
                residual_and_norm(1)


def _pack_weights(w_in, w_out, w_up, w_down):
    a = 384
    seg = {"hq": 0, "hf": a, "hi": 2 * a, "hg": 3 * a, "rq": 4 * a, "rk": 4 * a + 192, "rv": 4 * a + 384, "rg": 5 * a + 384, "su": 6 * a + 384}
    pad = np.zeros((DEPTH, D_MODEL, 64), w_in.dtype)

    def cut(name, n):
        return w_in[:, :, seg[name]:seg[name] + n]

    cols = np.concatenate([cut("su", 256), cut("hf", a), cut("hq", a), cut("hi", a), cut("rq", 192), pad, cut("rk", 192), pad,
                           cut("rv", a), cut("hg", a), cut("rg", a)], axis=2)
    out = []
    for w in (cols, w_out, w_up):
        m = w.shape[2] // 128
        out.append(w.reshape(DEPTH, KT, 128, m // 2, 2, 128).transpose(0, 3, 2, 4, 1, 5).reshape(DEPTH, m // 2, 128, CHUNK))
    w = w_down.reshape(DEPTH, 2, 16, 128, KT, 128).transpose(0, 4, 1, 3, 2, 5).reshape(DEPTH, 2 * KT, 128, CHUNK)
    out.append(w)
    return np.ascontiguousarray(np.concatenate(out, axis=1))


def _columns(x, tiles):
    return x.reshape(DEPTH, tiles, 128).transpose(2, 0, 1)


def _constants():
    c = np.zeros((128, N_CV), np.float32)

    def put(name, value):
        a, n = CV[name]
        c[:, a:a + n] = value

    put("ident", np.eye(128))
    put("head_mean", np.kron(np.eye(2), np.ones((64, 64))) / 64)
    put("model_mean", 1.0 / D_MODEL)
    half = RET_DK // 2
    inv = np.float32(ROPE_BASE) ** (-np.arange(half, dtype=np.float32) / np.float32(half))
    pos = np.concatenate([np.arange(SEQ), np.full(NSAMP, PAST_LEN)]).astype(np.float32)
    ang = (inv[:, None] * pos[None, :]).astype(np.float32).astype(np.float64)
    p = np.arange(128) % 32
    cos, sin = np.cos(ang)[p % half], np.sin(ang)[p % half] * np.where(p < half, -1.0, 1.0)[:, None]
    put("cos_q", cos), put("sin_q", sin)
    put("cos_k", cos * RET_DK ** -0.5), put("sin_k", sin * RET_DK ** -0.5)
    log_gamma = np.log1p(-np.exp2(-5.0 - np.arange(HEADS))).astype(np.float32).astype(np.float64)
    s, t = np.arange(128)[:, None], np.arange(256)[None, :]
    dec = np.where(t >= s, np.exp(log_gamma[:, None, None] * np.maximum(t - s, 0)), 0.0)
    put("decay", dec.transpose(1, 0, 2).reshape(128, -1))
    left = 255 - np.arange(256)
    kd = np.zeros((2, 128, 256))
    kd[:, :, :192] = np.exp(left[:, None] * np.repeat(log_gamma, RET_DK)[None, :]).reshape(2, 128, 192)
    put("k_decay", kd.transpose(1, 0, 2).reshape(128, 512))
    g = np.zeros((128, 2))
    g[:, 0] = np.repeat(np.exp(log_gamma[:4]), 32)
    g[:64, 1] = np.repeat(np.exp(log_gamma[4:]), 32)
    put("gamma", g)
    put("eps", EPS)
    masks = np.zeros((128, LEVELS, 128), np.float32)
    masks[:, 0, :] = np.eye(128)
    s, t = np.arange(128)[:, None], np.arange(128)[None, :]
    for L in range(7):
        masks[:, L + 1, :] = (s >> (L + 1) == t >> (L + 1)) & ((s >> L) & 1 == 0) & ((t >> L) & 1 == 1)
    return c, masks


def kernel(**inputs):
    import concourse.bacc as bacc
    from concourse.bass_utils import run_bass_kernel_spmd

    a = {k: np.asarray(v) for k, v in inputs.items()}
    f = np.float32
    x = np.concatenate([a["x_prompt"].reshape(SEQ, D_MODEL), a["x_sample"].reshape(NSAMP, D_MODEL)])
    arrays = {}
    arrays["xT"] = np.ascontiguousarray(x.reshape(T, KT, 128).transpose(2, 1, 0))
    arrays["weights"] = _pack_weights(a["w_in"], a["w_out"], a["w_up"], a["w_down"])
    vec = np.zeros((128, DEPTH, N_PV), f)

    def put(name, value):
        at, n = PV[name]
        vec[:, :, at:at + n] = value

    put("log_dt", _columns(np.repeat(a["s5_log_dt"], 64, axis=1), 8))
    put("a_re", _columns(a["s5_a_re"], 8))
    put("a_im", _columns(a["s5_a_im"], 8))
    put("d", _columns(a["s5_d"], 2))
    put("glu_b", _columns(a["s5_glu_b"], 2))
    put("hg_norm", _columns(np.tile(a["hgrn_norm_w"], (1, 2)), 1))
    put("ret_norm", _columns(a["ret_norm_w"], 3))
    for n in ("ln1_w", "ln1_b", "ln2_w", "ln2_b"):
        put(n, _columns(a[n], KT))
    put("logits", _columns(a["hgrn_lb_logits"], 3))
    arrays["vectors"] = vec
    mats = np.zeros((DEPTH, 128, MATS), f)
    Bm = np.zeros((DEPTH, 128, 2, 2, 128), f)
    Cm = np.zeros((DEPTH, 128, 8, 2, 32), f)
    for g in range(16):
        s, j, o = g // 8, g // 2, g % 2
        for r, n in enumerate(("re", "im")):
            Bm[:, 16 * (g % 8):16 * (g % 8) + 16, s, r, 64 * o:64 * o + 64] = a[f"s5_b_{n}"][:, g].transpose(0, 2, 1)
            Cm[:, 64 * o:64 * o + 64, j, r, 16 * o:16 * o + 16] = a[f"s5_c_{n}"][:, g].transpose(0, 2, 1)
    mats[:, :, 0:512] = Bm.reshape(DEPTH, 128, 512)
    mats[:, :, 512:1024] = Cm.reshape(DEPTH, 128, 512)
    mats[:, :, 1024:1536] = a["s5_glu_w"].reshape(DEPTH, 2, 128, 256).transpose(0, 2, 1, 3).reshape(DEPTH, 128, 512)
    arrays["matrices"] = mats
    arrays["constants"], arrays["level_masks"] = _constants()
    arrays["state_hg"] = np.ascontiguousarray(a["state_hgrn"].reshape(DEPTH, NSAMP, 3, 128, DV).transpose(0, 3, 2, 1, 4))
    rt = np.zeros((DEPTH, NSAMP, 2 * 128, DV), f)
    rt[:, :, :192] = a["state_ret"].reshape(DEPTH, NSAMP, 192, DV)
    arrays["state_rt"] = np.ascontiguousarray(rt.reshape(DEPTH, NSAMP, 2, 128, DV).transpose(0, 3, 2, 1, 4))
    s5 = np.stack([a["state_s5_re"], a["state_s5_im"]])
    arrays["state_s5"] = np.ascontiguousarray(s5.reshape(2, DEPTH, NSAMP, 8, 128).transpose(4, 1, 0, 3, 2))

    nc = bacc.Bacc("TRN2", target_bir_lowering=False, num_devices=1)
    ins = [nc.dram_tensor("in_" + n, v.shape, mybir.dt.from_np(v.dtype), kind="ExternalInput").ap() for n, v in arrays.items()]
    out_shapes = {"y": (128, KT, T), "hg_p": (DEPTH, 128, 3, DV), "rt_p": (DEPTH, 128, 2, DV), "s5_p": (DEPTH, 128, 2, 8),
                  "hg_s": (DEPTH, 128, 3, NSAMP, DV), "rt_s": (DEPTH, 128, 2, NSAMP, DV), "s5_s": (DEPTH, 128, 2, 8, NSAMP)}
    out_aps = [nc.dram_tensor("out_" + n, s, F32, kind="ExternalOutput").ap() for n, s in out_shapes.items()]
    build(nc, *ins, *out_aps)
    r = run_bass_kernel_spmd(nc, [{"in_" + n: v for n, v in arrays.items()}], core_ids=[0]).results[0]
    o = {n: np.asarray(r["out_" + n]) for n in out_shapes}
    y = o["y"].transpose(2, 1, 0).reshape(T, D_MODEL)
    hg_p = o["hg_p"].transpose(0, 2, 1, 3).reshape(DEPTH, 1, HEADS, 64, DV)
    rt_p = o["rt_p"].transpose(0, 2, 1, 3).reshape(DEPTH, 256, DV)[:, :192].reshape(DEPTH, 1, HEADS, RET_DK, DV)
    s5_p = o["s5_p"].transpose(2, 0, 3, 1).reshape(2, DEPTH, 1, 16, 64)
    hg_s = o["hg_s"].transpose(0, 3, 2, 1, 4).reshape(DEPTH, NSAMP, HEADS, 64, DV)
    rt_s = o["rt_s"].transpose(0, 3, 2, 1, 4).reshape(DEPTH, NSAMP, 256, DV)[:, :, :192].reshape(DEPTH, NSAMP, HEADS, RET_DK, DV)
    s5_s = o["s5_s"].transpose(2, 0, 4, 3, 1).reshape(2, DEPTH, NSAMP, 16, 64)
    return tuple(np.ascontiguousarray(v) for v in (
        y[:SEQ].reshape(1, SEQ, D_MODEL), y[SEQ:].reshape(NSAMP, 1, D_MODEL),
        hg_p, rt_p, s5_p[0], s5_p[1], hg_s, rt_s, s5_s[0], s5_s[1]))
```

```python
from contextlib import ExitStack

import numpy as np

import concourse.bass as bass
from concourse import mybir

ALU = mybir.AluOpType
ACT = mybir.ActivationFunctionType
F32 = mybir.dt.float32
F32R = mybir.dt.float32r
U8 = mybir.dt.uint8

DEPTH = 2
D_MODEL = 1024
SEQ = 256
NSAMP = 8
PAST_LEN = 2048
T = SEQ + NSAMP
KT = D_MODEL // 128
HEADS = 6
DV = 64
HG_FT = HEADS * DV // 128
RET_DK = 32
S5_TILES = 8
FF_TILES = 32
EPS = 1e-5
ALPHA = (2.0 * DEPTH) ** 0.25
LEVELS = 8
ROPE_BASE = 10000.0
GELU_C0 = 2.0 * (2.0 / np.pi) ** 0.5
GELU_C1 = GELU_C0 * 0.044715

SU, HF, HQ, HI, RQ, RK, RV, HGT, RG = 0, 2, 5, 8, 11, 13, 15, 18, 21
N_IN = 24
OUT0 = N_IN
UP_A = OUT0 + KT
DOWN_A = UP_A + FF_TILES // 2
UP_B = DOWN_A + 2 * KT
DOWN_B = UP_B + FF_TILES // 2
N_CHUNKS = DOWN_B + 2 * KT
FF_HALF = FF_TILES // 2
CHUNK = 8 * 128
RAW_SLOTS = 3
SPLIT_SLOTS = 3
AHEAD = 2
STREAM_BANKS = 4


def tile_index(c):
    if c < DOWN_A:
        return c
    if c < UP_B:
        return DOWN_A + (c - DOWN_A) // 2
    if c < DOWN_B:
        return DOWN_A + KT + (c - UP_B)
    return DOWN_A + KT + FF_HALF + (c - DOWN_B) // 2


N_TILES = tile_index(N_CHUNKS - 1) + 1
assert N_TILES % STREAM_BANKS == 0

PV = {}
_at = 0
for _name, _n in (("log_dt", 8), ("a_re", 8), ("a_im", 8), ("d", 2), ("glu_b", 2), ("hg_norm", 1), ("ret_norm", 3),
                  ("ln1_w", 8), ("ln1_b", 8), ("ln2_w", 8), ("ln2_b", 8), ("logits", 3)):
    PV[_name] = (_at, _n)
    _at += _n
N_PV = _at
CV = {}
_at = 0
for _name, _n in (("ident", 128), ("head_mean", 128), ("model_mean", 128), ("cos", T), ("sin", T),
                  ("decay", HEADS * 256), ("k_decay", 512), ("gamma", 2), ("eps", 1), ("pair_sum", 2), ("quad_sum", 4)):
    CV[_name] = (_at, _n)
    _at += _n
N_CV = _at
MATS = 512 + 512 + 512

PLAN = {c: [] for c in range(N_CHUNKS)}


def _plan(step, *names):
    PLAN[step] += names


_plan(1, ("s5_in", 0), ("s5_in", 1))
for _j in range(2, S5_TILES):
    _plan(_j, ("s5_in", _j))
_plan(8, ("s5_in_sample",))
for _j in range(S5_TILES):
    _plan(_j + 3, ("s5_out", _j))
_plan(11, ("tr_hi", 0), ("tr_hi", 1), ("tr_hi_sample",))
_plan(12, ("tr_hk_sample",), ("s5_out_sample",))
for _r in range(7):
    _plan(12 + _r, *[("hg_level", _r, part) for part in range(3)])
_plan(15, ("glu", 0), ("glu", 1))
_plan(14, ("hg_kv", 0))
_plan(15, ("hg_kv", 1))
_plan(16, ("hg_kv", 2))
_plan(18, ("hg_o_sample",), ("tr_rv_sample",), ("tr_rk_sample",))
_plan(19, ("hg_far", 0), ("hg_far", 1), ("tr_hkd", 0), ("tr_hkd", 1))
_plan(20, ("tr_rv", 0), ("tr_rv", 1), ("tr_rk", 0), ("tr_rk", 1))
_plan(21, ("hg_o", 0), ("hg_o", 1), ("hg_o", 2), ("hg_state",), ("ret_kv", 0), ("ret_kv", 1))
_plan(22, ("ret_score", 0), ("ret_score", 1), ("ret_score", 2), ("ret_state",))
_plan(23, ("ret_score", 3), ("ret_score", 4), ("ret_score", 5), ("ret_o_sample",),
      ("ret_o", 0), ("ret_o", 1), ("ret_o", 2), ("hg_ms", 0), ("hg_ms", 1), ("hg_ms", 2),
      ("ret_mu", 0), ("ret_mu", 1), ("ret_mu", 2), ("ret_var", 0), ("ret_var", 1), ("ret_var", 2))
_plan(UP_A - 1, ("ln1_mu",), ("ln1_var",))
_plan(N_CHUNKS - 1, ("ln2_mu",), ("ln2_var",))
UNIT_ORDER = [u for c in range(N_CHUNKS) for u in PLAN[c] if u[0] != "s5_out"]
UNIT_AT = {u: n for n, u in enumerate(UNIT_ORDER)}
N_UNITS = len(UNIT_ORDER)
MIX_BANKS = 3
NEAR_PARTS = [[(0, f, t) for f in (0, 1) for t in (0, 1)], [(1, f, t) for f in (0, 1) for t in (0, 1)],
              [(h, 2, t) for h in (0, 1) for t in (0, 1)]]


def build(nc, xT, weights, vectors, matrices, constants, level_masks, state_hg, state_rt, state_s5,
          y_out, hg_p_out, rt_p_out, s5_p_out, hg_s_out, rt_s_out, s5_s_out):
    with ExitStack() as ctx:
        def sb(name, shape, dt=F32):
            return ctx.enter_context(nc.sbuf_tensor(name, shape, dt))

        def sem(name):
            return ctx.enter_context(nc.semaphore(name))

        w_raw = sb("w_raw", [128, RAW_SLOTS, CHUNK])
        w_high = sb("w_high", [128, SPLIT_SLOTS, CHUNK], F32R)
        w_low = sb("w_low", [128, SPLIT_SLOTS, CHUNK], F32R)
        a_high = sb("a_high", [128, KT, T], F32R)
        a_low = sb("a_low", [128, KT, T], F32R)
        X = sb("X", [128, KT, T])
        X1 = sb("X1", [128, KT, T])
        MIX = sb("MIX", [128, KT, T])
        rot = sb("rot", [128, 2, S5_TILES, SEQ])
        consts = sb("consts", [128, N_CV])
        masks = sb("masks", [128, 7, 128], U8)
        vecs = sb("vecs", [128, DEPTH, N_PV])
        mats = sb("mats", [128, MATS])
        s5x0 = sb("s5x0", [128, DEPTH, 2, S5_TILES, NSAMP])
        Cg = sb("Cg", [128, S5_TILES, 2, 32])
        Cs = sb("Cs", [128, S5_TILES, 32])
        s5xs = sb("s5xs", [128, 2, S5_TILES, NSAMP])
        s5fin = sb("s5fin", [128, 2, S5_TILES])
        par = sb("par", [128, 20, S5_TILES])
        low = sb("low", [128, 8, HG_FT])
        st_p = sb("st_p", [128, 5, DV])
        S_hg = sb("S_hg", [128, HG_FT, NSAMP, DV])
        S_rt = sb("S_rt", [128, 2, NSAMP, DV])
        near = sb("near", [128, 2, HG_FT, 2, 128])
        V_tok = sb("V_tok", [128, 2, 2, 384])

        with ExitStack() as mixers:
            def msb(name, shape, dt=F32):
                return mixers.enter_context(nc.sbuf_tensor(name, shape, dt))

            scratch = msb("scratch", [128, 8448])
            Kg = msb("Kg", [128, HG_FT, T])
            Qg = msb("Qg", [128, HG_FT, T])
            Fg = msb("Fg", [128, HG_FT, SEQ])
            Fs = msb("Fs", [128, HG_FT, NSAMP])
            U = msb("U", [128, 2, T])
            gates = msb("gates", [128, 6, T])
            QR = msb("QR", [128, 2, T])
            KR = msb("KR", [128, 2, T])
            v_own = msb("v_own", [NSAMP, NSAMP, 128])
            vs_tok = msb("vs_tok", [NSAMP, 2, 384])
            ks_tok = msb("ks_tok", [NSAMP, 640])
            s5tmp = msb("s5tmp", [128, 2, S5_TILES, NSAMP])
            s5last = msb("s5last", [128, 2, S5_TILES])
        with ExitStack() as mlp:
            def fsb(name, shape, dt=F32):
                return mlp.enter_context(nc.sbuf_tensor(name, shape, dt))

            h_high = fsb("h_high", [128, FF_HALF, T], F32R)
            h_low = fsb("h_low", [128, FF_HALF, T], F32R)
            relu = fsb("relu", [128, 2, T])
            h_full = fsb("h_full", [128, 2, T])

        def flat(a, b):
            return scratch[:, a:b]

        P1, P2, W5, Z5 = (flat(512 * i, 512 * i + 512) for i in range(4))
        XS = [flat(2048 + 512 * i, 2560 + 512 * i) for i in range(2)]
        kt_hg = flat(0, 768).rearrange("p (a b) -> p a b", a=2)
        far = flat(768, 1536).rearrange("p (a b c) -> p a b c", a=2, b=3)
        kt_rt = flat(1536, 2048).rearrange("p (a b) -> p a b", a=2)
        qs_rt = flat(2048, 3072).rearrange("p (a b v) -> p a b v", a=2, b=NSAMP)
        qdec = [flat(3072 + 1536 * i, 3840 + 1536 * i).rearrange("p (a b) -> p a b", a=3) for i in range(2)]
        kdec = [flat(3840 + 1536 * i, 4608 + 1536 * i).rearrange("p (a b) -> p a b", a=3) for i in range(2)]
        level_space = flat(3072, 6144)
        qs_hg = flat(6144, 7680).rearrange("p (a b v) -> p a b v", a=3, b=NSAMP)
        RS = flat(6144, 8448).rearrange("p (a b) -> p a b", a=HEADS)
        masks_f32 = flat(6144, 7040).rearrange("p (a b) -> p a b", a=7)
        head_sq = flat(4608, 4608 + 6 * T).rearrange("p (a b) -> p a b", a=6)
        swapped = X1[:, 0:2, :]
        sig_f, sig_n, gel = X1[:, 0:3, :], X1[:, 3:6, :], X1[:, 6:8, :]
        Gg = X1[:, 3:6, :].rearrange("p a b -> p (a b)")[:, 0:3 * SEQ].rearrange("p (a b) -> p a b", a=3)
        Vf, Y = MIX[:, 0:6, :], MIX[:, 6:8, :]
        sq0 = flat(KT * T, KT * T + T)
        sq_r = flat(KT * T + T, KT * T + 2 * T)
        sq = flat(0, KT * T).rearrange("p (a b) -> p a b", a=KT)

        def cv(name):
            a, n = CV[name]
            return consts[:, a:a + n]

        def pv(l, name):
            a, n = PV[name]
            return vecs[:, l, a:a + n]

        ident = cv("ident")
        decay = cv("decay").rearrange("p (h t) -> p h t", h=HEADS)
        k_decay = cv("k_decay").rearrange("p (a b) -> p a b", a=2)
        B_s5 = mats[:, 0:512].rearrange("p (s r n) -> p s r n", s=2, r=2)
        C_s5 = mats[:, 512:1024].rearrange("p (j r c) -> p j r c", j=8, r=2)
        glu_w = mats[:, 1024:1536].rearrange("p (k m) -> p k m", k=2)

        stream_bank = [ctx.enter_context(nc.psum_tensor(f"stream{i}", [128, 512], F32)) for i in range(STREAM_BANKS)]
        mix_bank = [ctx.enter_context(nc.psum_tensor(f"mix{i}", [128, 512], F32)) for i in range(MIX_BANKS)]
        y5_bank = ctx.enter_context(nc.psum_tensor("y5_bank", [128, 2, 256], F32))

        raw_loaded = [sem(f"raw_loaded{i}") for i in range(RAW_SLOTS)]
        x_loaded, const_loaded, mats_loaded, states_loaded = sem("x_loaded"), sem("const_loaded"), sem("mats_loaded"), sem("states_loaded")
        high_ready = sem("high_ready")
        low_ready = sem("low_ready")
        chunk_done = sem("chunk_done")
        tile_free = [sem(f"tile_free{i}") for i in range(STREAM_BANKS)]
        unit_done = sem("unit_done")
        unit_free = [sem(f"unit_free{i}") for i in range(MIX_BANKS)]
        row_tile_done = sem("row_tile_done")
        y5_done, y5_free = sem("y5_done"), sem("y5_free")
        u_ready = sem("u_ready")
        sig_ready = sem("sig_ready")
        qsig_ready = sem("qsig_ready")
        gsig_ready = sem("gsig_ready")
        v_ready = sem("v_ready")
        rqk_ready = sem("rqk_ready")
        vtok_ready = sem("vtok_ready")
        vs_ready = sem("vs_ready")
        ks_ready = sem("ks_ready")
        vown_ready = sem("vown_ready")
        kt_ready = sem("kt_ready")
        ktr_ready = sem("ktr_ready")
        far_ready = sem("far_ready")
        ohg_copied = sem("ohg_copied")
        ort_copied = sem("ort_copied")
        hsq_ready = sem("hsq_ready")
        rsq_ready = sem("rsq_ready")
        hsd_ready = sem("hsd_ready")
        rsd_ready = sem("rsd_ready")
        gel_ready = sem("gel_ready")
        act_params = sem("act_params")
        softmax_exp = sem("softmax_exp")
        lnsq_ready = sem("lnsq_ready")
        lnsd_ready = sem("lnsd_ready")
        relu_ready = sem("relu_ready")
        hhigh_ready = sem("hhigh_ready")
        ahigh_ready = sem("ahigh_ready")
        stp_ready = sem("stp_ready")

        dve_step = sem("dve_step")
        par_ready = sem("par_ready")
        table_ready = sem("table_ready")
        xs_ready = sem("xs_ready")
        xss_ready = sem("xss_ready")
        k_ready = sem("k_ready")
        q_ready = sem("q_ready")
        dec_ready = sem("dec_ready")
        near_ready = sem("near_ready")
        ret_ready = sem("ret_ready")
        rs_ready = sem("rs_ready")
        shg_ready = sem("shg_ready")
        srt_ready = sem("srt_ready")
        qshg_ready = sem("qshg_ready")
        qsrt_ready = sem("qsrt_ready")
        gelarg_ready = sem("gelarg_ready")
        gelu_done = sem("gelu_done")
        glu_done = sem("glu_done")
        orc_ready = sem("orc_ready")
        hmix_ready = sem("hmix_ready")
        rmix_ready = sem("rmix_ready")
        res_ready = sem("res_ready")
        lnc_ready = sem("lnc_ready")
        lns_ready = sem("lns_ready")
        ln_ready = sem("ln_ready")
        hfull_ready = sem("hfull_ready")
        h_ready = sem("h_ready")
        a_ready = sem("a_ready")
        s5fin_ready = sem("s5fin_ready")
        cleared = sem("cleared")
        vown_read = sem("vown_read")
        outs = {n: sem("stored_" + n) for n in ("y", "hg_p", "rt_p", "s5_p", "hg_s", "rt_s", "s5_s")}

        MIX_ORDER = (6, 7, 0, 1, 2, 3, 4, 5)

        def unit_index(l, name):
            return l * N_UNITS + UNIT_AT[name]

        def bank(l, name):
            return mix_bank[unit_index(l, name) % MIX_BANKS]

        def unit_freed(l, name):
            return unit_free[unit_index(l, name) % MIX_BANKS]

        def need(eng, s, n):
            if n > 0:
                eng.wait_ge(s, n)

        def dense_tile(eng, l, c):
            eng.wait_ge(chunk_done, l * N_CHUNKS + c + 1)
            g = l * N_TILES + tile_index(c)
            return stream_bank[g % STREAM_BANKS][:, 0:T], tile_free[g % STREAM_BANKS]

        block = ctx.enter_context(nc.Block())

        @block.sync
        def _(sp):
            for n in range(DEPTH * N_CHUNKS):
                if n >= RAW_SLOTS:
                    sp.wait_ge(low_ready, n - RAW_SLOTS + 1)
                sp.dma_start(w_raw[:, n % RAW_SLOTS, :], weights[n // N_CHUNKS, n % N_CHUNKS]).then_inc(raw_loaded[n % RAW_SLOTS], 16)
            sp.wait_ge(ln_ready, 16 * DEPTH)
            sp.dma_start(y_out, X[:, :, :]).then_inc(outs["y"], 16)
            sp.wait_ge(outs["y"], 16)

        @block.gpsimd
        def _(pool):
            pool.dma_start(vecs[:, :, :], vectors).then_inc(const_loaded, 16)
            pool.dma_start(masks_f32, level_masks).then_inc(const_loaded, 16)
            pool.dma_start(consts[:, :], constants).then_inc(const_loaded, 16)
            pool.dma_start(s5x0[:, :, :, :, :], state_s5).then_inc(const_loaded, 16)
            pool.memset(near[:, :, :, :, :], 0.0).then_inc(cleared, 1)
            pool.memset(st_p[:, :, :], 0.0).then_inc(cleared, 1)
            pool.memset(level_space, 0.0).then_inc(cleared, 1)
            for l in range(DEPTH):
                if l:
                    pool.wait_ge(unit_done, unit_index(l - 1, ("glu", 1)) + 1)
                    pool.wait_ge(table_ready, l)
                pool.dma_start(mats[:, :], matrices[l]).then_inc(mats_loaded, 16)
                if l:
                    pool.wait_ge(outs["hg_s"], 16 * l)
                    pool.wait_ge(outs["rt_s"], 16 * l)
                    pool.wait_ge(qshg_ready, l)
                    pool.wait_ge(qsrt_ready, l)
                pool.dma_start(S_hg[:, :, :, :], state_hg[l]).then_inc(states_loaded, 16)
                pool.dma_start(S_rt[:, :, :, :], state_rt[l]).then_inc(states_loaded, 16)
                if l:
                    pool.wait_ge(chunk_done, l * N_CHUNKS)
                    pool.memset(level_space, 0.0).then_inc(cleared, 1)
                for i in range(6):
                    pool.wait_ge(vs_ready, 2 * l + i // 3 + 1)
                    if 1 <= i <= 3:
                        pool.wait_ge(unit_done, unit_index(l, ("hg_kv", i - 1)) + 1)
                    elif i >= 4:
                        pool.wait_ge(vown_read, 2 * l + i - 3)
                    elif l:
                        pool.wait_ge(unit_done, unit_index(l - 1, ("ret_kv", 1)) + 1)
                    src = vs_tok[:, i // 3, 128 * (i % 3):128 * (i % 3) + 128]
                    pool.affine_select(out=v_own[:, :, :], in_=src.unsqueeze(1).broadcast_to([NSAMP, NSAMP, 128]),
                                       compare_op=ALU.is_equal, fill=0.0, base=0, pattern=[[-1, NSAMP], [0, 128]],
                                       channel_multiplier=1).then_inc(vown_ready, 1)
                    if i == 2:
                        pool.wait_ge(shg_ready, 3 * l + 3)
                        pool.dma_start(hg_s_out[l], S_hg[:, :, :, :]).then_inc(outs["hg_s"], 16)
                pool.wait_ge(srt_ready, 2 * l + 2)
                pool.dma_start(rt_s_out[l], S_rt[:, :, :, :]).then_inc(outs["rt_s"], 16)
                pool.wait_ge(s5fin_ready, 2 * l + 2)
                pool.dma_start(s5_p_out[l], s5fin[:, :, :]).then_inc(outs["s5_p"], 16)
                pool.dma_start(s5_s_out[l], s5xs[:, :, :, :]).then_inc(outs["s5_s"], 16)
                pool.wait_ge(stp_ready, 3 * l + 3)
                pool.dma_start(hg_p_out[l], st_p[:, 0:3, :]).then_inc(outs["hg_p"], 16)
                pool.dma_start(rt_p_out[l], st_p[:, 3:5, :]).then_inc(outs["rt_p"], 16)
            for n in ("hg_p", "rt_p", "s5_p", "hg_s", "rt_s", "s5_s"):
                pool.wait_ge(outs[n], 16 * DEPTH)

        @block.tensor
        def _(pe):
            def unit(l, name):
                g = unit_index(l, name)
                need(pe, unit_free[g % MIX_BANKS], g // MIX_BANKS)
                return mix_bank[g % MIX_BANKS]

            fences = [0]

            def row_tile_fence(mm):
                fences[0] += 1
                mm.then_inc(row_tile_done, 1)
                pe.wait_ge(row_tile_done, fences[0])

            def s5_in(l, u):
                j = u[1]
                if j == 0:
                    pe.wait_ge(u_ready, 2 * l + 2)
                    pe.wait_ge(mats_loaded, 16 * (l + 1))
                b = unit(l, u)
                q = 32 * (j % 4)
                for r in range(2):
                    mm = pe.matmul(b[:, 256 * r:256 * r + 256], B_s5[q:q + 32, j // 4, r, :], U[q:q + 32, j // 4, 0:256], start=True, stop=True, tile_position=(q, 0))
                mm.then_inc(unit_done, 1)

            def s5_in_sample(l, u):
                b = unit(l, u)
                bv = b[:, 0:128].rearrange("p (r j t) -> p r j t", r=2, j=8)
                for q in range(0, 128, 32):
                    for s in range(2):
                        for r in range(2):
                            mm = pe.matmul(bv[:, r, 4 * s + q // 32, :], B_s5[q:q + 32, s, r, :], U[q:q + 32, s, 256:T], start=True, stop=True, tile_position=(q, 0))
                    if q < 96:
                        row_tile_fence(mm)
                mm.then_inc(unit_done, 1)

            def s5_out(l, u):
                j = u[1]
                if j == 0:
                    need(pe, y5_free, l)
                    pe.wait_ge(table_ready, l + 1)
                pe.wait_ge(xs_ready, 8 * l + j + 1)
                q = 32 * (j % 4)
                o = y5_bank[q:q + 32, j // 4, :]
                pe.matmul(o, Cg[:, j, 0, :], XS[j % 2][:, 0:256], start=True, stop=False, tile_position=(0, q))
                pe.matmul(o, Cg[:, j, 1, :], XS[j % 2][:, 256:512], start=False, stop=True, tile_position=(0, q)).then_inc(y5_done, 1)

            def s5_out_sample(l, u):
                pe.wait_ge(xss_ready, l + 1)
                b = unit(l, u)
                for j in range(8):
                    q = 32 * (j % 4)
                    o = b[q:q + 32, 8 * (j // 4):8 * (j // 4) + 8]
                    pe.matmul(o, C_s5[:, j, 0, :], s5xs[:, 0, j, :], start=True, stop=False, tile_position=(0, q))
                    mm = pe.matmul(o, Cs[:, j, :], s5xs[:, 1, j, :], start=False, stop=True, tile_position=(0, q))
                mm.then_inc(unit_done, 1)

            def transposes(l, u, src, rows, cols):
                b = unit(l, u)
                for i in range(src.shape[1]):
                    mm = pe.transpose(b[0:rows, 128 * i:128 * i + 128], src[:, i, cols], ident)
                mm.then_inc(unit_done, 1)

            def token_tile(t):
                return slice(128 * t, 128 * t + 128)

            sample = slice(SEQ, T)

            def tr_hi(l, u):
                pe.wait_ge(v_ready, 6 * l + 3)
                transposes(l, u, Vf[:, 0:3, :], 128, token_tile(u[1]))

            def tr_hi_sample(l, u):
                transposes(l, u, Vf[:, 0:3, :], NSAMP, sample)

            def tr_rv(l, u):
                transposes(l, u, Vf[:, 3:6, :], 128, token_tile(u[1]))

            def tr_rv_sample(l, u):
                pe.wait_ge(v_ready, 6 * l + 6)
                transposes(l, u, Vf[:, 3:6, :], NSAMP, sample)

            def tr_hk_sample(l, u):
                pe.wait_ge(k_ready, l + 1)
                transposes(l, u, Kg, NSAMP, sample)

            def tr_rk_sample(l, u):
                pe.wait_ge(ret_ready, 2 * l + 1)
                transposes(l, u, KR, NSAMP, sample)

            def tr_rk(l, u):
                transposes(l, u, KR, 128, token_tile(u[1]))

            def tr_hkd(l, u):
                pe.wait_ge(dec_ready, 9 * l + 9)
                transposes(l, u, kdec[0], 128, token_tile(u[1]))

            def hg_level(l, u):
                r, part = u[1:]
                if r == 0:
                    pe.wait_ge(q_ready, l + 1)
                pe.wait_ge(dec_ready, 9 * l + r + 1)
                b = unit(l, u)
                for c, (h, f, t) in enumerate(NEAR_PARTS[part]):
                    if c == 2 and part == 2:
                        row_tile_fence(mm)
                    rows = slice(64 * h, 64 * h + 64)
                    pos = (64 * h, 0)
                    o = b[:, 128 * c:128 * c + 128]
                    if r == 0:
                        ov = o.rearrange("p (n c) -> p n c", c=2)
                        qv = Qg[rows, f, token_tile(t)].rearrange("p (n c) -> p n c", c=2)
                        pe.matmul(ov[:, :, 0], Kg[rows, f, token_tile(t)], qv[:, :, 0], start=True, stop=True, tile_position=pos)
                        mm = pe.matmul(ov[:, :, 1], kdec[0][rows, f, token_tile(t)], qv[:, :, 1], start=True, stop=True, tile_position=pos)
                    else:
                        mm = pe.matmul(o, kdec[r % 2][rows, f, token_tile(t)], qdec[r % 2][rows, f, token_tile(t)], start=True, stop=True, tile_position=pos)
                mm.then_inc(unit_done, 1)

            def hg_far(l, u):
                pe.wait_ge(dec_ready, 9 * l + 8)
                b = unit(l, u)
                h = u[1]
                for f in range(3):
                    mm = pe.matmul(b[:, 128 * f:128 * f + 128], kdec[1][64 * h:64 * h + 64, f, 0:128],
                                   qdec[1][64 * h:64 * h + 64, f, 128:256], start=True, stop=True, tile_position=(64 * h, 0))
                mm.then_inc(unit_done, 1)

            def hg_state(l, u):
                pe.wait_ge(kt_ready, 2 * l + 2)
                b = unit(l, u)
                for h in range(HEADS):
                    o = b[64 * (h % 2):64 * (h % 2) + 64, 64 * (h // 2):64 * (h // 2) + 64]
                    for t in range(2):
                        mm = pe.matmul(o, kt_hg[:, t, 64 * h:64 * h + 64], V_tok[:, t, 0, 64 * h:64 * h + 64], start=(t == 0), stop=(t == 1),
                                       tile_position=(0, 64 * (h % 2)))
                mm.then_inc(unit_done, 1)

            def hg_kv(l, u):
                ft = u[1]
                pe.wait_ge(ks_ready, 2 * l + 1)
                pe.wait_ge(vown_ready, 6 * l + ft + 1)
                b = unit(l, u)
                for h in range(2):
                    mm = pe.matmul(b[64 * h:64 * h + 64, :].rearrange("p (b v) -> p b v", b=8), ks_tok[:, 128 * ft + 64 * h:128 * ft + 64 * h + 64],
                                   v_own[:, :, 64 * h:64 * h + 64], start=True, stop=True, tile_position=(0, 64 * h))
                mm.then_inc(unit_done, 1)

            def ret_kv(l, u):
                i = u[1]
                pe.wait_ge(ks_ready, 2 * l + 2)
                b = unit(l, u)
                for h in range(4 * i, min(4 * i + 4, HEADS)):
                    pe.wait_ge(vown_ready, 6 * l + 3 + h // 2 + 1)
                    o = b[32 * (h % 4):32 * (h % 4) + 32, :].rearrange("p (b v) -> p b v", b=8)
                    mm = pe.matmul(o, ks_tok[:, 384 + 32 * h:384 + 32 * h + 32], v_own[:, :, 64 * (h % 2):64 * (h % 2) + 64],
                                   start=True, stop=True, tile_position=(0, 32 * (h % 4)))
                    if h == 1:
                        mm.then_inc(vown_read, 1)
                    if h == 3:
                        mm.then_inc(vown_read, 1)
                        pe.wait_ge(vown_read, 2 * l + 2)
                        pe.sem_inc(unit_done, 1)
                    if h == 5:
                        mm.then_inc(unit_done, 1)

            def hg_o(l, u):
                ft = u[1]
                if ft == 0:
                    pe.wait_ge(near_ready, 7 * l + 7)
                    pe.wait_ge(far_ready, 2 * l + 2)
                    pe.wait_ge(vtok_ready, 4 * l + 2)
                b = unit(l, u)
                for h in range(2):
                    o = b[64 * h:64 * h + 64, :]
                    hc = slice(128 * ft + 64 * h, 128 * ft + 64 * h + 64)
                    pos = (0, 64 * h)
                    pe.matmul(o[:, 0:128], V_tok[:, 0, 0, hc], near[:, h, ft, 0, :], start=True, stop=True, tile_position=pos)
                    pe.matmul(o[:, 128:256], V_tok[:, 0, 0, hc], far[:, h, ft, :], start=True, stop=False, tile_position=pos)
                    mm = pe.matmul(o[:, 128:256], V_tok[:, 1, 0, hc], near[:, h, ft, 1, :], start=False, stop=True, tile_position=pos)
                mm.then_inc(unit_done, 1)

            def hg_o_sample(l, u):
                pe.wait_ge(qshg_ready, l + 1)
                b = unit(l, u)
                for ft in range(3):
                    for bp in range(NSAMP // 2):
                        at = 2 * (4 * ft + bp)
                        mm = pe.matmul(b[:, at:at + 2], qs_hg[:, ft, 2 * bp:2 * bp + 2, :].rearrange("p b v -> p (b v)"), cv("pair_sum"), start=True, stop=True)
                mm.then_inc(unit_done, 1)

            def ret_o_sample(l, u):
                pe.wait_ge(qsrt_ready, l + 1)
                b = unit(l, u)
                for bp in range(NSAMP // 2):
                    pe.matmul(b[:, 4 * bp:4 * bp + 4], qs_rt[:, 0, 2 * bp:2 * bp + 2, :].rearrange("p b v -> p (b v)"), cv("quad_sum"), start=True, stop=True)
                for bp in range(NSAMP // 2):
                    mm = pe.matmul(b[:, 16 + 4 * bp:20 + 4 * bp], qs_rt[:, 1, 2 * bp:2 * bp + 2, :].rearrange("p b v -> p (b v)"), cv("quad_sum"), start=True, stop=True)
                mm.then_inc(unit_done, 1)

            def ret_score(l, u):
                h = u[1]
                pe.wait_ge(ret_ready, 2 * l + 2)
                b = unit(l, u)
                q, i = 32 * (h % 4), h // 4
                pe.matmul(b[:, 0:256], KR[q:q + 32, i, 0:128], QR[q:q + 32, i, 0:256], start=True, stop=True, tile_position=(q, 0))
                pe.matmul(b[:, 256:384], KR[q:q + 32, i, 128:256], QR[q:q + 32, i, 128:256], start=True, stop=True, tile_position=(q, 0)).then_inc(unit_done, 1)

            def ret_state(l, u):
                pe.wait_ge(ktr_ready, 2 * l + 2)
                pe.wait_ge(vtok_ready, 4 * l + 4)
                b = unit(l, u)
                for h in range(HEADS):
                    q, i = 32 * (h % 4), h // 4
                    for t in range(2):
                        mm = pe.matmul(b[q:q + 32, 64 * i:64 * i + 64], kt_rt[:, t, 32 * h:32 * h + 32], V_tok[:, t, 1, 64 * h:64 * h + 64],
                                       start=(t == 0), stop=(t == 1), tile_position=(0, q))
                mm.then_inc(unit_done, 1)

            def ret_o(l, u):
                ft = u[1]
                pe.wait_ge(rs_ready, 6 * l + 2 * ft + 2)
                pe.wait_ge(vtok_ready, 4 * l + 4)
                b = unit(l, u)
                for hh in range(2):
                    h = 2 * ft + hh
                    o = b[64 * hh:64 * hh + 64, :]
                    hc = slice(64 * h, 64 * h + 64)
                    pos = (0, 64 * hh)
                    pe.matmul(o[:, 0:128], V_tok[:, 0, 1, hc], RS[:, h, 0:128], start=True, stop=True, tile_position=pos)
                    pe.matmul(o[:, 128:256], V_tok[:, 0, 1, hc], RS[:, h, 128:256], start=True, stop=False, tile_position=pos)
                    mm = pe.matmul(o[:, 128:256], V_tok[:, 1, 1, hc], RS[:, h, 256:384], start=False, stop=True, tile_position=pos)
                mm.then_inc(unit_done, 1)

            def glu(l, u):
                pe.wait_ge(gelu_done, l + 1)
                b = unit(l, u)
                for k in range(2):
                    mm = pe.matmul(b[:, 0:T], glu_w[:, k, 128 * u[1]:128 * u[1] + 128], Y[:, k, :], start=(k == 0), stop=(k == 1))
                mm.then_inc(unit_done, 1)

            def head_mean(l, u, src):
                b = unit(l, u)
                pe.matmul(b[:, 0:T], cv("head_mean"), src, start=True, stop=True).then_inc(unit_done, 1)

            def hg_ms(l, u):
                pe.wait_ge(hsq_ready, 3 * l + u[1] + 1)
                head_mean(l, u, head_sq[:, u[1], :])

            def ret_mu(l, u):
                pe.wait_ge(ort_copied, 11 * l + 8 + u[1] + 1)
                head_mean(l, u, MIX[:, 3 + u[1], :])

            def ret_var(l, u):
                pe.wait_ge(rsq_ready, 3 * l + u[1] + 1)
                head_mean(l, u, head_sq[:, 3 + u[1], :])

            def model_mean(l, u, w, ready, src):
                b = unit(l, u)
                for k in range(KT):
                    pe.wait_ge(ready, 16 * l + 8 * w + k + 1)
                    mm = pe.matmul(b[:, 0:T], cv("model_mean"), src[:, k, :], start=(k == 0), stop=(k == KT - 1))
                mm.then_inc(unit_done, 1)

            def ln1_mu(l, u):
                model_mean(l, u, 0, res_ready, X1)

            def ln1_var(l, u):
                model_mean(l, u, 0, lnsq_ready, sq)

            def ln2_mu(l, u):
                model_mean(l, u, 1, res_ready, X)

            def ln2_var(l, u):
                model_mean(l, u, 1, lnsq_ready, sq)

            units = dict(s5_in=s5_in, s5_in_sample=s5_in_sample, s5_out=s5_out, s5_out_sample=s5_out_sample, tr_hi=tr_hi, tr_hi_sample=tr_hi_sample,
                         tr_rv=tr_rv, tr_rv_sample=tr_rv_sample, tr_hk_sample=tr_hk_sample, tr_rk_sample=tr_rk_sample, tr_rk=tr_rk, tr_hkd=tr_hkd,
                         hg_level=hg_level, hg_far=hg_far, hg_state=hg_state, hg_kv=hg_kv, ret_kv=ret_kv, hg_o=hg_o, hg_o_sample=hg_o_sample,
                         ret_o_sample=ret_o_sample, ret_score=ret_score, ret_state=ret_state, ret_o=ret_o, glu=glu, hg_ms=hg_ms, ret_mu=ret_mu,
                         ret_var=ret_var, ln1_mu=ln1_mu, ln1_var=ln1_var, ln2_mu=ln2_mu, ln2_var=ln2_var)

            pe.wait_ge(const_loaded, 64)
            for l in range(DEPTH):
                for c in range(N_CHUNKS):
                    n = l * N_CHUNKS + c
                    g = l * N_TILES + tile_index(c)
                    bnk = stream_bank[g % STREAM_BANKS]
                    first = c < DOWN_A or (UP_B <= c < DOWN_B) or (c - DOWN_A) % 2 == 0
                    last = c < DOWN_A or (UP_B <= c < DOWN_B) or (c - DOWN_A) % 2 == 1
                    if first:
                        need(pe, tile_free[g % STREAM_BANKS], g // STREAM_BANKS)
                    pe.wait_ge(low_ready, n + 1)
                    down = DOWN_A <= c < UP_B or c >= DOWN_B
                    for kk in range(8):
                        if down:
                            k = kk + (0 if first else 8)
                            xh, xl = h_high[:, k, :], h_low[:, k, :]
                            if c in (DOWN_A, DOWN_A + 1, DOWN_B, DOWN_B + 1):
                                pe.wait_ge(h_ready, 32 * l + (FF_HALF if c >= DOWN_B else 0) + k + 1)
                        else:
                            k = MIX_ORDER[kk] if OUT0 <= c < UP_A else kk
                            xh, xl = a_high[:, k, :], a_low[:, k, :]
                            if c in (0, OUT0, UP_A):
                                pe.wait_ge(a_ready, 24 * l + 8 * (0, OUT0, UP_A).index(c) + kk + 1)
                        blk = slice(128 * k % CHUNK, 128 * k % CHUNK + 128)
                        wh, wl = w_high[:, n % SPLIT_SLOTS, blk], w_low[:, n % SPLIT_SLOTS, blk]
                        pe.matmul(bnk[:, 0:T], wh, xh, start=(first and kk == 0), stop=False)
                        pe.matmul(bnk[:, 0:T], wh, xl, start=False, stop=False)
                        mm = pe.matmul(bnk[:, 0:T], wl, xh, start=False, stop=(last and kk == 7))
                    mm.then_inc(chunk_done, 1)
                    for u in PLAN[c]:
                        units[u[0]](l, u)

        @block.scalar
        def _(act):
            def tile(l, c):
                return dense_tile(act, l, c)

            def got(l, name):
                act.wait_ge(unit_done, unit_index(l, name) + 1)
                return bank(l, name), unit_freed(l, name)

            def copied(s, n, freed):
                act.wait_ge(s, n)
                act.sem_inc(freed, 1)

            def split_high(n):
                if n >= DEPTH * N_CHUNKS:
                    return
                act.wait_ge(raw_loaded[n % RAW_SLOTS], 16 * (n // RAW_SLOTS + 1))
                if n >= SPLIT_SLOTS:
                    act.wait_ge(chunk_done, n - SPLIT_SLOTS + 1)
                act.activation(w_high[:, n % SPLIT_SLOTS, :], w_raw[:, n % RAW_SLOTS, :], ACT.Copy).then_inc(high_ready, 1)

            def s5_dt(l):
                act.activation(par[:, 0, :], pv(l, "log_dt"), ACT.Exp).then_inc(act_params, 1)

            def s5_sin(l):
                act.wait_ge(par_ready, l + 1)
                act.activation(par[:, 3:5, :], par[:, 1:3, :], ACT.Sin).then_inc(act_params, 1)

            def gate_sigmoid(l, i):
                p, _ = tile(l, HGT + i)
                act.activation(gates[:, i, :], p, ACT.Sigmoid).then_inc(gsig_ready, 1)

            def mixer_work(l, c):
                if c in (1, 2):
                    i = c - 1
                    p, fr = tile(l, SU + i)
                    act.activation(U[:, i, :], p, ACT.Copy).then_inc(u_ready, 1)
                    copied(u_ready, 2 * l + i + 1, fr)
                elif HF < c <= HF + 3:
                    i = c - 1 - HF
                    p, fr = tile(l, HF + i)
                    act.activation(sig_f[:, i, :], p, ACT.Sigmoid).then_inc(sig_ready, 1)
                    act.activation(sig_n[:, i, :], p, ACT.Sigmoid, scale=-1.0).then_inc(sig_ready, 1)
                    copied(sig_ready, 6 * l + 2 * i + 2, fr)
                elif HQ < c <= HQ + 3:
                    i = c - 1 - HQ
                    p, fr = tile(l, HQ + i)
                    act.activation(Qg[:, i, :], p, ACT.Sigmoid).then_inc(qsig_ready, 1)
                elif HI < c <= HI + 3:
                    i = c - 1 - HI
                    p, fr = tile(l, HI + i)
                    act.activation(Vf[:, i, :], p, ACT.Copy).then_inc(v_ready, 1)
                    copied(v_ready, 6 * l + i + 1, fr)
                elif RQ < c <= RQ + 4:
                    i = c - 1 - RQ
                    p, fr = tile(l, RQ + i)
                    dst = QR[:, i, :] if i < 2 else KR[:, i - 2, :]
                    act.activation(dst, p, ACT.Copy, scale=1.0 if i < 2 else RET_DK ** -0.5).then_inc(rqk_ready, 1)
                    copied(rqk_ready, 4 * l + i + 1, fr)
                elif RV < c <= RV + 3:
                    i = c - 1 - RV
                    p, fr = tile(l, RV + i)
                    act.activation(Vf[:, 3 + i, :], p, ACT.Copy).then_inc(v_ready, 1)
                    copied(v_ready, 6 * l + 3 + i + 1, fr)
                elif HGT < c <= HGT + 5:
                    gate_sigmoid(l, c - 1 - HGT)
                if c == 12:
                    for t in range(2):
                        b, fu = got(l, ("tr_hi", t))
                        act.activation(V_tok[:, t, 0, :], b[:, 0:384], ACT.Copy).then_inc(vtok_ready, 1)
                        copied(vtok_ready, 4 * l + t + 1, fu)
                    b, fu = got(l, ("tr_hi_sample",))
                    act.activation(vs_tok[:, 0, :], b[0:NSAMP, 0:384], ACT.Copy).then_inc(vs_ready, 1)
                    copied(vs_ready, 2 * l + 1, fu)
                    b, fu = got(l, ("tr_hk_sample",))
                    act.activation(ks_tok[:, 0:384], b[0:NSAMP, 0:384], ACT.Copy).then_inc(ks_ready, 1)
                    copied(ks_ready, 2 * l + 1, fu)
                if c == 14:
                    act.wait_ge(gelarg_ready, l + 1)
                    act.activation(gel, gel, ACT.Sigmoid).then_inc(gel_ready, 1)
                if c == 16:
                    for m in range(2):
                        b, fu = got(l, ("glu", m))
                        act.activation(gel[:, m, :], b[:, 0:T], ACT.Sigmoid, bias=pv(l, "glu_b")[:, m:m + 1]).then_inc(gel_ready, 1)
                        copied(gel_ready, 3 * l + m + 2, fu)
                if c == 19:
                    b, fu = got(l, ("hg_o_sample",))
                    pv_ = b[:, 0:24].rearrange("p (f b h) -> p f b h", f=3, b=4)
                    for h in range(2):
                        for bb in range(2):
                            dst = MIX[64 * h:64 * h + 64, 0:3, SEQ:T].rearrange("p f (b c) -> p f b c", c=2)[:, :, :, bb]
                            act.activation(dst, pv_[64 * bb:64 * bb + 64, :, :, h], ACT.Copy).then_inc(ohg_copied, 1)
                    copied(ohg_copied, 7 * l + 4, fu)
                    b, fu = got(l, ("tr_rv_sample",))
                    act.activation(vs_tok[:, 1, :], b[0:NSAMP, 0:384], ACT.Copy).then_inc(vs_ready, 1)
                    copied(vs_ready, 2 * l + 2, fu)
                    b, fu = got(l, ("tr_rk_sample",))
                    act.activation(ks_tok[:, 384:640], b[0:NSAMP, 0:256], ACT.Copy).then_inc(ks_ready, 1)
                    copied(ks_ready, 2 * l + 2, fu)
                if c == 20:
                    for h in range(2):
                        b, fu = got(l, ("hg_far", h))
                        act.activation(far[:, h, :, :], b[:, 0:384].rearrange("p (a b) -> p a b", a=3), ACT.Copy).then_inc(far_ready, 1)
                        copied(far_ready, 2 * l + h + 1, fu)
                    for t in range(2):
                        b, fu = got(l, ("tr_hkd", t))
                        act.activation(kt_hg[:, t, :], b[:, 0:384], ACT.Copy).then_inc(kt_ready, 1)
                        copied(kt_ready, 2 * l + t + 1, fu)
                    for t in range(2):
                        b, fu = got(l, ("tr_rv", t))
                        act.activation(V_tok[:, t, 1, :], b[:, 0:384], ACT.Copy).then_inc(vtok_ready, 1)
                        copied(vtok_ready, 4 * l + 2 + t + 1, fu)
                if c == 22:
                    for ft in range(3):
                        b, fu = got(l, ("hg_o", ft))
                        act.activation(MIX[:, ft, 0:SEQ], b[:, 0:SEQ], ACT.Copy).then_inc(ohg_copied, 1)
                        copied(ohg_copied, 7 * l + 4 + ft + 1, fu)
                        act.activation(head_sq[:, ft, :], MIX[:, ft, :], ACT.Square).then_inc(hsq_ready, 1)
                    b, fu = got(l, ("hg_state",))
                    if l:
                        act.wait_ge(outs["hg_p"], 16 * l)
                        act.wait_ge(outs["rt_p"], 16 * l)
                    act.activation(st_p[:, 0:3, :], b[:, 0:192].rearrange("p (a b) -> p a b", a=3), ACT.Copy).then_inc(stp_ready, 1)
                    copied(stp_ready, 3 * l + 1, fu)
                if c == 23:
                    b, fu = got(l, ("ret_state",))
                    act.activation(st_p[:, 3, :], b[:, 0:64], ACT.Copy).then_inc(stp_ready, 1)
                    act.activation(st_p[0:64, 4, :], b[0:64, 64:128], ACT.Copy).then_inc(stp_ready, 1)
                    copied(stp_ready, 3 * l + 3, fu)

            def split_a(l, part, src, ready, n):
                act.wait_ge(ready, n)
                act.activation(a_high[:, src[1], :], src[0][:, src[1], :], ACT.Copy).then_inc(ahigh_ready, 1)

            def mixer_end(l):
                gate_sigmoid(l, 5)
                for i in (6, 7):
                    split_a(l, 1, (MIX, i), glu_done, l + 1)
                b, fu = got(l, ("ret_o_sample",))
                pq = b[:, 0:32].rearrange("p (i b h) -> p i b h", i=2, b=4)
                for hp in range(2):
                    for bb in range(2):
                        dst = MIX[64 * hp:64 * hp + 64, 3:6, SEQ:T].rearrange("p f (b c) -> p f b c", c=2)[:, :, :, bb]
                        src = pq[64 * bb:64 * bb + 64, :, :, :]
                        act.activation(dst[:, 0:2, :], src[:, 0, :, hp::2].rearrange("p b h -> p h b"), ACT.Copy).then_inc(ort_copied, 1)
                        act.activation(dst[:, 2, :], src[:, 1, :, hp], ACT.Copy).then_inc(ort_copied, 1)
                copied(ort_copied, 11 * l + 8, fu)
                for ft in range(3):
                    b, fu = got(l, ("ret_o", ft))
                    act.activation(MIX[:, 3 + ft, 0:SEQ], b[:, 0:SEQ], ACT.Copy).then_inc(ort_copied, 1)
                    copied(ort_copied, 11 * l + 8 + ft + 1, fu)
                for ft in range(3):
                    b, fu = got(l, ("hg_ms", ft))
                    act.activation(head_sq[:, ft, :], b[:, 0:T], ACT.Sqrt, bias=cv("eps")).then_inc(hsd_ready, 1)
                    copied(hsd_ready, 3 * l + ft + 1, fu)
                for ft in range(3):
                    act.wait_ge(orc_ready, 3 * l + ft + 1)
                    act.activation(head_sq[:, 3 + ft, :], MIX[:, 3 + ft, :], ACT.Square).then_inc(rsq_ready, 1)
                for ft in range(3):
                    b, fu = got(l, ("ret_var", ft))
                    act.activation(head_sq[:, 3 + ft, :], b[:, 0:T], ACT.Sqrt, bias=cv("eps")).then_inc(rsd_ready, 1)
                    copied(rsd_ready, 3 * l + ft + 1, fu)
                for i in range(3):
                    split_a(l, 1, (MIX, i), hmix_ready, l + 1)
                for i in range(3, 6):
                    split_a(l, 1, (MIX, i), rmix_ready, l + 1)

            def norm(l, w):
                x = X1 if w == 0 else X
                for m in range(KT):
                    act.wait_ge(lnc_ready, 16 * l + 8 * w + m + 1)
                    act.activation(sq[:, m, :], x[:, m, :], ACT.Square).then_inc(lnsq_ready, 1)
                b, fu = got(l, (f"ln{w + 1}_var",))
                act.activation(sq[:, 0, :], b[:, 0:T], ACT.Sqrt, bias=cv("eps")).then_inc(lnsd_ready, 1)
                copied(lnsd_ready, 2 * l + w + 1, fu)
                if w and l == DEPTH - 1:
                    return
                for m in range(KT):
                    act.wait_ge(lns_ready, 16 * l + 8 * w + m + 1)
                    act.activation(a_high[:, m, :], sq[:, m, :] if m else sq0, ACT.Identity, scale=pv(l, f"ln{w + 1}_w")[:, m:m + 1],
                                   bias=pv(l, f"ln{w + 1}_b")[:, m:m + 1]).then_inc(ahigh_ready, 1)

            def hidden(l, m):
                c = UP_A + m if m < FF_HALF else UP_B + m - FF_HALF
                p, fr = tile(l, c)
                n = 32 * l + m
                if m >= 2 or l:
                    act.wait_ge(hfull_ready, n - 1)
                act.activation(relu[:, m % 2, :], p, ACT.Relu).then_inc(relu_ready, 1)
                copied(relu_ready, n + 1, fr)
                act.wait_ge(hfull_ready, n + 1)
                act.activation(h_high[:, m % FF_HALF, :], h_full[:, m % 2, :], ACT.Copy).then_inc(hhigh_ready, 1)

            act.dma_start(X[:, :, :], xT).then_inc(x_loaded, 16)
            act.wait_ge(const_loaded, 64)
            s5_dt(0)
            s5_sin(0)
            act.wait_ge(dve_step, 3)
            act.activation(low[:, 0:2, :], low[:, 2:4, :], ACT.Exp).then_inc(softmax_exp, 1)
            act.wait_ge(x_loaded, 16)
            for m in range(KT):
                act.activation(a_high[:, m, :], X[:, m, :], ACT.Copy).then_inc(ahigh_ready, 1)
            for n in range(AHEAD):
                split_high(n)
            for l in range(DEPTH):
                for c in range(N_CHUNKS):
                    split_high(l * N_CHUNKS + c + AHEAD)
                    if c < N_IN:
                        mixer_work(l, c)
                        if c == N_IN - 1:
                            mixer_end(l)
                    elif c == UP_A - 1:
                        norm(l, 0)
                        if l + 1 < DEPTH:
                            act.wait_ge(table_ready, l + 1)
                            s5_dt(l + 1)
                    elif UP_A < c <= DOWN_A:
                        hidden(l, c - 1 - UP_A)
                    elif c == DOWN_A + 3 and l + 1 < DEPTH:
                        s5_sin(l + 1)
                    elif UP_B < c <= DOWN_B:
                        hidden(l, c - 1 - UP_B + FF_HALF)
                norm(l, 1)

        @block.vector
        def _(dve):
            last = {"sem": None, "n": 0}
            count = {}

            def put(ins, s=None):
                s = dve_step if s is None else s
                count[s.name] = count.get(s.name, 0) + 1
                ins.then_inc(s, 1)
                last["sem"], last["n"] = s, count[s.name]

            def settle():
                dve.wait_ge(last["sem"], last["n"])

            def chain(ins, s=None):
                put(ins, s)
                settle()

            def free(s):
                settle()
                dve.sem_inc(s, 1)

            def got(l, name):
                dve.wait_ge(unit_done, unit_index(l, name) + 1)
                return bank(l, name), unit_freed(l, name)

            def tile(l, c):
                return dense_tile(dve, l, c)

            tt, ts, stt, cp = dve.tensor_tensor, dve.tensor_scalar, dve.scalar_tensor_tensor, dve.tensor_copy
            DT, RC, RS_, COS, SIN, TH, ZR, EX, MAG, ABR, ABI, DEN, GR, GI, T0, T1, T2, PC, PS, NR = range(20)

            def row(i):
                return par[:, i, :]

            def split_low(n):
                if n >= DEPTH * N_CHUNKS:
                    return
                dve.wait_ge(high_ready, n + 1)
                put(tt(w_low[:, n % SPLIT_SLOTS, :], w_raw[:, n % RAW_SLOTS, :], w_high[:, n % SPLIT_SLOTS, :].bitcast(F32), ALU.subtract), low_ready)

            def split_a(l, part, k, src, m):
                dve.wait_ge(ahigh_ready, 24 * l + 8 * part + k + 1)
                put(tt(a_low[:, m, :], src[:, m, :], a_high[:, m, :].bitcast(F32), ALU.subtract), a_ready)

            rot_tmp = MIX[:, :, :].rearrange("p a b -> p (a b)")

            def s5_tables(l):
                are, aim = pv(l, "a_re"), pv(l, "a_im")
                dve.wait_ge(act_params, 2 * l + 1)
                chain(tt(row(TH), row(DT), aim, ALU.mult))
                two_pi_hi, two_pi_lo = 6.28125, float(2 * np.pi - 6.28125)
                magic = 12582912.0
                for dst, shift in ((RS_, 0.0), (RC, 0.25)):
                    chain(ts(row(T0), row(TH), float(1 / (2 * np.pi)), shift, ALU.mult, ALU.add))
                    chain(ts(row(T0), row(T0), magic, None, ALU.add))
                    chain(ts(row(T0), row(T0), -magic, None, ALU.add))
                    chain(stt(row(T1), row(T0), -two_pi_hi, row(TH), ALU.mult, ALU.add))
                    chain(stt(row(T1), row(T0), -two_pi_lo, row(T1), ALU.mult, ALU.add))
                    chain(ts(row(T1), row(T1), float(shift * 2 * np.pi), None, ALU.add))
                    chain(ts(row(dst), row(T1), 3.1415925, -3.1415925, ALU.min, ALU.max), par_ready if dst == RC else None)
                yield
                chain(tt(row(ZR), row(DT), are, ALU.mult))
                chain(ts(row(ZR), row(ZR), 1.0 / 16, None, ALU.mult))
                chain(ts(row(EX), row(ZR), 1.0 / 8, 1.0, ALU.mult, ALU.add))
                for n in range(7, 0, -1):
                    chain(tt(row(EX), row(EX), row(ZR), ALU.mult))
                    chain(ts(row(EX), row(EX), 1.0 / n, 1.0, ALU.mult, ALU.add))
                yield
                for n in range(4):
                    chain(tt(row(MAG if n == 3 else EX), row(EX), row(EX), ALU.mult))
                dve.wait_ge(act_params, 2 * l + 2)
                chain(tt(row(ABR), row(MAG), row(COS), ALU.mult))
                chain(tt(row(ABI), row(MAG), row(SIN), ALU.mult))
                chain(ts(row(NR), row(ABR), -1.0, None, ALU.add))
                chain(tt(row(T0), are, are, ALU.mult))
                chain(tt(row(T1), aim, aim, ALU.mult))
                chain(tt(row(DEN), row(T0), row(T1), ALU.add))
                chain(dve.reciprocal(row(DEN), row(DEN)))
                yield
                chain(tt(row(T0), row(NR), are, ALU.mult))
                chain(tt(row(T1), row(ABI), aim, ALU.mult))
                chain(tt(row(T0), row(T0), row(T1), ALU.add))
                chain(tt(row(GR), row(T0), row(DEN), ALU.mult))
                chain(tt(row(T0), row(ABI), are, ALU.mult))
                chain(tt(row(T1), row(NR), aim, ALU.mult))
                chain(tt(row(T0), row(T0), row(T1), ALU.subtract))
                chain(tt(row(GI), row(T0), row(DEN), ALU.mult))
                yield
                C, S = rot[:, 0, :, :], rot[:, 1, :, :]
                chain(dve.memset(rot[:, 0, :, 0:1], 1.0))
                chain(dve.memset(rot[:, 1, :, 0:1], 0.0))
                put(cp(row(PC), row(COS)))
                chain(cp(row(PS), row(SIN)))
                n = 1
                while n < SEQ:
                    pc = row(PC).unsqueeze(2).broadcast_to([128, 8, n])
                    ps = row(PS).unsqueeze(2).broadcast_to([128, 8, n])
                    tmp = rot_tmp[:, 0:8 * n].rearrange("p (a b) -> p a b", a=8)
                    put(tt(tmp, S[:, :, 0:n], ps, ALU.mult))
                    chain(tt(C[:, :, n:2 * n], C[:, :, 0:n], pc, ALU.mult))
                    put(tt(C[:, :, n:2 * n], C[:, :, n:2 * n], tmp, ALU.subtract))
                    chain(tt(S[:, :, n:2 * n], S[:, :, 0:n], pc, ALU.mult))
                    chain(tt(tmp, C[:, :, 0:n], ps, ALU.mult))
                    chain(tt(S[:, :, n:2 * n], S[:, :, n:2 * n], tmp, ALU.add))
                    n *= 2
                    if n < SEQ:
                        chain(tt(row(T0), row(PC), row(PC), ALU.mult))
                        chain(tt(row(T1), row(PS), row(PS), ALU.mult))
                        chain(tt(row(T2), row(PC), row(PS), ALU.mult))
                        chain(tt(row(PC), row(T0), row(T1), ALU.subtract))
                        chain(ts(row(PS), row(T2), 2.0, None, ALU.mult))
                    yield
                dve.wait_ge(mats_loaded, 16 * (l + 1))
                gr = row(GR).unsqueeze(2).broadcast_to([128, 8, 32])
                gi = row(GI).unsqueeze(2).broadcast_to([128, 8, 32])
                tmp = rot_tmp[:, 0:256].rearrange("p (a b) -> p a b", a=8)
                chain(tt(Cg[:, :, 0, :], C_s5[:, :, 0, :], gr, ALU.mult))
                chain(tt(tmp, C_s5[:, :, 1, :], gi, ALU.mult))
                chain(tt(Cg[:, :, 0, :], Cg[:, :, 0, :], tmp, ALU.subtract))
                chain(tt(Cg[:, :, 1, :], C_s5[:, :, 1, :], gr, ALU.mult))
                chain(tt(tmp, C_s5[:, :, 0, :], gi, ALU.mult))
                chain(stt(Cg[:, :, 1, :], Cg[:, :, 1, :], -1.0, tmp, ALU.mult, ALU.subtract))
                chain(ts(Cs[:, :, :], C_s5[:, :, 1, :], -1.0, None, ALU.mult), table_ready)

            def run(pieces):
                for _ in pieces:
                    pass

            def s5_tile(l, j):
                b, fu = got(l, ("s5_in", j))
                bb = b[:, :].rearrange("p (r t) -> p r t", r=2)
                c = rot[:, 0, j, :].unsqueeze(1).broadcast_to([128, 2, SEQ])
                s = rot[:, 1, j, :].unsqueeze(1).broadcast_to([128, 2, SEQ])
                p1, p2 = (p.rearrange("p (r t) -> p r t", r=2) for p in (P1, P2))
                put(tt(p1, bb, c, ALU.mult))
                chain(tt(p2, bb, s, ALU.mult))
                dve.sem_inc(fu, 1)
                put(tt(W5[:, 0:256], P1[:, 0:256], P2[:, 256:512], ALU.add))
                chain(tt(W5[:, 256:512], P1[:, 256:512], P2[:, 0:256], ALU.subtract))
                mag = row(MAG)[:, j:j + 1].broadcast_to([128, SEQ])
                for r in range(2):
                    put(dve.tensor_tensor_scan(Z5[:, 256 * r:256 * r + 256], mag, W5[:, 256 * r:256 * r + 256], 0.0, ALU.mult, ALU.add))
                settle()
                z = Z5.rearrange("p (r t) -> p r t", r=2)
                put(tt(p1, z, c, ALU.mult))
                chain(tt(p2, z, s, ALU.mult))
                if j >= 2:
                    dve.wait_ge(y5_done, 8 * l + j - 1)
                x = XS[j % 2]
                put(tt(x[:, 0:256], P1[:, 0:256], P2[:, 256:512], ALU.subtract))
                chain(tt(x[:, 256:512], P1[:, 256:512], P2[:, 0:256], ALU.add), xs_ready)
                put(cp(s5last[:, :, j], x.rearrange("p (r t) -> p r t", r=2)[:, :, 255]))

            def hgrn_gate(l, j):
                lb, one_lb = low[:, l, :], low[:, 6 + l, :]
                dve.wait_ge(sig_ready, 6 * l + 2 * j + 2)
                put(ts(Fg[:, j, :], sig_f[:, j, 0:256], one_lb[:, j:j + 1], lb[:, j:j + 1], ALU.mult, ALU.add))
                put(ts(Fs[:, j, :], sig_f[:, j, 256:T], one_lb[:, j:j + 1], lb[:, j:j + 1], ALU.mult, ALU.add))
                put(ts(Kg[:, j, :], sig_n[:, j, :], one_lb[:, j:j + 1], None, ALU.mult), None if j < 2 else k_ready)

            def hgrn_q(l, j):
                dve.wait_ge(qsig_ready, 3 * l + j + 1)
                p, fr = tile(l, HQ + j)
                put(tt(Qg[:, j, :], Qg[:, j, :], p, ALU.mult), None if j < 2 else q_ready)
                free(fr)

            def s5_states(l):
                settle()
                if l:
                    dve.wait_ge(outs["s5_p"], 16 * l)
                    dve.wait_ge(outs["s5_s"], 16 * l)
                put(tt(s5fin[:, 0, :], s5last[:, 0, :], row(GR), ALU.mult))
                chain(tt(row(T0), s5last[:, 1, :], row(GI), ALU.mult))
                put(tt(s5fin[:, 0, :], s5fin[:, 0, :], row(T0), ALU.subtract))
                put(tt(s5fin[:, 1, :], s5last[:, 0, :], row(GI), ALU.mult))
                chain(tt(row(T1), s5last[:, 1, :], row(GR), ALU.mult))
                put(tt(s5fin[:, 1, :], s5fin[:, 1, :], row(T1), ALU.add), s5fin_ready)
                b, fu = got(l, ("s5_in_sample",))
                bv = b[:, 0:128].rearrange("p (r j t) -> p r j t", r=2, j=8)

                def wide(i):
                    return row(i).unsqueeze(2).broadcast_to([128, 8, NSAMP])

                for cr, ci, src in ((ABR, ABI, s5x0[:, l, :, :, :]), (GR, GI, bv)):
                    for r, op in enumerate((ALU.subtract, ALU.add)):
                        put(tt(s5tmp[:, 0, :, :], src[:, r, :, :], wide(cr), ALU.mult))
                        chain(tt(s5tmp[:, 1, :, :], src[:, 1 - r, :, :], wide(ci), ALU.mult))
                        if cr == ABR:
                            chain(tt(s5xs[:, r, :, :], s5tmp[:, 0, :, :], s5tmp[:, 1, :, :], op))
                        else:
                            chain(tt(s5tmp[:, 0, :, :], s5tmp[:, 0, :, :], s5tmp[:, 1, :, :], op))
                            chain(tt(s5xs[:, r, :, :], s5xs[:, r, :, :], s5tmp[:, 0, :, :], ALU.add), s5fin_ready if r == 1 else None)
                dve.sem_inc(fu, 1)
                dve.sem_inc(xss_ready, 1)

            def s5_gelu_argument(l):
                dve.wait_ge(y5_done, 8 * l + 8)
                for m in range(2):
                    put(stt(Y[:, m, 0:256], U[:, m, 0:256], pv(l, "d")[:, m:m + 1], y5_bank[:, m, :], ALU.mult, ALU.add))
                free(y5_free)
                b, fu = got(l, ("s5_out_sample",))
                for m in range(2):
                    put(stt(Y[:, m, 256:T], U[:, m, 256:T], pv(l, "d")[:, m:m + 1], b[:, 8 * m:8 * m + 8], ALU.mult, ALU.add))
                free(fu)
                chain(tt(gel, Y, Y, ALU.mult))
                chain(ts(gel, gel, GELU_C1, GELU_C0, ALU.mult, ALU.add))
                put(tt(gel, gel, Y, ALU.mult), gelarg_ready)

            def halves(x, half):
                v = x.rearrange("p f (n c) -> p f n c", c=2 * half)
                return v[:, :, :, 0:half], v[:, :, :, half:2 * half]

            def level_decay(l, r):
                half = 1 << r
                k_l, k_r = halves(Kg[:, :, 0:256], half)
                q_l, q_r = halves(Qg[:, :, 0:256], half)
                F_l, F_r = halves(Fg[:, :, :], half)
                G_l, G_r = halves(Gg[:, :, :], half)
                if r >= 2:
                    dve.wait_ge(unit_done, unit_index(l, ("hg_level", r - 2, 2)) + 1)
                settle()
                if r == 0:
                    put(cp(halves(kdec[0], 1)[1], k_r))
                    put(tt(halves(kdec[0], 1)[0], k_l, F_r, ALU.mult), dec_ready)
                    put(dve.memset(G_r, 1.0))
                    put(cp(G_l, F_r))
                    chain(tt(F_r, F_r, F_l, ALU.mult))
                    return
                put(tt(halves(qdec[r % 2], half)[1], q_r, F_r, ALU.mult))
                put(tt(halves(kdec[r % 2], half)[0], k_l, G_l, ALU.mult), dec_ready)
                nb = 3 * SEQ // (2 * half)
                F2 = Fg[:, :, :].rearrange("p f (n c) -> p (f n) c", c=2 * half)
                G2 = Gg[:, :, :].rearrange("p f (n c) -> p (f n) c", c=2 * half)
                settle()
                chain(tt(G2[:, :, 0:half], G2[:, :, 0:half], F2[:, :, 2 * half - 1:2 * half].broadcast_to([128, nb, half]), ALU.mult))
                if r < 7:
                    put(tt(F2[:, :, half:2 * half], F2[:, :, half:2 * half], F2[:, :, half - 1:half].broadcast_to([128, nb, half]), ALU.mult))

            def near_level(l, r):
                for part in range(3):
                    b, fu = got(l, ("hg_level", r, part))
                    m = masks[:, r, :].unsqueeze(1).unsqueeze(1).broadcast_to([128, 2, 2, 128])
                    dst = near[:, part, 0:2, :, :] if part < 2 else near[:, :, 2, :, :]
                    put(dve.copy_predicated(dst, m, b[:, :].rearrange("p (a c t) -> p a c t", a=2, c=2)), fu)
                settle()
                dve.sem_inc(near_ready, 1)

            def rotary(l, X_):
                sw = swapped
                settle()
                chain(dve.stream_shuffle(sw, X_[:, :, :], [i ^ 16 for i in range(32)]))
                put(tt(X_[:, :, :], X_[:, :, :], cv("cos").unsqueeze(1).broadcast_to([128, 2, T]), ALU.mult))
                chain(tt(sw, sw, cv("sin").unsqueeze(1).broadcast_to([128, 2, T]), ALU.mult))
                put(tt(X_[:, :, :], X_[:, :, :], sw, ALU.add), ret_ready)

            def output_gate(l, i):
                dve.wait_ge(gsig_ready, 6 * l + i + 1)
                p, fr = tile(l, HGT + i)
                w = pv(l, "hg_norm")[:, 0:1] if i < 3 else pv(l, "ret_norm")[:, i - 3:i - 2]
                put(stt(gates[:, i, :], gates[:, i, :], w, p, ALU.mult, ALU.mult), fr)

            def hgrn_sample_decay(l):
                dve.wait_ge(states_loaded, 32 * (l + 1))
                S = S_hg[:, :, :, :].rearrange("p a b v -> p (a b) v")
                put(tt(S, S, Fs[:, :, :].rearrange("p a b -> p (a b)").unsqueeze(2).broadcast_to([128, 24, DV]), ALU.mult))

            def hgrn_sample_add(l, ft):
                b, fu = got(l, ("hg_kv", ft))
                S = S_hg[:, ft, :, :].rearrange("p b v -> p (b v)")
                settle()
                put(tt(S, S, b[:, :], ALU.add), shg_ready)
                free(fu)

            def hgrn_sample_q(l):
                settle()
                for ft in range(3):
                    put(tt(qs_hg[:, ft, :, :], S_hg[:, ft, :, :], Qg[:, ft, SEQ:T].unsqueeze(2).broadcast_to([128, NSAMP, DV]), ALU.mult),
                        qshg_ready if ft == 2 else None)

            def ret_sample_add(l, i):
                b, fu = got(l, ("ret_kv", i))
                n = 128 if i == 0 else 64
                S = S_rt[0:n, i, :, :].rearrange("p b v -> p (b v)")
                put(stt(S, S, cv("gamma")[0:n, i:i + 1], b[0:n, :], ALU.mult, ALU.add), srt_ready)
                free(fu)

            def ret_sample_q(l):
                settle()
                for i in range(2):
                    put(tt(qs_rt[:, i, :, :], S_rt[:, i, :, :], QR[:, i, SEQ:T].unsqueeze(2).broadcast_to([128, NSAMP, DV]), ALU.mult),
                        qsrt_ready if i == 1 else None)

            def ret_scores(l, h):
                b, fu = got(l, ("ret_score", h))
                if h == 0:
                    dve.wait_ge(unit_done, unit_index(l, ("hg_o_sample",)) + 1)
                put(tt(RS[:, h, 0:256], b[:, 0:256], decay[:, h, :], ALU.mult))
                put(tt(RS[:, h, 256:384], b[:, 256:384], decay[:, h, 0:128], ALU.mult), rs_ready)
                free(fu)

            def ret_k_decay(l, t):
                b, fu = got(l, ("tr_rk", t))
                put(tt(kt_rt[:, t, :], b[:, 0:256], k_decay[:, t, :], ALU.mult), ktr_ready)
                free(fu)

            def mixer_work(l, c):
                if 2 <= c < 2 + S5_TILES:
                    s5_tile(l, c - 2)
                if 5 <= c < 8:
                    hgrn_gate(l, c - 5)
                if 8 <= c < 11:
                    hgrn_q(l, c - 8)
                if c == 10:
                    s5_states(l)
                if c == 12:
                    s5_gelu_argument(l)
                if 13 <= c < 20:
                    near_level(l, c - 13)
                if 15 <= c < 18:
                    hgrn_sample_add(l, c - 15)
                if c == 10:
                    dve.wait_ge(cleared, 3 + l)
                if 10 <= c < 18:
                    level_decay(l, c - 10)
                if c == 12:
                    hgrn_sample_decay(l)
                if c == 14:
                    dve.wait_ge(gel_ready, 3 * l + 1)
                    put(tt(Y, Y, gel, ALU.mult), gelu_done)
                if c == 17:
                    hgrn_sample_q(l)
                    dve.wait_ge(rqk_ready, 4 * l + 4)
                    rotary(l, KR)
                if c == 18:
                    dve.wait_ge(unit_done, unit_index(l, ("hg_level", 6, 2)) + 1)
                    settle()
                    put(tt(kdec[0], Kg[:, :, 0:256], Gg, ALU.mult), dec_ready)
                    rotary(l, QR)
                    dve.wait_ge(gel_ready, 3 * l + 3)
                    put(tt(Y, Y, gel, ALU.mult), glu_done)
                if 19 <= c < 24:
                    output_gate(l, c - 19)
                if c == 21:
                    for t in range(2):
                        ret_k_decay(l, t)
                if c == 22:
                    for i in range(2):
                        ret_sample_add(l, i)
                    ret_sample_q(l)
                if c == 23:
                    for h in range(3):
                        ret_scores(l, h)

            def mixer_end(l):
                for h in range(3, HEADS):
                    ret_scores(l, h)
                output_gate(l, 5)
                for k in range(2):
                    split_a(l, 1, k, MIX, MIX_ORDER[k])
                for ft in range(3):
                    b, fu = got(l, ("ret_mu", ft))
                    put(tt(MIX[:, 3 + ft, :], MIX[:, 3 + ft, :], b[:, 0:T], ALU.subtract), orc_ready)
                    free(fu)
                for f0, sd, mixed in ((0, hsd_ready, hmix_ready), (3, rsd_ready, rmix_ready)):
                    dve.wait_ge(sd, 3 * l + 3)
                    chain(dve.reciprocal(head_sq[:, f0:f0 + 3, :], head_sq[:, f0:f0 + 3, :]))
                    chain(tt(MIX[:, f0:f0 + 3, :], MIX[:, f0:f0 + 3, :], head_sq[:, f0:f0 + 3, :], ALU.mult))
                    put(tt(MIX[:, f0:f0 + 3, :], MIX[:, f0:f0 + 3, :], gates[:, f0:f0 + 3, :], ALU.mult), mixed)
                for k in range(2, KT):
                    split_a(l, 1, k, MIX, MIX_ORDER[k])

            def residual(l, w, m):
                c = OUT0 + m if w == 0 else DOWN_B + 2 * m + 1
                p, fr = tile(l, c)
                if w == 0:
                    put(stt(X1[:, m, :], X[:, m, :], ALPHA, p, ALU.mult, ALU.add), res_ready)
                else:
                    put(tt(X[:, m, :], X[:, m, :], p, ALU.add), res_ready)
                free(fr)

            def half_down(l, m):
                p, fr = tile(l, DOWN_A + 2 * m + 1)
                put(stt(X[:, m, :], X1[:, m, :], ALPHA, p, ALU.mult, ALU.add), fr)

            def hidden(l, m):
                n = 32 * l + m
                dve.wait_ge(relu_ready, n + 1)
                put(tt(h_full[:, m % 2, :], relu[:, m % 2, :], relu[:, m % 2, :], ALU.mult), hfull_ready)

            def hidden_low(l, m):
                dve.wait_ge(hhigh_ready, 32 * l + m + 1)
                put(tt(h_low[:, m % FF_HALF, :], h_full[:, m % 2, :], h_high[:, m % FF_HALF, :].bitcast(F32), ALU.subtract), h_ready)

            def norm(l, w):
                x = X1 if w == 0 else X
                b, fu = got(l, (f"ln{w + 1}_mu",))
                for m in range(KT):
                    put(tt(x[:, m, :], x[:, m, :], b[:, 0:T], ALU.subtract), lnc_ready)
                free(fu)
                dve.wait_ge(lnsd_ready, 2 * l + w + 1)
                chain(dve.reciprocal(sq_r, sq[:, 0, :]))
                final = w and l == DEPTH - 1
                for m in range(KT):
                    s = sq[:, m, :] if m else sq0
                    put(tt(s, x[:, m, :], sq_r, ALU.mult), lns_ready)
                settle()
                for m in range(KT):
                    s = sq[:, m, :] if m else sq0
                    put(ts(x[:, m, :], s, pv(l, f"ln{w + 1}_w")[:, m:m + 1], pv(l, f"ln{w + 1}_b")[:, m:m + 1], ALU.mult, ALU.add), ln_ready)
                    if not final:
                        settle()
                        if w == 0:
                            split_a(l, 2, m, x, m)
                        else:
                            split_a(l + 1, 0, m, x, m)

            dve.wait_ge(const_loaded, 64)
            lg = [pv(l, "logits") for l in range(DEPTH)]
            chain(tt(low[:, 4, :], lg[0], lg[1], ALU.max))
            chain(tt(low[:, 2, :], lg[0], low[:, 4, :], ALU.subtract))
            chain(tt(low[:, 3, :], lg[1], low[:, 4, :], ALU.subtract))
            first_table = s5_tables(0)
            next(first_table)
            put(cp(masks[:, :, :], masks_f32))
            dve.wait_ge(x_loaded, 16)
            for m in range(KT):
                split_a(0, 0, m, X, m)
            for n in range(AHEAD):
                split_low(n)
            dve.wait_ge(softmax_exp, 1)
            chain(tt(low[:, 4, :], low[:, 0, :], low[:, 1, :], ALU.add))
            chain(dve.reciprocal(low[:, 4, :], low[:, 4, :]))
            chain(tt(low[:, 2, :], low[:, 0, :], low[:, 4, :], ALU.mult))
            chain(tt(low[:, 3, :], low[:, 1, :], low[:, 4, :], ALU.mult))
            chain(tt(low[:, 0, :], low[:, 2, :], low[:, 2, :], ALU.subtract))
            chain(tt(low[:, 3, :], low[:, 2, :], low[:, 3, :], ALU.add))
            chain(tt(low[:, 1, :], low[:, 3, :], low[:, 2, :], ALU.subtract))
            for l in range(DEPTH):
                chain(ts(low[:, 6 + l, :], low[:, l, :], -1.0, 1.0, ALU.mult, ALU.add))

            for l in range(DEPTH):
                if l == 0:
                    table = first_table
                for c in range(N_CHUNKS):
                    split_low(l * N_CHUNKS + c + AHEAD)
                    if c < N_IN:
                        if c == 1 and l == 0:
                            run(table)
                        mixer_work(l, c)
                        if c == N_IN - 1:
                            mixer_end(l)
                    elif c < UP_A:
                        if c > OUT0:
                            residual(l, 0, c - 1 - OUT0)
                        if c == UP_A - 1:
                            residual(l, 0, KT - 1)
                            norm(l, 0)
                            table = s5_tables(l + 1) if l + 1 < DEPTH else iter(())
                    elif UP_A < c <= DOWN_A:
                        hidden(l, c - 1 - UP_A)
                        hidden_low(l, c - 1 - UP_A)
                    elif DOWN_A < c < UP_B and (c - DOWN_A) % 2 == 0:
                        half_down(l, (c - DOWN_A) // 2 - 1)
                        next(table, None)
                    elif UP_B <= c <= DOWN_B:
                        if c == UP_B:
                            half_down(l, KT - 1)
                        else:
                            hidden(l, c - 1 - UP_B + FF_HALF)
                            hidden_low(l, c - 1 - UP_B + FF_HALF)
                    elif c > DOWN_B:
                        if (c - DOWN_B) % 2 == 0:
                            residual(l, 1, (c - DOWN_B) // 2 - 1)
                        elif c < N_CHUNKS - 1:
                            next(table, None)
                        if c == N_CHUNKS - 1:
                            run(table)
                            residual(l, 1, KT - 1)
                norm(l, 1)


def _pack_weights(w_in, w_out, w_up, w_down):
    a = 384
    seg = {"hq": 0, "hf": a, "hi": 2 * a, "hg": 3 * a, "rq": 4 * a, "rk": 4 * a + 192, "rv": 4 * a + 384, "rg": 5 * a + 384, "su": 6 * a + 384}
    pad = np.zeros((DEPTH, D_MODEL, 64), w_in.dtype)

    def cut(name, n):
        return w_in[:, :, seg[name]:seg[name] + n]

    cols = np.concatenate([cut("su", 256), cut("hf", a), cut("hq", a), cut("hi", a), cut("rq", 192), pad, cut("rk", 192), pad,
                           cut("rv", a), cut("hg", a), cut("rg", a)], axis=2)
    def by_tiles(w):
        m = w.shape[2] // 128
        return w.reshape(DEPTH, KT, 128, m, 128).transpose(0, 3, 2, 1, 4).reshape(DEPTH, m, 128, CHUNK)

    up = by_tiles(w_up)
    down = w_down.reshape(DEPTH, 2, 2, 8, 128, KT, 128).transpose(0, 1, 5, 2, 4, 3, 6).reshape(DEPTH, 2, 2 * KT, 128, CHUNK)
    out = (by_tiles(cols), by_tiles(w_out), up[:, :FF_HALF], down[:, 0], up[:, FF_HALF:], down[:, 1])
    return np.ascontiguousarray(np.concatenate(out, axis=1))


def _columns(x, tiles):
    return x.reshape(DEPTH, tiles, 128).transpose(2, 0, 1)


def _constants():
    c = np.zeros((128, N_CV), np.float32)

    def put(name, value):
        a, n = CV[name]
        c[:, a:a + n] = value

    put("ident", np.eye(128))
    put("head_mean", np.kron(np.eye(2), np.ones((64, 64))) / 64)
    put("model_mean", 1.0 / D_MODEL)
    half = RET_DK // 2
    inv = np.float32(ROPE_BASE) ** (-np.arange(half, dtype=np.float32) / np.float32(half))
    pos = np.concatenate([np.arange(SEQ), np.full(NSAMP, PAST_LEN)]).astype(np.float32)
    ang = (inv[:, None] * pos[None, :]).astype(np.float32).astype(np.float64)
    p = np.arange(128) % 32
    cos, sin = np.cos(ang)[p % half], np.sin(ang)[p % half] * np.where(p < half, -1.0, 1.0)[:, None]
    put("cos", cos), put("sin", sin)
    log_gamma = np.log1p(-np.exp2(-5.0 - np.arange(HEADS))).astype(np.float32).astype(np.float64)
    s, t = np.arange(128)[:, None], np.arange(256)[None, :]
    dec = np.where(t >= s, np.exp(log_gamma[:, None, None] * np.maximum(t - s, 0)), 0.0)
    put("decay", dec.transpose(1, 0, 2).reshape(128, -1))
    left = 255 - np.arange(256)
    kd = np.zeros((2, 128, 256))
    kd[:, :, :192] = np.exp(left[:, None] * np.repeat(log_gamma, RET_DK)[None, :]).reshape(2, 128, 192)
    put("k_decay", kd.transpose(1, 0, 2).reshape(128, 512))
    g = np.zeros((128, 2))
    g[:, 0] = np.repeat(np.exp(log_gamma[:4]), 32)
    g[:64, 1] = np.repeat(np.exp(log_gamma[4:]), 32)
    put("gamma", g)
    put("eps", EPS)
    put("pair_sum", np.kron(np.eye(2), np.ones((64, 1))))
    put("quad_sum", np.kron(np.eye(4), np.ones((32, 1))))
    masks = np.zeros((128, 7, 128), np.float32)
    s, t = np.arange(128)[:, None], np.arange(128)[None, :]
    masks[:, 0, :] = (s >> 1 == t >> 1) & (s <= t)
    for L in range(1, 7):
        masks[:, L, :] = (s >> (L + 1) == t >> (L + 1)) & ((s >> L) & 1 == 0) & ((t >> L) & 1 == 1)
    return c, masks


def kernel(**inputs):
    import concourse.bacc as bacc
    from concourse.bass_utils import run_bass_kernel_spmd

    a = {k: np.asarray(v) for k, v in inputs.items()}
    f = np.float32
    x = np.concatenate([a["x_prompt"].reshape(SEQ, D_MODEL), a["x_sample"].reshape(NSAMP, D_MODEL)])
    arrays = {}
    arrays["xT"] = np.ascontiguousarray(x.reshape(T, KT, 128).transpose(2, 1, 0))
    arrays["weights"] = _pack_weights(a["w_in"], a["w_out"], a["w_up"], a["w_down"])
    vec = np.zeros((128, DEPTH, N_PV), f)

    def put(name, value):
        at, n = PV[name]
        vec[:, :, at:at + n] = value

    put("log_dt", _columns(np.repeat(a["s5_log_dt"], 64, axis=1), 8))
    put("a_re", _columns(a["s5_a_re"], 8))
    put("a_im", _columns(a["s5_a_im"], 8))
    put("d", _columns(a["s5_d"], 2))
    put("glu_b", _columns(a["s5_glu_b"], 2))
    put("hg_norm", _columns(np.tile(a["hgrn_norm_w"], (1, 2)), 1))
    put("ret_norm", _columns(a["ret_norm_w"], 3))
    for n in ("ln1_w", "ln1_b", "ln2_w", "ln2_b"):
        put(n, _columns(a[n], KT))
    put("logits", _columns(a["hgrn_lb_logits"], 3))
    arrays["vectors"] = vec
    mats = np.zeros((DEPTH, 128, MATS), f)
    Bm = np.zeros((DEPTH, 128, 2, 2, 128), f)
    Cm = np.zeros((DEPTH, 128, 8, 2, 32), f)
    for g in range(16):
        s, j, o = g // 8, g // 2, g % 2
        for r, n in enumerate(("re", "im")):
            Bm[:, 16 * (g % 8):16 * (g % 8) + 16, s, r, 64 * o:64 * o + 64] = a[f"s5_b_{n}"][:, g].transpose(0, 2, 1)
            Cm[:, 64 * o:64 * o + 64, j, r, 16 * o:16 * o + 16] = a[f"s5_c_{n}"][:, g].transpose(0, 2, 1)
    mats[:, :, 0:512] = Bm.reshape(DEPTH, 128, 512)
    mats[:, :, 512:1024] = Cm.reshape(DEPTH, 128, 512)
    mats[:, :, 1024:1536] = a["s5_glu_w"].reshape(DEPTH, 2, 128, 256).transpose(0, 2, 1, 3).reshape(DEPTH, 128, 512)
    arrays["matrices"] = mats
    arrays["constants"], arrays["level_masks"] = _constants()
    arrays["state_hg"] = np.ascontiguousarray(a["state_hgrn"].reshape(DEPTH, NSAMP, 3, 128, DV).transpose(0, 3, 2, 1, 4))
    rt = np.zeros((DEPTH, NSAMP, 2 * 128, DV), f)
    rt[:, :, :192] = a["state_ret"].reshape(DEPTH, NSAMP, 192, DV)
    arrays["state_rt"] = np.ascontiguousarray(rt.reshape(DEPTH, NSAMP, 2, 128, DV).transpose(0, 3, 2, 1, 4))
    s5 = np.stack([a["state_s5_re"], a["state_s5_im"]])
    arrays["state_s5"] = np.ascontiguousarray(s5.reshape(2, DEPTH, NSAMP, 8, 128).transpose(4, 1, 0, 3, 2))

    nc = bacc.Bacc("TRN2", target_bir_lowering=False, num_devices=1)
    ins = [nc.dram_tensor("in_" + n, v.shape, mybir.dt.from_np(v.dtype), kind="ExternalInput").ap() for n, v in arrays.items()]
    out_shapes = {"y": (128, KT, T), "hg_p": (DEPTH, 128, 3, DV), "rt_p": (DEPTH, 128, 2, DV), "s5_p": (DEPTH, 128, 2, 8),
                  "hg_s": (DEPTH, 128, 3, NSAMP, DV), "rt_s": (DEPTH, 128, 2, NSAMP, DV), "s5_s": (DEPTH, 128, 2, 8, NSAMP)}
    out_aps = [nc.dram_tensor("out_" + n, s, F32, kind="ExternalOutput").ap() for n, s in out_shapes.items()]
    build(nc, *ins, *out_aps)
    r = run_bass_kernel_spmd(nc, [{"in_" + n: v for n, v in arrays.items()}], core_ids=[0]).results[0]
    o = {n: np.asarray(r["out_" + n]) for n in out_shapes}
    y = o["y"].transpose(2, 1, 0).reshape(T, D_MODEL)
    hg_p = o["hg_p"].transpose(0, 2, 1, 3).reshape(DEPTH, 1, HEADS, 64, DV)
    rt_p = o["rt_p"].transpose(0, 2, 1, 3).reshape(DEPTH, 256, DV)[:, :192].reshape(DEPTH, 1, HEADS, RET_DK, DV)
    s5_p = o["s5_p"].transpose(2, 0, 3, 1).reshape(2, DEPTH, 1, 16, 64)
    hg_s = o["hg_s"].transpose(0, 3, 2, 1, 4).reshape(DEPTH, NSAMP, HEADS, 64, DV)
    rt_s = o["rt_s"].transpose(0, 3, 2, 1, 4).reshape(DEPTH, NSAMP, 256, DV)[:, :, :192].reshape(DEPTH, NSAMP, HEADS, RET_DK, DV)
    s5_s = o["s5_s"].transpose(2, 0, 4, 3, 1).reshape(2, DEPTH, NSAMP, 16, 64)
    return tuple(np.ascontiguousarray(v) for v in (
        y[:SEQ].reshape(1, SEQ, D_MODEL), y[SEQ:].reshape(NSAMP, 1, D_MODEL),
        hg_p, rt_p, s5_p[0], s5_p[1], hg_s, rt_s, s5_s[0], s5_s[1]))
```

```python
from contextlib import ExitStack

import numpy as np

import concourse.bass as bass
from concourse import mybir

ALU = mybir.AluOpType
ACT = mybir.ActivationFunctionType
F32 = mybir.dt.float32
F32R = mybir.dt.float32r
U8 = mybir.dt.uint8

DEPTH = 2
D_MODEL = 1024
SEQ = 256
NSAMP = 8
PAST_LEN = 2048
T = SEQ + NSAMP
KT = D_MODEL // 128
HEADS = 6
DV = 64
HG_FT = HEADS * DV // 128
RET_DK = 32
S5_TILES = 8
FF_TILES = 32
EPS = 1e-5
ALPHA = (2.0 * DEPTH) ** 0.25
LEVELS = 8
ROPE_BASE = 10000.0
GELU_C0 = 2.0 * (2.0 / np.pi) ** 0.5
GELU_C1 = GELU_C0 * 0.044715

SU, HF, HQ, HI, RQ, RK, RV, HGT, RG = 0, 2, 5, 8, 11, 13, 15, 18, 21
N_IN = 24
OUT0 = N_IN
UP_A = OUT0 + KT
DOWN_A = UP_A + FF_TILES // 2
UP_B = DOWN_A + 2 * KT
DOWN_B = UP_B + FF_TILES // 2
N_CHUNKS = DOWN_B + 2 * KT
FF_HALF = FF_TILES // 2
CHUNK = 8 * 128
RAW_SLOTS = 3
SPLIT_SLOTS = 3
AHEAD = 2
STREAM_BANKS = 3


def tile_index(c):
    if c < DOWN_A:
        return c
    if c < UP_B:
        return DOWN_A + (c - DOWN_A) // 2
    if c < DOWN_B:
        return DOWN_A + KT + (c - UP_B)
    return DOWN_A + KT + FF_HALF + (c - DOWN_B) // 2


N_TILES = tile_index(N_CHUNKS - 1) + 1


PV = {}
_at = 0
for _name, _n in (("log_dt", 8), ("a_re", 8), ("a_im", 8), ("d", 2), ("glu_b", 2), ("hg_norm", 1), ("ret_norm", 3),
                  ("ln1_w", 8), ("ln1_b", 8), ("ln2_w", 8), ("ln2_b", 8), ("logits", 3)):
    PV[_name] = (_at, _n)
    _at += _n
N_PV = _at
CV = {}
_at = 0
for _name, _n in (("ident", 128), ("head_mean", 128), ("model_mean", 128), ("cos", T), ("sin", T),
                  ("decay", HEADS * 256), ("k_decay", 512), ("gamma", 2), ("eps", 1), ("pair_sum", 2), ("quad_sum", 4)):
    CV[_name] = (_at, _n)
    _at += _n
N_CV = _at
MATS = 512 + 512 + 512

PLAN = {c: [] for c in range(N_CHUNKS)}


def _plan(step, *names):
    PLAN[step] += names


for _j in range(S5_TILES):
    _plan(_j + 2, ("s5_in", _j))
_plan(10, ("s5_in_sample",))
for _r in range(7):
    _plan(8 + _r, *[("hg_level", _r, part) for part in range(3)])
for _j in range(S5_TILES):
    _plan(_j + 4, ("s5_out", _j))
_plan(11, ("tr_hi", 0), ("tr_hi", 1), ("tr_hi_sample",), ("tr_hk_sample",))
_plan(12, ("s5_out_sample",))
for _f in range(3):
    _plan(13 + _f, ("hg_kv", _f))
_plan(15, ("glu", 0), ("glu", 1), ("hg_far", 0), ("hg_far", 1))
_plan(16, ("tr_hkd", 0), ("tr_hkd", 1), ("tr_rk", 0), ("tr_rk", 1), ("ret_score", 0), ("ret_score", 1))
_plan(17, ("hg_o_sample",), ("hg_o", 0), ("hg_o", 1), ("hg_o", 2), ("hg_state",), ("ret_score", 2), ("ret_score", 3))
_plan(18, ("tr_rv_sample",), ("tr_rk_sample",), ("tr_rv", 0), ("tr_rv", 1), ("ret_score", 4), ("ret_score", 5))
_plan(19, ("hg_ms", 0), ("hg_ms", 1), ("hg_ms", 2))
_plan(20, ("ret_kv", 0), ("ret_kv", 1), ("ret_o", 0), ("ret_o", 1), ("ret_o", 2), ("ret_state",))
_plan(21, ("ret_o_sample",))
_plan(22, ("ret_mu", 0), ("ret_mu", 1), ("ret_mu", 2))
_plan(23, ("ret_var", 0), ("ret_var", 1), ("ret_var", 2))
for _k in range(KT - 2):
    _plan(OUT0 + _k + 2, ("ln_mu_part", 0, _k))
    _plan(DOWN_B + 2 * _k + 3, ("ln_mu_part", 1, _k))
_plan(UP_A - 1, ("ln1_mu",), ("ln1_var",))
_plan(N_CHUNKS - 1, ("ln2_mu",), ("ln2_var",))
UNIT_ORDER = [u for c in range(N_CHUNKS) for u in PLAN[c] if u[0] not in ("s5_out", "ln_mu_part")]
UNIT_AT = {u: n for n, u in enumerate(UNIT_ORDER)}
N_UNITS = len(UNIT_ORDER)
MIX_BANKS = 4
NEAR_PARTS = [[(0, f, t) for f in (0, 1) for t in (0, 1)], [(1, f, t) for f in (0, 1) for t in (0, 1)],
              [(h, 2, t) for h in (0, 1) for t in (0, 1)]]


def build(nc, xT, weights, vectors, matrices, constants, level_masks, state_hg, state_rt, state_s5,
          y_out, hg_p_out, rt_p_out, s5_p_out, hg_s_out, rt_s_out, s5_s_out):
    with ExitStack() as ctx:
        def sb(name, shape, dt=F32):
            return ctx.enter_context(nc.sbuf_tensor(name, shape, dt))

        def sem(name):
            return ctx.enter_context(nc.semaphore(name))

        w_raw = sb("w_raw", [128, RAW_SLOTS, CHUNK])
        w_high = sb("w_high", [128, SPLIT_SLOTS, CHUNK], F32R)
        w_low = sb("w_low", [128, SPLIT_SLOTS, CHUNK], F32R)
        a_high = sb("a_high", [128, KT, T], F32R)
        a_low = sb("a_low", [128, KT, T], F32R)
        X = sb("X", [128, KT, T])
        X1 = sb("X1", [128, KT, T])
        MIX = sb("MIX", [128, KT, T])
        rot = sb("rot", [128, 2, S5_TILES, SEQ])
        consts = sb("consts", [128, N_CV])
        masks = sb("masks", [128, 7, 128], U8)
        vecs = sb("vecs", [128, DEPTH, N_PV])
        mats = sb("mats", [128, MATS])
        s5x0 = sb("s5x0", [128, DEPTH, 2, S5_TILES, NSAMP])
        Cg = sb("Cg", [128, S5_TILES, 3, 32])
        Cs = sb("Cs", [128, S5_TILES, 32])
        s5xs = sb("s5xs", [128, 2, S5_TILES, NSAMP])
        s5fin = sb("s5fin", [128, 2, S5_TILES])
        par = sb("par", [128, 20, S5_TILES])
        low = sb("low", [128, 8, HG_FT])
        st_p = sb("st_p", [128, 5, DV])
        S_hg = sb("S_hg", [128, HG_FT, NSAMP, DV])
        S_rt = sb("S_rt", [128, 2, NSAMP, DV])
        near = sb("near", [128, 2, HG_FT, 2, 128])
        V_tok = sb("V_tok", [128, 2, 2, 384])

        with ExitStack() as mixers:
            def msb(name, shape, dt=F32):
                return mixers.enter_context(nc.sbuf_tensor(name, shape, dt))

            scratch = msb("scratch", [128, 8448])
            Kg = msb("Kg", [128, HG_FT, T])
            Qg = msb("Qg", [128, HG_FT, T])
            Fg = msb("Fg", [128, HG_FT, SEQ])
            Fs = msb("Fs", [128, HG_FT, NSAMP])
            U = msb("U", [128, 2, T])
            gates = msb("gates", [128, 6, T])
            QR = msb("QR", [128, 2, T])
            KR = msb("KR", [128, 2, T])
            v_own = msb("v_own", [NSAMP, NSAMP, 128])
            vs_tok = msb("vs_tok", [NSAMP, 2, 384])
            ks_tok = msb("ks_tok", [NSAMP, 640])
            s5tmp = msb("s5tmp", [128, 2, S5_TILES, NSAMP])
            s5last = msb("s5last", [128, 2, S5_TILES])
        with ExitStack() as mlp:
            def fsb(name, shape, dt=F32):
                return mlp.enter_context(nc.sbuf_tensor(name, shape, dt))

            h_high = fsb("h_high", [128, FF_HALF, T], F32R)
            h_low = fsb("h_low", [128, FF_HALF, T], F32R)
            relu = fsb("relu", [128, 2, T])
            h_full = fsb("h_full", [128, 2, T])

        def flat(a, b):
            return scratch[:, a:b]

        P1, P2 = flat(0, 512), flat(512, 1024)
        W5, Z5 = P1, P2
        XS = [flat(1024 + 1024 * i, 2048 + 1024 * i) for i in range(2)]
        kt_hg = flat(0, 768).rearrange("p (a b) -> p a b", a=2)
        far = flat(768, 1536).rearrange("p (a b c) -> p a b c", a=2, b=3)
        kt_rt = flat(3072, 3584).rearrange("p (a b) -> p a b", a=2)
        qs_rt = flat(2048, 3072).rearrange("p (a b v) -> p a b v", a=2, b=NSAMP)
        qdec = [flat(3072 + 1536 * i, 3840 + 1536 * i).rearrange("p (a b) -> p a b", a=3) for i in range(2)]
        kdec = [flat(3840 + 1536 * i, 4608 + 1536 * i).rearrange("p (a b) -> p a b", a=3) for i in range(2)]
        level_space = flat(3072, 6144)
        qs_hg = flat(1536, 3072).rearrange("p (a b v) -> p a b v", a=3, b=NSAMP)
        RS = flat(6144, 8448).rearrange("p (a b) -> p a b", a=HEADS)
        masks_f32 = flat(6144, 7040).rearrange("p (a b) -> p a b", a=7)
        head_sq = flat(4608, 4608 + 6 * T).rearrange("p (a b) -> p a b", a=6)
        swapped = X1[:, 0:2, :]
        sig_f, sig_n, gel = X1[:, 0:3, :], X1[:, 3:6, :], X1[:, 6:8, :]
        Gg = X1[:, 3:6, :].rearrange("p a b -> p (a b)")[:, 0:3 * SEQ].rearrange("p (a b) -> p a b", a=3)
        Vf, Y = MIX[:, 0:6, :], MIX[:, 6:8, :]
        sq0 = flat(KT * T, KT * T + T)
        sq_r = flat(KT * T + T, KT * T + 2 * T)
        sq = flat(0, KT * T).rearrange("p (a b) -> p a b", a=KT)

        def cv(name):
            a, n = CV[name]
            return consts[:, a:a + n]

        def pv(l, name):
            a, n = PV[name]
            return vecs[:, l, a:a + n]

        ident = cv("ident")
        decay = cv("decay").rearrange("p (h t) -> p h t", h=HEADS)
        k_decay = cv("k_decay").rearrange("p (a b) -> p a b", a=2)
        B_s5 = mats[:, 0:512].rearrange("p (s r n) -> p s r n", s=2, r=2)
        C_s5 = mats[:, 512:1024].rearrange("p (j r c) -> p j r c", j=8, r=2)
        glu_w = mats[:, 1024:1536].rearrange("p (k m) -> p k m", k=2)

        stream_bank = [ctx.enter_context(nc.psum_tensor(f"stream{i}", [128, 512], F32)) for i in range(STREAM_BANKS)]
        mix_bank = [ctx.enter_context(nc.psum_tensor(f"mix{i}", [128, 512], F32)) for i in range(MIX_BANKS)]
        y5_bank = ctx.enter_context(nc.psum_tensor("y5_bank", [128, 2, 256], F32))

        raw_loaded = [sem(f"raw_loaded{i}") for i in range(RAW_SLOTS)]
        vecs_loaded = sem("vecs_loaded")
        x_loaded, const_loaded, mats_loaded, states_loaded = sem("x_loaded"), sem("const_loaded"), sem("mats_loaded"), sem("states_loaded")
        high_ready = sem("high_ready")
        low_ready = sem("low_ready")
        in_low_ready = sem("in_low_ready")
        bounds_ready = sem("bounds_ready")
        gate_ready = sem("gate_ready")
        chunk_done = sem("chunk_done")
        tile_free = [sem(f"tile_free{i}") for i in range(STREAM_BANKS)]
        unit_done = sem("unit_done")
        unit_free = [sem(f"unit_free{i}") for i in range(MIX_BANKS)]
        row_tile_done = sem("row_tile_done")
        y5_done, y5_free = sem("y5_done"), sem("y5_free")
        u_ready = sem("u_ready")
        sig_ready = sem("sig_ready")
        qsig_ready = sem("qsig_ready")
        gsig_ready = sem("gsig_ready")
        v_ready = sem("v_ready")
        rqk_ready = sem("rqk_ready")
        vtok_ready = sem("vtok_ready")
        vs_ready = sem("vs_ready")
        ks_ready = sem("ks_ready")
        vown_ready = sem("vown_ready")
        kt_ready = sem("kt_ready")
        ktr_ready = sem("ktr_ready")
        far_ready = sem("far_ready")
        ohg_copied = sem("ohg_copied")
        ort_copied = sem("ort_copied")
        hsq_ready = sem("hsq_ready")
        rsq_ready = sem("rsq_ready")
        hsd_ready = sem("hsd_ready")
        rsd_ready = sem("rsd_ready")
        gel_ready = sem("gel_ready")
        act_params = sem("act_params")
        softmax_exp = sem("softmax_exp")
        lnsq_ready = sem("lnsq_ready")
        lnsd_ready = sem("lnsd_ready")
        relu_ready = sem("relu_ready")
        hhigh_ready = sem("hhigh_ready")
        ahigh_ready = sem("ahigh_ready")
        stp_ready = sem("stp_ready")

        dve_step = sem("dve_step")
        par_ready = sem("par_ready")
        table_ready = sem("table_ready")
        xs_ready = sem("xs_ready")
        xss_ready = sem("xss_ready")
        q_ready = sem("q_ready")
        dec_ready = sem("dec_ready")
        near_ready = sem("near_ready")
        ret_ready = sem("ret_ready")
        rs_ready = sem("rs_ready")
        shg_ready = sem("shg_ready")
        srt_ready = sem("srt_ready")
        qshg_ready = sem("qshg_ready")
        qsrt_ready = sem("qsrt_ready")
        gelarg_ready = sem("gelarg_ready")
        gelu_done = sem("gelu_done")
        glu_done = sem("glu_done")
        orc_ready = sem("orc_ready")
        hmix_ready = sem("hmix_ready")
        rmix_ready = sem("rmix_ready")
        res_ready = sem("res_ready")
        lnc_ready = sem("lnc_ready")
        lns_ready = sem("lns_ready")
        ln_ready = sem("ln_ready")
        hfull_ready = sem("hfull_ready")
        h_ready = sem("h_ready")
        a_ready = sem("a_ready")
        s5fin_ready = sem("s5fin_ready")
        cleared = sem("cleared")
        vown_read = sem("vown_read")
        outs = {n: sem("stored_" + n) for n in ("y", "hg_p", "rt_p", "s5_p", "hg_s", "rt_s", "s5_s")}

        MIX_ORDER = (0, 1, 2, 6, 7, 3, 4, 5)

        def unit_index(l, name):
            return l * N_UNITS + UNIT_AT[name]

        def bank(l, name):
            return mix_bank[unit_index(l, name) % MIX_BANKS]

        def unit_freed(l, name):
            return unit_free[unit_index(l, name) % MIX_BANKS]

        def need(eng, s, n):
            if n > 0:
                eng.wait_ge(s, n)

        def wait_low(eng, n):
            l, c = divmod(n, N_CHUNKS)
            if c < N_IN:
                eng.wait_ge(in_low_ready, l * N_IN + c + 1)
            else:
                eng.wait_ge(low_ready, l * (N_CHUNKS - N_IN) + c - N_IN + 1)

        def dense_tile(eng, l, c):
            eng.wait_ge(chunk_done, l * N_CHUNKS + c + 1)
            g = l * N_TILES + tile_index(c)
            return stream_bank[g % STREAM_BANKS][:, 0:T], tile_free[g % STREAM_BANKS]

        block = ctx.enter_context(nc.Block())

        @block.sync
        def _(sp):
            for n in range(DEPTH * N_CHUNKS):
                if n >= RAW_SLOTS:
                    wait_low(sp, n - RAW_SLOTS)
                sp.dma_start(w_raw[:, n % RAW_SLOTS, :], weights[n // N_CHUNKS, n % N_CHUNKS]).then_inc(raw_loaded[n % RAW_SLOTS], 16)
            sp.wait_ge(ln_ready, 16 * DEPTH)
            sp.dma_start(y_out, X[:, :, :]).then_inc(outs["y"], 16)
            sp.wait_ge(outs["y"], 16)

        @block.gpsimd
        def _(pool):
            def split_low(n):
                pool.wait_ge(high_ready, n + 1)
                pool.tensor_tensor(w_low[:, n % SPLIT_SLOTS, :], w_raw[:, n % RAW_SLOTS, :], w_high[:, n % SPLIT_SLOTS, :].bitcast(F32), ALU.subtract).then_inc(in_low_ready, 1)

            def load_states(l):
                pool.dma_start(S_hg[:, :, :, :], state_hg[l]).then_inc(states_loaded, 16)
                pool.dma_start(S_rt[:, :, :, :], state_rt[l]).then_inc(states_loaded, 16)

            def own_block(l, i):
                pool.wait_ge(vs_ready, 2 * l + i // 3 + 1)
                if 1 <= i <= 3:
                    pool.wait_ge(unit_done, unit_index(l, ("hg_kv", i - 1)) + 1)
                elif i >= 4:
                    pool.wait_ge(vown_read, 2 * l + i - 3)
                elif l:
                    pool.wait_ge(unit_done, unit_index(l - 1, ("ret_kv", 1)) + 1)
                src = vs_tok[:, i // 3, 128 * (i % 3):128 * (i % 3) + 128]
                pool.affine_select(out=v_own[:, :, :], in_=src.unsqueeze(1).broadcast_to([NSAMP, NSAMP, 128]),
                                   compare_op=ALU.is_equal, fill=0.0, base=0, pattern=[[-1, NSAMP], [0, 128]],
                                   channel_multiplier=1).then_inc(vown_ready, 1)

            pool.dma_start(vecs[:, :, :], vectors).then_inc(vecs_loaded, 16)
            pool.dma_start(mats[:, :], matrices[0]).then_inc(mats_loaded, 16)
            pool.dma_start(consts[:, :], constants).then_inc(const_loaded, 16)
            pool.dma_start(masks_f32, level_masks).then_inc(const_loaded, 16)
            pool.dma_start(s5x0[:, :, :, :, :], state_s5).then_inc(const_loaded, 16)
            for l in range(DEPTH):
                for k in range(N_IN):
                    split_low(l * N_CHUNKS + k)
                    if k == 2:
                        if l == 0:
                            pool.memset(near[:, :, :, :, :], 0.0).then_inc(cleared, 1)
                            pool.memset(st_p[:, :, :], 0.0).then_inc(cleared, 1)
                            load_states(0)
                        else:
                            pool.wait_ge(chunk_done, l * N_CHUNKS)
                        pool.memset(level_space, 0.0).then_inc(cleared, 1)
                    if 14 <= k <= 16:
                        own_block(l, k - 14)
                    if k == 18:
                        pool.wait_ge(shg_ready, 3 * l + 3)
                        pool.dma_start(hg_s_out[l], S_hg[:, :, :, :]).then_inc(outs["hg_s"], 16)
                        pool.wait_ge(s5fin_ready, 2 * l + 2)
                        pool.dma_start(s5_p_out[l], s5fin[:, :, :]).then_inc(outs["s5_p"], 16)
                        pool.dma_start(s5_s_out[l], s5xs[:, :, :, :]).then_inc(outs["s5_s"], 16)
                    if k == 21:
                        own_block(l, 3)
                    if k == 22:
                        own_block(l, 4)
                        own_block(l, 5)
                pool.wait_ge(srt_ready, 2 * l + 2)
                pool.dma_start(rt_s_out[l], S_rt[:, :, :, :]).then_inc(outs["rt_s"], 16)
                pool.wait_ge(stp_ready, 3 * l + 3)
                pool.dma_start(hg_p_out[l], st_p[:, 0:3, :]).then_inc(outs["hg_p"], 16)
                pool.dma_start(rt_p_out[l], st_p[:, 3:5, :]).then_inc(outs["rt_p"], 16)
                if l + 1 < DEPTH:
                    pool.wait_ge(unit_done, unit_index(l, ("glu", 1)) + 1)
                    pool.wait_ge(table_ready, l + 1)
                    pool.dma_start(mats[:, :], matrices[l + 1]).then_inc(mats_loaded, 16)
                    pool.wait_ge(outs["hg_s"], 16 * (l + 1))
                    pool.wait_ge(outs["rt_s"], 16 * (l + 1))
                    pool.wait_ge(qshg_ready, l + 1)
                    pool.wait_ge(qsrt_ready, l + 1)
                    load_states(l + 1)
            for n in ("hg_p", "rt_p", "s5_p", "hg_s", "rt_s", "s5_s"):
                pool.wait_ge(outs[n], 16 * DEPTH)

        @block.tensor
        def _(pe):
            def unit(l, name):
                g = unit_index(l, name)
                need(pe, unit_free[g % MIX_BANKS], g // MIX_BANKS)
                return mix_bank[g % MIX_BANKS]

            fences = [0]

            def row_tile_fence(mm):
                fences[0] += 1
                mm.then_inc(row_tile_done, 1)
                pe.wait_ge(row_tile_done, fences[0])

            def s5_in(l, u):
                j = u[1]
                if j == 0:
                    pe.wait_ge(u_ready, 2 * l + 2)
                    pe.wait_ge(mats_loaded, 16 * (l + 1))
                b = unit(l, u)
                q = 32 * (j % 4)
                for r in range(2):
                    mm = pe.matmul(b[:, 256 * r:256 * r + 256], B_s5[q:q + 32, j // 4, r, :], U[q:q + 32, j // 4, 0:256], start=True, stop=True, tile_position=(q, 0))
                mm.then_inc(unit_done, 1)

            def s5_in_sample(l, u):
                b = unit(l, u)
                bv = b[:, 0:128].rearrange("p (r j t) -> p r j t", r=2, j=8)
                for q in range(0, 128, 32):
                    for s in range(2):
                        for r in range(2):
                            mm = pe.matmul(bv[:, r, 4 * s + q // 32, :], B_s5[q:q + 32, s, r, :], U[q:q + 32, s, 256:T], start=True, stop=True, tile_position=(q, 0))
                    if q < 96:
                        row_tile_fence(mm)
                mm.then_inc(unit_done, 1)

            def s5_out(l, u):
                j = u[1]
                if j == 0:
                    need(pe, y5_free, l)
                    pe.wait_ge(table_ready, l + 1)
                pe.wait_ge(xs_ready, 8 * l + j + 1)
                q = 32 * (j % 4)
                o = y5_bank[q:q + 32, j // 4, :]
                for i, (coefficient, part) in enumerate(((0, 0), (1, 1), (1, 2), (2, 3))):
                    mm = pe.matmul(o, Cg[:, j, coefficient, :], XS[j % 2][:, 256 * part:256 * part + 256], start=(i == 0), stop=(i == 3), tile_position=(0, q))
                mm.then_inc(y5_done, 1)

            def s5_out_sample(l, u):
                pe.wait_ge(xss_ready, l + 1)
                b = unit(l, u)
                for j in range(8):
                    q = 32 * (j % 4)
                    o = b[q:q + 32, 8 * (j // 4):8 * (j // 4) + 8]
                    pe.matmul(o, C_s5[:, j, 0, :], s5xs[:, 0, j, :], start=True, stop=False, tile_position=(0, q))
                    mm = pe.matmul(o, Cs[:, j, :], s5xs[:, 1, j, :], start=False, stop=True, tile_position=(0, q))
                mm.then_inc(unit_done, 1)

            def transposes(l, u, src, rows, cols):
                b = unit(l, u)
                for i in range(src.shape[1]):
                    mm = pe.transpose(b[0:rows, 128 * i:128 * i + 128], src[:, i, cols], ident)
                mm.then_inc(unit_done, 1)

            def token_tile(t):
                return slice(128 * t, 128 * t + 128)

            sample = slice(SEQ, T)

            def tr_hi(l, u):
                pe.wait_ge(v_ready, 6 * l + 3)
                transposes(l, u, Vf[:, 0:3, :], 128, token_tile(u[1]))

            def tr_hi_sample(l, u):
                transposes(l, u, Vf[:, 0:3, :], NSAMP, sample)

            def tr_rv(l, u):
                transposes(l, u, Vf[:, 3:6, :], 128, token_tile(u[1]))

            def tr_rv_sample(l, u):
                pe.wait_ge(v_ready, 6 * l + 6)
                transposes(l, u, Vf[:, 3:6, :], NSAMP, sample)

            def tr_hk_sample(l, u):
                pe.wait_ge(gate_ready, 9 * l + 9)
                transposes(l, u, Kg, NSAMP, sample)

            def tr_rk_sample(l, u):
                transposes(l, u, KR, NSAMP, sample)

            def tr_rk(l, u):
                transposes(l, u, KR, 128, token_tile(u[1]))

            def tr_hkd(l, u):
                pe.wait_ge(dec_ready, 9 * l + 9)
                transposes(l, u, kdec[0], 128, token_tile(u[1]))

            def hg_level(l, u):
                r, part = u[1:]
                if r == 0:
                    pe.wait_ge(q_ready, l + 1)
                pe.wait_ge(dec_ready, 9 * l + r + 1)
                b = unit(l, u)
                for c, (h, f, t) in enumerate(NEAR_PARTS[part]):
                    if c == 2 and part == 2:
                        row_tile_fence(mm)
                    rows = slice(64 * h, 64 * h + 64)
                    pos = (64 * h, 0)
                    o = b[:, 128 * c:128 * c + 128]
                    if r == 0:
                        ov = o.rearrange("p (n c) -> p n c", c=2)
                        qv = Qg[rows, f, token_tile(t)].rearrange("p (n c) -> p n c", c=2)
                        pe.matmul(ov[:, :, 0], Kg[rows, f, token_tile(t)], qv[:, :, 0], start=True, stop=True, tile_position=pos)
                        mm = pe.matmul(ov[:, :, 1], kdec[0][rows, f, token_tile(t)], qv[:, :, 1], start=True, stop=True, tile_position=pos)
                    else:
                        mm = pe.matmul(o, kdec[r % 2][rows, f, token_tile(t)], qdec[r % 2][rows, f, token_tile(t)], start=True, stop=True, tile_position=pos)
                mm.then_inc(unit_done, 1)

            def hg_far(l, u):
                pe.wait_ge(dec_ready, 9 * l + 8)
                b = unit(l, u)
                h = u[1]
                for f in range(3):
                    mm = pe.matmul(b[:, 128 * f:128 * f + 128], kdec[1][64 * h:64 * h + 64, f, 0:128],
                                   qdec[1][64 * h:64 * h + 64, f, 128:256], start=True, stop=True, tile_position=(64 * h, 0))
                mm.then_inc(unit_done, 1)

            def hg_state(l, u):
                pe.wait_ge(kt_ready, 2 * l + 2)
                b = unit(l, u)
                for h in range(HEADS):
                    o = b[64 * (h % 2):64 * (h % 2) + 64, 64 * (h // 2):64 * (h // 2) + 64]
                    for t in range(2):
                        mm = pe.matmul(o, kt_hg[:, t, 64 * h:64 * h + 64], V_tok[:, t, 0, 64 * h:64 * h + 64], start=(t == 0), stop=(t == 1),
                                       tile_position=(0, 64 * (h % 2)))
                mm.then_inc(unit_done, 1)

            def hg_kv(l, u):
                ft = u[1]
                pe.wait_ge(ks_ready, 2 * l + 1)
                pe.wait_ge(vown_ready, 6 * l + ft + 1)
                b = unit(l, u)
                for h in range(2):
                    mm = pe.matmul(b[64 * h:64 * h + 64, :].rearrange("p (b v) -> p b v", b=8), ks_tok[:, 128 * ft + 64 * h:128 * ft + 64 * h + 64],
                                   v_own[:, :, 64 * h:64 * h + 64], start=True, stop=True, tile_position=(0, 64 * h))
                mm.then_inc(unit_done, 1)

            def ret_kv(l, u):
                i = u[1]
                pe.wait_ge(ks_ready, 2 * l + 2)
                b = unit(l, u)
                for h in range(4 * i, min(4 * i + 4, HEADS)):
                    pe.wait_ge(vown_ready, 6 * l + 3 + h // 2 + 1)
                    o = b[32 * (h % 4):32 * (h % 4) + 32, :].rearrange("p (b v) -> p b v", b=8)
                    mm = pe.matmul(o, ks_tok[:, 384 + 32 * h:384 + 32 * h + 32], v_own[:, :, 64 * (h % 2):64 * (h % 2) + 64],
                                   start=True, stop=True, tile_position=(0, 32 * (h % 4)))
                    if h == 1:
                        mm.then_inc(vown_read, 1)
                    if h == 3:
                        mm.then_inc(vown_read, 1)
                        pe.wait_ge(vown_read, 2 * l + 2)
                        pe.sem_inc(unit_done, 1)
                    if h == 5:
                        mm.then_inc(unit_done, 1)

            def hg_o(l, u):
                ft = u[1]
                if ft == 0:
                    pe.wait_ge(near_ready, 7 * l + 7)
                    pe.wait_ge(far_ready, 2 * l + 2)
                    pe.wait_ge(vtok_ready, 4 * l + 2)
                b = unit(l, u)
                for h in range(2):
                    o = b[64 * h:64 * h + 64, :]
                    hc = slice(128 * ft + 64 * h, 128 * ft + 64 * h + 64)
                    pos = (0, 64 * h)
                    pe.matmul(o[:, 0:128], V_tok[:, 0, 0, hc], near[:, h, ft, 0, :], start=True, stop=True, tile_position=pos)
                    pe.matmul(o[:, 128:256], V_tok[:, 0, 0, hc], far[:, h, ft, :], start=True, stop=False, tile_position=pos)
                    mm = pe.matmul(o[:, 128:256], V_tok[:, 1, 0, hc], near[:, h, ft, 1, :], start=False, stop=True, tile_position=pos)
                mm.then_inc(unit_done, 1)

            def hg_o_sample(l, u):
                pe.wait_ge(qshg_ready, l + 1)
                b = unit(l, u)
                for ft in range(3):
                    for bp in range(NSAMP // 2):
                        at = 2 * (4 * ft + bp)
                        mm = pe.matmul(b[:, at:at + 2], qs_hg[:, ft, 2 * bp:2 * bp + 2, :].rearrange("p b v -> p (b v)"), cv("pair_sum"), start=True, stop=True)
                mm.then_inc(unit_done, 1)

            def ret_o_sample(l, u):
                pe.wait_ge(qsrt_ready, l + 1)
                b = unit(l, u)
                for bp in range(NSAMP // 2):
                    pe.matmul(b[:, 4 * bp:4 * bp + 4], qs_rt[:, 0, 2 * bp:2 * bp + 2, :].rearrange("p b v -> p (b v)"), cv("quad_sum"), start=True, stop=True)
                for bp in range(NSAMP // 2):
                    mm = pe.matmul(b[:, 16 + 4 * bp:20 + 4 * bp], qs_rt[:, 1, 2 * bp:2 * bp + 2, :].rearrange("p b v -> p (b v)"), cv("quad_sum"), start=True, stop=True)
                mm.then_inc(unit_done, 1)

            def ret_score(l, u):
                h = u[1]
                pe.wait_ge(ret_ready, 2 * l + 2)
                b = unit(l, u)
                q, i = 32 * (h % 4), h // 4
                pe.matmul(b[:, 0:256], KR[q:q + 32, i, 0:128], QR[q:q + 32, i, 0:256], start=True, stop=True, tile_position=(q, 0))
                pe.matmul(b[:, 256:384], KR[q:q + 32, i, 128:256], QR[q:q + 32, i, 128:256], start=True, stop=True, tile_position=(q, 0)).then_inc(unit_done, 1)

            def ret_state(l, u):
                pe.wait_ge(ktr_ready, 2 * l + 2)
                pe.wait_ge(vtok_ready, 4 * l + 4)
                b = unit(l, u)
                for h in range(HEADS):
                    q, i = 32 * (h % 4), h // 4
                    for t in range(2):
                        mm = pe.matmul(b[q:q + 32, 64 * i:64 * i + 64], kt_rt[:, t, 32 * h:32 * h + 32], V_tok[:, t, 1, 64 * h:64 * h + 64],
                                       start=(t == 0), stop=(t == 1), tile_position=(0, q))
                mm.then_inc(unit_done, 1)

            def ret_o(l, u):
                ft = u[1]
                pe.wait_ge(rs_ready, 6 * l + 2 * ft + 2)
                pe.wait_ge(vtok_ready, 4 * l + 4)
                b = unit(l, u)
                for hh in range(2):
                    h = 2 * ft + hh
                    o = b[64 * hh:64 * hh + 64, :]
                    hc = slice(64 * h, 64 * h + 64)
                    pos = (0, 64 * hh)
                    pe.matmul(o[:, 0:128], V_tok[:, 0, 1, hc], RS[:, h, 0:128], start=True, stop=True, tile_position=pos)
                    pe.matmul(o[:, 128:256], V_tok[:, 0, 1, hc], RS[:, h, 128:256], start=True, stop=False, tile_position=pos)
                    mm = pe.matmul(o[:, 128:256], V_tok[:, 1, 1, hc], RS[:, h, 256:384], start=False, stop=True, tile_position=pos)
                mm.then_inc(unit_done, 1)

            def glu(l, u):
                pe.wait_ge(gelu_done, l + 1)
                b = unit(l, u)
                for k in range(2):
                    mm = pe.matmul(b[:, 0:T], glu_w[:, k, 128 * u[1]:128 * u[1] + 128], Y[:, k, :], start=(k == 0), stop=(k == 1))
                mm.then_inc(unit_done, 1)

            def head_mean(l, u, src):
                b = unit(l, u)
                pe.matmul(b[:, 0:T], cv("head_mean"), src, start=True, stop=True).then_inc(unit_done, 1)

            def hg_ms(l, u):
                pe.wait_ge(hsq_ready, 3 * l + u[1] + 1)
                head_mean(l, u, head_sq[:, u[1], :])

            def ret_mu(l, u):
                pe.wait_ge(ort_copied, 11 * l + 11)
                head_mean(l, u, MIX[:, 3 + u[1], :])

            def ret_var(l, u):
                pe.wait_ge(rsq_ready, 3 * l + u[1] + 1)
                head_mean(l, u, head_sq[:, 3 + u[1], :])

            def ln_mu_part(l, u):
                w, k = u[1:]
                b = unit(l, (f"ln{w + 1}_mu",)) if k == 0 else bank(l, (f"ln{w + 1}_mu",))
                pe.wait_ge(res_ready, 16 * l + 8 * w + k + 1)
                pe.matmul(b[:, 0:T], cv("model_mean"), (X1, X)[w][:, k, :], start=(k == 0), stop=False)

            def model_mean(l, u, w, ready, src):
                mean = ready is res_ready
                b = bank(l, u) if mean else unit(l, u)
                for k in range(KT - 2 if mean else 0, KT):
                    pe.wait_ge(ready, 16 * l + 8 * w + k + 1)
                    mm = pe.matmul(b[:, 0:T], cv("model_mean"), src[:, k, :], start=(k == 0), stop=(k == KT - 1))
                mm.then_inc(unit_done, 1)

            def ln1_mu(l, u):
                model_mean(l, u, 0, res_ready, X1)

            def ln1_var(l, u):
                model_mean(l, u, 0, lnsq_ready, sq)

            def ln2_mu(l, u):
                model_mean(l, u, 1, res_ready, X)

            def ln2_var(l, u):
                model_mean(l, u, 1, lnsq_ready, sq)

            units = dict(s5_in=s5_in, s5_in_sample=s5_in_sample, s5_out=s5_out, s5_out_sample=s5_out_sample, tr_hi=tr_hi, tr_hi_sample=tr_hi_sample,
                         tr_rv=tr_rv, tr_rv_sample=tr_rv_sample, tr_hk_sample=tr_hk_sample, tr_rk_sample=tr_rk_sample, tr_rk=tr_rk, tr_hkd=tr_hkd,
                         hg_level=hg_level, hg_far=hg_far, hg_state=hg_state, hg_kv=hg_kv, ret_kv=ret_kv, hg_o=hg_o, hg_o_sample=hg_o_sample,
                         ret_o_sample=ret_o_sample, ret_score=ret_score, ret_state=ret_state, ret_o=ret_o, glu=glu, hg_ms=hg_ms, ret_mu=ret_mu,
                         ret_var=ret_var, ln_mu_part=ln_mu_part, ln1_mu=ln1_mu, ln1_var=ln1_var, ln2_mu=ln2_mu, ln2_var=ln2_var)

            for l in range(DEPTH):
                for c in range(N_CHUNKS):
                    n = l * N_CHUNKS + c
                    g = l * N_TILES + tile_index(c)
                    bnk = stream_bank[g % STREAM_BANKS]
                    first = c < DOWN_A or (UP_B <= c < DOWN_B) or (c - DOWN_A) % 2 == 0
                    last = c < DOWN_A or (UP_B <= c < DOWN_B) or (c - DOWN_A) % 2 == 1
                    if first:
                        need(pe, tile_free[g % STREAM_BANKS], g // STREAM_BANKS)
                    wait_low(pe, n)
                    down = DOWN_A <= c < UP_B or c >= DOWN_B
                    for kk in range(8):
                        if down:
                            k = kk + (0 if first else 8)
                            xh, xl = h_high[:, k, :], h_low[:, k, :]
                            if c in (DOWN_A, DOWN_A + 1, DOWN_B, DOWN_B + 1):
                                pe.wait_ge(h_ready, 32 * l + (FF_HALF if c >= DOWN_B else 0) + k + 1)
                        else:
                            k = MIX_ORDER[kk] if OUT0 <= c < UP_A else kk
                            xh, xl = a_high[:, k, :], a_low[:, k, :]
                            if c in (0, OUT0, UP_A):
                                pe.wait_ge(a_ready, 24 * l + 8 * (0, OUT0, UP_A).index(c) + kk + 1)
                        blk = slice(128 * k % CHUNK, 128 * k % CHUNK + 128)
                        wh, wl = w_high[:, n % SPLIT_SLOTS, blk], w_low[:, n % SPLIT_SLOTS, blk]
                        pe.matmul(bnk[:, 0:T], wh, xh, start=(first and kk == 0), stop=False)
                        pe.matmul(bnk[:, 0:T], wh, xl, start=False, stop=False)
                        mm = pe.matmul(bnk[:, 0:T], wl, xh, start=False, stop=(last and kk == 7))
                    mm.then_inc(chunk_done, 1)
                    if l == 0 and c == 0:
                        pe.wait_ge(const_loaded, 48)
                    for u in PLAN[c]:
                        units[u[0]](l, u)

        @block.scalar
        def _(act):
            def tile(l, c):
                return dense_tile(act, l, c)

            def got(l, name):
                act.wait_ge(unit_done, unit_index(l, name) + 1)
                return bank(l, name), unit_freed(l, name)

            def copied(s, n, freed):
                act.wait_ge(s, n)
                act.sem_inc(freed, 1)

            def split_high(n):
                if n >= DEPTH * N_CHUNKS:
                    return
                act.wait_ge(raw_loaded[n % RAW_SLOTS], 16 * (n // RAW_SLOTS + 1))
                if n >= SPLIT_SLOTS:
                    act.wait_ge(chunk_done, n - SPLIT_SLOTS + 1)
                act.activation(w_high[:, n % SPLIT_SLOTS, :], w_raw[:, n % RAW_SLOTS, :], ACT.Copy).then_inc(high_ready, 1)

            def s5_dt(l):
                act.activation(par[:, 0, :], pv(l, "log_dt"), ACT.Exp).then_inc(act_params, 1)

            def s5_sin(l):
                act.wait_ge(par_ready, l + 1)
                act.activation(par[:, 3:5, :], par[:, 1:3, :], ACT.Sin).then_inc(act_params, 1)

            def gate_sigmoid(l, i):
                p, _ = tile(l, HGT + i)
                act.activation(gates[:, i, :], p, ACT.Sigmoid).then_inc(gsig_ready, 1)

            def mixer_work(l, c):
                if HF < c <= HF + 3:
                    i = c - 1 - HF
                    lb, one_lb = low[:, l, i:i + 1], low[:, 6 + l, i:i + 1]
                    p, fr = tile(l, HF + i)
                    act.activation(sig_f[:, i, :], p, ACT.Sigmoid).then_inc(sig_ready, 1)
                    act.activation(sig_n[:, i, :], p, ACT.Sigmoid, scale=-1.0).then_inc(sig_ready, 1)
                    copied(sig_ready, 6 * l + 2 * i + 2, fr)
                    act.wait_ge(bounds_ready, 1)
                    act.activation(Fg[:, i, :], sig_f[:, i, 0:SEQ], ACT.Identity, scale=one_lb, bias=lb).then_inc(gate_ready, 1)
                    act.activation(Fs[:, i, :], sig_f[:, i, SEQ:T], ACT.Identity, scale=one_lb, bias=lb).then_inc(gate_ready, 1)
                    act.activation(Kg[:, i, :], sig_n[:, i, :], ACT.Copy, scale=one_lb).then_inc(gate_ready, 1)
                elif HQ < c <= HQ + 3:
                    i = c - 1 - HQ
                    p, fr = tile(l, HQ + i)
                    act.activation(Qg[:, i, :], p, ACT.Sigmoid).then_inc(qsig_ready, 1)
                elif SU < c <= SU + 2:
                    i = c - 1 - SU
                    p, fr = tile(l, SU + i)
                    act.activation(U[:, i, :], p, ACT.Copy).then_inc(u_ready, 1)
                    copied(u_ready, 2 * l + i + 1, fr)
                elif HI < c <= HI + 3:
                    i = c - 1 - HI
                    p, fr = tile(l, HI + i)
                    act.wait_ge(table_ready, l + 1)
                    act.activation(Vf[:, i, :], p, ACT.Copy).then_inc(v_ready, 1)
                    copied(v_ready, 6 * l + i + 1, fr)
                elif RQ < c <= RQ + 4:
                    i = c - 1 - RQ
                    p, fr = tile(l, RQ + i)
                    dst = QR[:, i, :] if i < 2 else KR[:, i - 2, :]
                    act.activation(dst, p, ACT.Copy, scale=1.0 if i < 2 else RET_DK ** -0.5).then_inc(rqk_ready, 1)
                    copied(rqk_ready, 4 * l + i + 1, fr)
                elif RV < c <= RV + 3:
                    i = c - 1 - RV
                    p, fr = tile(l, RV + i)
                    act.activation(Vf[:, 3 + i, :], p, ACT.Copy).then_inc(v_ready, 1)
                    copied(v_ready, 6 * l + 3 + i + 1, fr)
                elif HGT < c <= HGT + 5:
                    gate_sigmoid(l, c - 1 - HGT)
                if c == 12:
                    for t in range(2):
                        b, fu = got(l, ("tr_hi", t))
                        act.activation(V_tok[:, t, 0, :], b[:, 0:384], ACT.Copy).then_inc(vtok_ready, 1)
                        copied(vtok_ready, 4 * l + t + 1, fu)
                    b, fu = got(l, ("tr_hi_sample",))
                    act.activation(vs_tok[:, 0, :], b[0:NSAMP, 0:384], ACT.Copy).then_inc(vs_ready, 1)
                    copied(vs_ready, 2 * l + 1, fu)
                    b, fu = got(l, ("tr_hk_sample",))
                    act.activation(ks_tok[:, 0:384], b[0:NSAMP, 0:384], ACT.Copy).then_inc(ks_ready, 1)
                    copied(ks_ready, 2 * l + 1, fu)
                if c == 14:
                    act.wait_ge(gelarg_ready, l + 1)
                    act.activation(gel, gel, ACT.Sigmoid).then_inc(gel_ready, 1)
                if c == 16:
                    for m in range(2):
                        b, fu = got(l, ("glu", m))
                        act.activation(gel[:, m, :], b[:, 0:T], ACT.Sigmoid, bias=pv(l, "glu_b")[:, m:m + 1]).then_inc(gel_ready, 1)
                        copied(gel_ready, 3 * l + m + 2, fu)
                    for h in range(2):
                        b, fu = got(l, ("hg_far", h))
                        act.activation(far[:, h, :, :], b[:, 0:384].rearrange("p (a b) -> p a b", a=3), ACT.Copy).then_inc(far_ready, 1)
                        copied(far_ready, 2 * l + h + 1, fu)
                if c == 17:
                    for t in range(2):
                        b, fu = got(l, ("tr_hkd", t))
                        act.activation(kt_hg[:, t, :], b[:, 0:384], ACT.Copy).then_inc(kt_ready, 1)
                        copied(kt_ready, 2 * l + t + 1, fu)
                if c == 18:
                    b, fu = got(l, ("hg_o_sample",))
                    pv_ = b[:, 0:24].rearrange("p (f b h) -> p f b h", f=3, b=4)
                    for h in range(2):
                        for bb in range(2):
                            dst = MIX[64 * h:64 * h + 64, 0:3, SEQ:T].rearrange("p f (b c) -> p f b c", c=2)[:, :, :, bb]
                            act.activation(dst, pv_[64 * bb:64 * bb + 64, :, :, h], ACT.Copy).then_inc(ohg_copied, 1)
                    copied(ohg_copied, 7 * l + 4, fu)
                    for ft in range(3):
                        b, fu = got(l, ("hg_o", ft))
                        act.activation(MIX[:, ft, 0:SEQ], b[:, 0:SEQ], ACT.Copy).then_inc(ohg_copied, 1)
                        copied(ohg_copied, 7 * l + 4 + ft + 1, fu)
                        act.activation(head_sq[:, ft, :], MIX[:, ft, :], ACT.Square).then_inc(hsq_ready, 1)
                    b, fu = got(l, ("hg_state",))
                    if l:
                        act.wait_ge(outs["hg_p"], 16 * l)
                        act.wait_ge(outs["rt_p"], 16 * l)
                    act.activation(st_p[:, 0:3, :], b[:, 0:192].rearrange("p (a b) -> p a b", a=3), ACT.Copy).then_inc(stp_ready, 1)
                    copied(stp_ready, 3 * l + 1, fu)
                if c == 19:
                    b, fu = got(l, ("tr_rv_sample",))
                    act.activation(vs_tok[:, 1, :], b[0:NSAMP, 0:384], ACT.Copy).then_inc(vs_ready, 1)
                    copied(vs_ready, 2 * l + 2, fu)
                    b, fu = got(l, ("tr_rk_sample",))
                    act.activation(ks_tok[:, 384:640], b[0:NSAMP, 0:256], ACT.Copy).then_inc(ks_ready, 1)
                    copied(ks_ready, 2 * l + 2, fu)
                    for t in range(2):
                        b, fu = got(l, ("tr_rv", t))
                        act.activation(V_tok[:, t, 1, :], b[:, 0:384], ACT.Copy).then_inc(vtok_ready, 1)
                        copied(vtok_ready, 4 * l + 2 + t + 1, fu)
                if c == 20:
                    for ft in range(3):
                        b, fu = got(l, ("hg_ms", ft))
                        act.activation(head_sq[:, ft, :], b[:, 0:T], ACT.Sqrt, bias=cv("eps")).then_inc(hsd_ready, 1)
                        copied(hsd_ready, 3 * l + ft + 1, fu)
                if c == 21:
                    for ft in range(3):
                        b, fu = got(l, ("ret_o", ft))
                        act.activation(MIX[:, 3 + ft, 0:SEQ], b[:, 0:SEQ], ACT.Copy).then_inc(ort_copied, 1)
                        copied(ort_copied, 11 * l + ft + 1, fu)
                    b, fu = got(l, ("ret_state",))
                    act.activation(st_p[:, 3, :], b[:, 0:64], ACT.Copy).then_inc(stp_ready, 1)
                    act.activation(st_p[0:64, 4, :], b[0:64, 64:128], ACT.Copy).then_inc(stp_ready, 1)
                    copied(stp_ready, 3 * l + 3, fu)
                if c == 22:
                    b, fu = got(l, ("ret_o_sample",))
                    pq = b[:, 0:32].rearrange("p (i b h) -> p i b h", i=2, b=4)
                    for hp in range(2):
                        for bb in range(2):
                            dst = MIX[64 * hp:64 * hp + 64, 3:6, SEQ:T].rearrange("p f (b c) -> p f b c", c=2)[:, :, :, bb]
                            src = pq[64 * bb:64 * bb + 64, :, :, :]
                            act.activation(dst[:, 0:2, :], src[:, 0, :, hp::2].rearrange("p b h -> p h b"), ACT.Copy).then_inc(ort_copied, 1)
                            act.activation(dst[:, 2, :], src[:, 1, :, hp], ACT.Copy).then_inc(ort_copied, 1)
                    copied(ort_copied, 11 * l + 11, fu)
                if c == 23:
                    for ft in range(3):
                        act.wait_ge(orc_ready, 3 * l + ft + 1)
                        act.activation(head_sq[:, 3 + ft, :], MIX[:, 3 + ft, :], ACT.Square).then_inc(rsq_ready, 1)

            def split_a(l, m, ready, n):
                act.wait_ge(ready, n)
                act.activation(a_high[:, m, :], MIX[:, m, :], ACT.Copy).then_inc(ahigh_ready, 1)

            def mixer_end(l):
                act.wait_ge(chunk_done, l * N_CHUNKS + N_IN)
                for i in (0, 1, 2):
                    split_a(l, i, hmix_ready, l + 1)
                for i in (6, 7):
                    split_a(l, i, glu_done, l + 1)
                gate_sigmoid(l, 5)
                for ft in range(3):
                    b, fu = got(l, ("ret_var", ft))
                    act.activation(head_sq[:, 3 + ft, :], b[:, 0:T], ACT.Sqrt, bias=cv("eps")).then_inc(rsd_ready, 1)
                    copied(rsd_ready, 3 * l + ft + 1, fu)
                for i in range(3, 6):
                    split_a(l, i, rmix_ready, 3 * l + i - 2)

            def norm(l, w):
                x = X1 if w == 0 else X
                for m in range(KT):
                    act.wait_ge(lnc_ready, 16 * l + 8 * w + m + 1)
                    act.activation(sq[:, m, :], x[:, m, :], ACT.Square).then_inc(lnsq_ready, 1)
                b, fu = got(l, (f"ln{w + 1}_var",))
                act.activation(sq[:, 0, :], b[:, 0:T], ACT.Sqrt, bias=cv("eps")).then_inc(lnsd_ready, 1)
                copied(lnsd_ready, 2 * l + w + 1, fu)
                for m in range(KT):
                    n = 16 * l + 8 * w + m + 1
                    act.wait_ge(lns_ready, n)
                    act.activation(x[:, m, :], sq[:, m, :] if m else sq0, ACT.Identity, scale=pv(l, f"ln{w + 1}_w")[:, m:m + 1],
                                   bias=pv(l, f"ln{w + 1}_b")[:, m:m + 1]).then_inc(ln_ready, 1)
                    if not (w and l == DEPTH - 1):
                        act.wait_ge(ln_ready, n)
                        act.activation(a_high[:, m, :], x[:, m, :], ACT.Copy).then_inc(ahigh_ready, 1)

            def hidden(l, m):
                c = UP_A + m if m < FF_HALF else UP_B + m - FF_HALF
                p, fr = tile(l, c)
                n = 32 * l + m
                if m >= 2 or l:
                    act.wait_ge(hfull_ready, n - 1)
                act.activation(relu[:, m % 2, :], p, ACT.Relu).then_inc(relu_ready, 1)
                copied(relu_ready, n + 1, fr)
                act.wait_ge(hfull_ready, n + 1)
                act.activation(h_high[:, m % FF_HALF, :], h_full[:, m % 2, :], ACT.Copy).then_inc(hhigh_ready, 1)

            for m in range(0, KT, 2):
                act.dma_start(X[:, m:m + 2, :], xT[:, m:m + 2, :]).then_inc(x_loaded, 16)
            act.wait_ge(vecs_loaded, 16)
            s5_dt(0)
            act.wait_ge(dve_step, 3)
            act.activation(low[:, 0:2, :], low[:, 2:4, :], ACT.Exp).then_inc(softmax_exp, 1)
            s5_sin(0)
            act.wait_ge(x_loaded, 64)
            for m in range(KT):
                act.activation(a_high[:, m, :], X[:, m, :], ACT.Copy).then_inc(ahigh_ready, 1)
            for n in range(AHEAD):
                split_high(n)
            for l in range(DEPTH):
                for c in range(N_CHUNKS):
                    split_high(l * N_CHUNKS + c + AHEAD)
                    if c < N_IN:
                        mixer_work(l, c)
                        if c == N_IN - 1:
                            mixer_end(l)
                    elif c == UP_A - 1:
                        norm(l, 0)
                        if l + 1 < DEPTH:
                            act.wait_ge(table_ready, l + 1)
                            s5_dt(l + 1)
                    elif UP_A < c <= DOWN_A:
                        hidden(l, c - 1 - UP_A)
                    elif c == DOWN_A + 3 and l + 1 < DEPTH:
                        s5_sin(l + 1)
                    elif UP_B < c <= DOWN_B:
                        hidden(l, c - 1 - UP_B + FF_HALF)
                norm(l, 1)

        @block.vector
        def _(dve):
            last = {"sem": None, "n": 0}
            count = {}

            def put(ins, s=None):
                s = dve_step if s is None else s
                count[s.name] = count.get(s.name, 0) + 1
                ins.then_inc(s, 1)
                last["sem"], last["n"] = s, count[s.name]

            def settle():
                dve.wait_ge(last["sem"], last["n"])

            def chain(ins, s=None):
                put(ins, s)
                settle()

            def free(s):
                settle()
                dve.sem_inc(s, 1)

            def got(l, name):
                dve.wait_ge(unit_done, unit_index(l, name) + 1)
                return bank(l, name), unit_freed(l, name)

            def tile(l, c):
                return dense_tile(dve, l, c)

            tt, ts, stt, cp = dve.tensor_tensor, dve.tensor_scalar, dve.scalar_tensor_tensor, dve.tensor_copy
            DT, RC, RS_, COS, SIN, TH, ZR, EX, MAG, ABR, ABI, DEN, GR, GI, T0, T1, T2, PC, PS, NR = range(20)

            def row(i):
                return par[:, i, :]

            def split_low(n):
                if n >= DEPTH * N_CHUNKS or n % N_CHUNKS < N_IN:
                    return
                dve.wait_ge(high_ready, n + 1)
                put(tt(w_low[:, n % SPLIT_SLOTS, :], w_raw[:, n % RAW_SLOTS, :], w_high[:, n % SPLIT_SLOTS, :].bitcast(F32), ALU.subtract), low_ready)

            def split_a(l, part, k, src, m):
                dve.wait_ge(ahigh_ready, 24 * l + 8 * part + k + 1)
                put(tt(a_low[:, m, :], src[:, m, :], a_high[:, m, :].bitcast(F32), ALU.subtract), a_ready)

            rot_tmp = MIX[:, :, :].rearrange("p a b -> p (a b)")

            def s5_tables(l):
                are, aim = pv(l, "a_re"), pv(l, "a_im")
                dve.wait_ge(act_params, 2 * l + 1)
                chain(tt(row(TH), row(DT), aim, ALU.mult))
                two_pi_hi, two_pi_lo = 6.28125, float(2 * np.pi - 6.28125)
                magic = 12582912.0
                for dst, shift in ((RS_, 0.0), (RC, 0.25)):
                    chain(ts(row(T0), row(TH), float(1 / (2 * np.pi)), shift, ALU.mult, ALU.add))
                    chain(ts(row(T0), row(T0), magic, None, ALU.add))
                    chain(ts(row(T0), row(T0), -magic, None, ALU.add))
                    chain(stt(row(T1), row(T0), -two_pi_hi, row(TH), ALU.mult, ALU.add))
                    chain(stt(row(T1), row(T0), -two_pi_lo, row(T1), ALU.mult, ALU.add))
                    chain(ts(row(T1), row(T1), float(shift * 2 * np.pi), None, ALU.add))
                    chain(ts(row(dst), row(T1), 3.1415925, -3.1415925, ALU.min, ALU.max), par_ready if dst == RC else None)
                yield
                chain(tt(row(ZR), row(DT), are, ALU.mult))
                chain(ts(row(ZR), row(ZR), 1.0 / 16, None, ALU.mult))
                chain(ts(row(EX), row(ZR), 1.0 / 8, 1.0, ALU.mult, ALU.add))
                for n in range(7, 0, -1):
                    chain(tt(row(EX), row(EX), row(ZR), ALU.mult))
                    chain(ts(row(EX), row(EX), 1.0 / n, 1.0, ALU.mult, ALU.add))
                yield
                for n in range(4):
                    chain(tt(row(MAG if n == 3 else EX), row(EX), row(EX), ALU.mult))
                dve.wait_ge(act_params, 2 * l + 2)
                chain(tt(row(ABR), row(MAG), row(COS), ALU.mult))
                chain(tt(row(ABI), row(MAG), row(SIN), ALU.mult))
                chain(ts(row(NR), row(ABR), -1.0, None, ALU.add))
                chain(tt(row(T0), are, are, ALU.mult))
                chain(tt(row(T1), aim, aim, ALU.mult))
                chain(tt(row(DEN), row(T0), row(T1), ALU.add))
                chain(dve.reciprocal(row(DEN), row(DEN)))
                yield
                chain(tt(row(T0), row(NR), are, ALU.mult))
                chain(tt(row(T1), row(ABI), aim, ALU.mult))
                chain(tt(row(T0), row(T0), row(T1), ALU.add))
                chain(tt(row(GR), row(T0), row(DEN), ALU.mult))
                chain(tt(row(T0), row(ABI), are, ALU.mult))
                chain(tt(row(T1), row(NR), aim, ALU.mult))
                chain(tt(row(T0), row(T0), row(T1), ALU.subtract))
                chain(tt(row(GI), row(T0), row(DEN), ALU.mult))
                yield
                C, S = rot[:, 0, :, :], rot[:, 1, :, :]
                chain(dve.memset(rot[:, 0, :, 0:1], 1.0))
                chain(dve.memset(rot[:, 1, :, 0:1], 0.0))
                put(cp(row(PC), row(COS)))
                chain(cp(row(PS), row(SIN)))
                n = 1
                while n < SEQ:
                    pc = row(PC).unsqueeze(2).broadcast_to([128, 8, n])
                    ps = row(PS).unsqueeze(2).broadcast_to([128, 8, n])
                    tmp = rot_tmp[:, 0:8 * n].rearrange("p (a b) -> p a b", a=8)
                    put(tt(tmp, S[:, :, 0:n], ps, ALU.mult))
                    chain(tt(C[:, :, n:2 * n], C[:, :, 0:n], pc, ALU.mult))
                    put(tt(C[:, :, n:2 * n], C[:, :, n:2 * n], tmp, ALU.subtract))
                    chain(tt(S[:, :, n:2 * n], S[:, :, 0:n], pc, ALU.mult))
                    chain(tt(tmp, C[:, :, 0:n], ps, ALU.mult))
                    chain(tt(S[:, :, n:2 * n], S[:, :, n:2 * n], tmp, ALU.add))
                    n *= 2
                    if n < SEQ:
                        chain(tt(row(T0), row(PC), row(PC), ALU.mult))
                        chain(tt(row(T1), row(PS), row(PS), ALU.mult))
                        chain(tt(row(T2), row(PC), row(PS), ALU.mult))
                        chain(tt(row(PC), row(T0), row(T1), ALU.subtract))
                        chain(ts(row(PS), row(T2), 2.0, None, ALU.mult))
                    yield
                dve.wait_ge(mats_loaded, 16 * (l + 1))
                gr = row(GR).unsqueeze(2).broadcast_to([128, 8, 32])
                gi = row(GI).unsqueeze(2).broadcast_to([128, 8, 32])
                tmp = rot_tmp[:, 0:256].rearrange("p (a b) -> p a b", a=8)
                chain(tt(Cg[:, :, 0, :], C_s5[:, :, 0, :], gr, ALU.mult))
                chain(tt(tmp, C_s5[:, :, 1, :], gi, ALU.mult))
                chain(tt(Cg[:, :, 0, :], Cg[:, :, 0, :], tmp, ALU.subtract))
                chain(tt(Cg[:, :, 1, :], C_s5[:, :, 1, :], gr, ALU.mult))
                chain(tt(tmp, C_s5[:, :, 0, :], gi, ALU.mult))
                chain(stt(Cg[:, :, 1, :], Cg[:, :, 1, :], -1.0, tmp, ALU.mult, ALU.subtract))
                chain(ts(Cg[:, :, 2, :], Cg[:, :, 0, :], -1.0, None, ALU.mult))
                chain(ts(Cs[:, :, :], C_s5[:, :, 1, :], -1.0, None, ALU.mult), table_ready)

            def run(pieces):
                for _ in pieces:
                    pass

            def s5_tile(l, j):
                b, fu = got(l, ("s5_in", j))
                bb = b[:, :].rearrange("p (r t) -> p r t", r=2)
                c = rot[:, 0, j, :].unsqueeze(1).broadcast_to([128, 2, SEQ])
                s = rot[:, 1, j, :].unsqueeze(1).broadcast_to([128, 2, SEQ])
                p1, p2 = (p.rearrange("p (r t) -> p r t", r=2) for p in (P1, P2))
                put(tt(p1, bb, c, ALU.mult))
                chain(tt(p2, bb, s, ALU.mult))
                dve.sem_inc(fu, 1)
                put(tt(W5[:, 0:256], P1[:, 0:256], P2[:, 256:512], ALU.add))
                chain(tt(W5[:, 256:512], P1[:, 256:512], P2[:, 0:256], ALU.subtract))
                mag = row(MAG)[:, j:j + 1].broadcast_to([128, SEQ])
                for r in range(2):
                    put(dve.tensor_tensor_scan(Z5[:, 256 * r:256 * r + 256], mag, W5[:, 256 * r:256 * r + 256], 0.0, ALU.mult, ALU.add))
                settle()
                if j >= 2:
                    dve.wait_ge(y5_done, 8 * l + j - 1)
                z = Z5.rearrange("p (r t) -> p r t", r=2)
                x = XS[j % 2]
                put(tt(x[:, 0:512].rearrange("p (r t) -> p r t", r=2), z, c, ALU.mult))
                chain(tt(x[:, 512:1024].rearrange("p (r t) -> p r t", r=2), z, s, ALU.mult), xs_ready)
                put(tt(s5last[:, 0, j:j + 1], x[:, 255:256], x[:, 1023:1024], ALU.subtract))
                put(tt(s5last[:, 1, j:j + 1], x[:, 511:512], x[:, 767:768], ALU.add))

            def hgrn_q(l, j):
                dve.wait_ge(qsig_ready, 3 * l + j + 1)
                p, fr = tile(l, HQ + j)
                put(tt(Qg[:, j, :], Qg[:, j, :], p, ALU.mult), None if j < 2 else q_ready)
                free(fr)

            def s5_states(l):
                settle()
                if l:
                    dve.wait_ge(outs["s5_p"], 16 * l)
                    dve.wait_ge(outs["s5_s"], 16 * l)
                put(tt(s5fin[:, 0, :], s5last[:, 0, :], row(GR), ALU.mult))
                chain(tt(row(T0), s5last[:, 1, :], row(GI), ALU.mult))
                put(tt(s5fin[:, 0, :], s5fin[:, 0, :], row(T0), ALU.subtract))
                put(tt(s5fin[:, 1, :], s5last[:, 0, :], row(GI), ALU.mult))
                chain(tt(row(T1), s5last[:, 1, :], row(GR), ALU.mult))
                put(tt(s5fin[:, 1, :], s5fin[:, 1, :], row(T1), ALU.add), s5fin_ready)
                b, fu = got(l, ("s5_in_sample",))
                bv = b[:, 0:128].rearrange("p (r j t) -> p r j t", r=2, j=8)

                def wide(i):
                    return row(i).unsqueeze(2).broadcast_to([128, 8, NSAMP])

                for cr, ci, src in ((ABR, ABI, s5x0[:, l, :, :, :]), (GR, GI, bv)):
                    for r, op in enumerate((ALU.subtract, ALU.add)):
                        put(tt(s5tmp[:, 0, :, :], src[:, r, :, :], wide(cr), ALU.mult))
                        chain(tt(s5tmp[:, 1, :, :], src[:, 1 - r, :, :], wide(ci), ALU.mult))
                        if cr == ABR:
                            chain(tt(s5xs[:, r, :, :], s5tmp[:, 0, :, :], s5tmp[:, 1, :, :], op))
                        else:
                            chain(tt(s5tmp[:, 0, :, :], s5tmp[:, 0, :, :], s5tmp[:, 1, :, :], op))
                            chain(tt(s5xs[:, r, :, :], s5xs[:, r, :, :], s5tmp[:, 0, :, :], ALU.add), s5fin_ready if r == 1 else None)
                dve.sem_inc(fu, 1)
                dve.sem_inc(xss_ready, 1)

            def s5_gelu_argument(l):
                dve.wait_ge(y5_done, 8 * l + 8)
                for m in range(2):
                    put(stt(Y[:, m, 0:256], U[:, m, 0:256], pv(l, "d")[:, m:m + 1], y5_bank[:, m, :], ALU.mult, ALU.add))
                free(y5_free)
                b, fu = got(l, ("s5_out_sample",))
                for m in range(2):
                    put(stt(Y[:, m, 256:T], U[:, m, 256:T], pv(l, "d")[:, m:m + 1], b[:, 8 * m:8 * m + 8], ALU.mult, ALU.add))
                free(fu)
                chain(tt(gel, Y, Y, ALU.mult))
                chain(ts(gel, gel, GELU_C1, GELU_C0, ALU.mult, ALU.add))
                put(tt(gel, gel, Y, ALU.mult), gelarg_ready)

            def halves(x, half):
                v = x.rearrange("p f (n c) -> p f n c", c=2 * half)
                return v[:, :, :, 0:half], v[:, :, :, half:2 * half]

            def level_decay(l, r):
                half = 1 << r
                k_l, k_r = halves(Kg[:, :, 0:256], half)
                q_l, q_r = halves(Qg[:, :, 0:256], half)
                F_l, F_r = halves(Fg[:, :, :], half)
                G_l, G_r = halves(Gg[:, :, :], half)
                if r >= 2:
                    dve.wait_ge(unit_done, unit_index(l, ("hg_level", r - 2, 2)) + 1)
                if r == 0:
                    dve.wait_ge(gate_ready, 9 * l + 9)
                settle()
                if r == 0:
                    put(cp(halves(kdec[0], 1)[1], k_r))
                    put(tt(halves(kdec[0], 1)[0], k_l, F_r, ALU.mult), dec_ready)
                    put(dve.memset(G_r, 1.0))
                    put(cp(G_l, F_r))
                    chain(tt(F_r, F_r, F_l, ALU.mult))
                    return
                put(tt(halves(qdec[r % 2], half)[1], q_r, F_r, ALU.mult))
                put(tt(halves(kdec[r % 2], half)[0], k_l, G_l, ALU.mult), dec_ready)
                nb = 3 * SEQ // (2 * half)
                F2 = Fg[:, :, :].rearrange("p f (n c) -> p (f n) c", c=2 * half)
                G2 = Gg[:, :, :].rearrange("p f (n c) -> p (f n) c", c=2 * half)
                settle()
                chain(tt(G2[:, :, 0:half], G2[:, :, 0:half], F2[:, :, 2 * half - 1:2 * half].broadcast_to([128, nb, half]), ALU.mult))
                if r < 7:
                    put(tt(F2[:, :, half:2 * half], F2[:, :, half:2 * half], F2[:, :, half - 1:half].broadcast_to([128, nb, half]), ALU.mult))

            def near_level(l, r):
                for part in range(3):
                    b, fu = got(l, ("hg_level", r, part))
                    m = masks[:, r, :].unsqueeze(1).unsqueeze(1).broadcast_to([128, 2, 2, 128])
                    dst = near[:, part, 0:2, :, :] if part < 2 else near[:, :, 2, :, :]
                    put(dve.copy_predicated(dst, m, b[:, :].rearrange("p (a c t) -> p a c t", a=2, c=2)))
                    if part == 1:
                        free(got(l, ("hg_level", r, 0))[1])
                        dve.sem_inc(fu, 1)
                free(fu)
                dve.sem_inc(near_ready, 1)

            def rotary(l, X_):
                sw = swapped
                settle()
                chain(dve.stream_shuffle(sw, X_[:, :, :], [i ^ 16 for i in range(32)]))
                put(tt(X_[:, :, :], X_[:, :, :], cv("cos").unsqueeze(1).broadcast_to([128, 2, T]), ALU.mult))
                chain(tt(sw, sw, cv("sin").unsqueeze(1).broadcast_to([128, 2, T]), ALU.mult))
                put(tt(X_[:, :, :], X_[:, :, :], sw, ALU.add), ret_ready)

            def output_gate(l, i):
                dve.wait_ge(gsig_ready, 6 * l + i + 1)
                p, fr = tile(l, HGT + i)
                w = pv(l, "hg_norm")[:, 0:1] if i < 3 else pv(l, "ret_norm")[:, i - 3:i - 2]
                put(stt(gates[:, i, :], gates[:, i, :], w, p, ALU.mult, ALU.mult))
                free(fr)

            def hgrn_sample_decay(l):
                dve.wait_ge(states_loaded, 32 * (l + 1))
                S = S_hg[:, :, :, :].rearrange("p a b v -> p (a b) v")
                put(tt(S, S, Fs[:, :, :].rearrange("p a b -> p (a b)").unsqueeze(2).broadcast_to([128, 24, DV]), ALU.mult))

            def hgrn_sample_add(l, ft):
                b, fu = got(l, ("hg_kv", ft))
                S = S_hg[:, ft, :, :].rearrange("p b v -> p (b v)")
                settle()
                put(tt(S, S, b[:, :], ALU.add), shg_ready)
                free(fu)

            def hgrn_sample_q(l):
                settle()
                for ft in range(3):
                    put(tt(qs_hg[:, ft, :, :], S_hg[:, ft, :, :], Qg[:, ft, SEQ:T].unsqueeze(2).broadcast_to([128, NSAMP, DV]), ALU.mult),
                        qshg_ready if ft == 2 else None)

            def ret_sample_add(l, i):
                b, fu = got(l, ("ret_kv", i))
                n = 128 if i == 0 else 64
                S = S_rt[0:n, i, :, :].rearrange("p b v -> p (b v)")
                put(stt(S, S, cv("gamma")[0:n, i:i + 1], b[0:n, :], ALU.mult, ALU.add), srt_ready)
                free(fu)

            def ret_sample_q(l):
                settle()
                for i in range(2):
                    put(tt(qs_rt[:, i, :, :], S_rt[:, i, :, :], QR[:, i, SEQ:T].unsqueeze(2).broadcast_to([128, NSAMP, DV]), ALU.mult),
                        qsrt_ready if i == 1 else None)

            def ret_scores(l, h):
                b, fu = got(l, ("ret_score", h))
                put(tt(RS[:, h, 0:256], b[:, 0:256], decay[:, h, :], ALU.mult))
                put(tt(RS[:, h, 256:384], b[:, 256:384], decay[:, h, 0:128], ALU.mult), rs_ready)
                free(fu)

            def ret_k_decay(l, t):
                b, fu = got(l, ("tr_rk", t))
                put(tt(kt_rt[:, t, :], b[:, 0:256], k_decay[:, t, :], ALU.mult), ktr_ready)
                free(fu)

            def mixer_work(l, c):
                if 3 <= c < 3 + S5_TILES:
                    s5_tile(l, c - 3)
                if 6 <= c < 9:
                    hgrn_q(l, c - 6)
                if c == 11:
                    s5_states(l)
                if c == 13:
                    s5_gelu_argument(l)
                if 9 <= c < 16:
                    near_level(l, c - 9)
                if 14 <= c < 17:
                    hgrn_sample_add(l, c - 14)
                if c == 7:
                    dve.wait_ge(cleared, 3 + l)
                if 7 <= c < 15:
                    level_decay(l, c - 7)
                if c == 12:
                    hgrn_sample_decay(l)
                if c == 14:
                    dve.wait_ge(gel_ready, 3 * l + 1)
                    put(tt(Y, Y, gel, ALU.mult), gelu_done)
                if c == 15:
                    dve.wait_ge(unit_done, unit_index(l, ("hg_level", 6, 2)) + 1)
                    settle()
                    put(tt(kdec[0], Kg[:, :, 0:256], Gg, ALU.mult), dec_ready)
                    dve.wait_ge(rqk_ready, 4 * l + 4)
                    rotary(l, KR)
                    rotary(l, QR)
                if c == 16:
                    hgrn_sample_q(l)
                    dve.wait_ge(gel_ready, 3 * l + 3)
                    put(tt(Y, Y, gel, ALU.mult), glu_done)
                if c == 17:
                    for t in range(2):
                        ret_k_decay(l, t)
                if 17 <= c < 20:
                    for h in range(2):
                        ret_scores(l, 2 * (c - 17) + h)
                if 19 <= c < 24:
                    output_gate(l, c - 19)
                if c == 21:
                    for i in range(2):
                        ret_sample_add(l, i)
                    ret_sample_q(l)
                if c == 22:
                    dve.wait_ge(hsd_ready, 3 * l + 3)
                    put(tt(MIX[:, 0:3, :], MIX[:, 0:3, :], gates[:, 0:3, :], ALU.mult))
                    chain(dve.reciprocal(head_sq[:, 0:3, :], head_sq[:, 0:3, :]))
                    put(tt(MIX[:, 0:3, :], MIX[:, 0:3, :], head_sq[:, 0:3, :], ALU.mult), hmix_ready)
                if c == 23:
                    for ft in range(3):
                        b, fu = got(l, ("ret_mu", ft))
                        put(tt(MIX[:, 3 + ft, :], MIX[:, 3 + ft, :], b[:, 0:T], ALU.subtract), orc_ready)
                        free(fu)

            def mixer_end(l):
                for k in range(5):
                    split_a(l, 1, k, MIX, MIX_ORDER[k])
                output_gate(l, 5)
                dve.wait_ge(rsq_ready, 3 * l + 3)
                settle()
                put(tt(MIX[:, 3:6, :], MIX[:, 3:6, :], gates[:, 3:6, :], ALU.mult))
                for ft in range(3):
                    dve.wait_ge(rsd_ready, 3 * l + ft + 1)
                    chain(dve.reciprocal(head_sq[:, 3 + ft, :], head_sq[:, 3 + ft, :]))
                    put(tt(MIX[:, 3 + ft, :], MIX[:, 3 + ft, :], head_sq[:, 3 + ft, :], ALU.mult), rmix_ready)
                for k in range(5, KT):
                    split_a(l, 1, k, MIX, MIX_ORDER[k])

            def residual(l, w, m):
                c = OUT0 + m if w == 0 else DOWN_B + 2 * m + 1
                p, fr = tile(l, c)
                if w == 0:
                    put(stt(X1[:, m, :], X[:, m, :], ALPHA, p, ALU.mult, ALU.add), res_ready)
                else:
                    put(tt(X[:, m, :], X[:, m, :], p, ALU.add), res_ready)
                free(fr)

            def half_down(l, m):
                p, fr = tile(l, DOWN_A + 2 * m + 1)
                put(stt(X[:, m, :], X1[:, m, :], ALPHA, p, ALU.mult, ALU.add))
                free(fr)

            def hidden(l, m):
                n = 32 * l + m
                dve.wait_ge(relu_ready, n + 1)
                put(tt(h_full[:, m % 2, :], relu[:, m % 2, :], relu[:, m % 2, :], ALU.mult), hfull_ready)

            def hidden_low(l, m):
                dve.wait_ge(hhigh_ready, 32 * l + m + 1)
                put(tt(h_low[:, m % FF_HALF, :], h_full[:, m % 2, :], h_high[:, m % FF_HALF, :].bitcast(F32), ALU.subtract), h_ready)

            def norm(l, w):
                x = X1 if w == 0 else X
                b, fu = got(l, (f"ln{w + 1}_mu",))
                for m in range(KT):
                    put(tt(x[:, m, :], x[:, m, :], b[:, 0:T], ALU.subtract), lnc_ready)
                free(fu)
                dve.wait_ge(lnsd_ready, 2 * l + w + 1)
                chain(dve.reciprocal(sq_r, sq[:, 0, :]))
                def scaled(m):
                    put(tt(sq[:, m, :] if m else sq0, x[:, m, :], sq_r, ALU.mult), lns_ready)

                scaled(0)
                scaled(1)
                for m in range(KT):
                    if m + 2 < KT:
                        scaled(m + 2)
                    if w == 0:
                        split_a(l, 2, m, x, m)
                    elif l + 1 < DEPTH:
                        split_a(l + 1, 0, m, x, m)
                if w and l == DEPTH - 1:
                    settle()

            dve.wait_ge(vecs_loaded, 16)
            lg = [pv(l, "logits") for l in range(DEPTH)]
            chain(tt(low[:, 4, :], lg[0], lg[1], ALU.max))
            chain(tt(low[:, 2, :], lg[0], low[:, 4, :], ALU.subtract))
            chain(tt(low[:, 3, :], lg[1], low[:, 4, :], ALU.subtract))
            first_table = s5_tables(0)
            next(first_table)
            dve.wait_ge(softmax_exp, 1)
            chain(tt(low[:, 4, :], low[:, 0, :], low[:, 1, :], ALU.add))
            chain(dve.reciprocal(low[:, 4, :], low[:, 4, :]))
            chain(tt(low[:, 2, :], low[:, 0, :], low[:, 4, :], ALU.mult))
            chain(tt(low[:, 3, :], low[:, 1, :], low[:, 4, :], ALU.mult))
            chain(tt(low[:, 0, :], low[:, 2, :], low[:, 2, :], ALU.subtract))
            chain(tt(low[:, 3, :], low[:, 2, :], low[:, 3, :], ALU.add))
            chain(tt(low[:, 1, :], low[:, 3, :], low[:, 2, :], ALU.subtract))
            for l in range(DEPTH):
                chain(ts(low[:, 6 + l, :], low[:, l, :], -1.0, 1.0, ALU.mult, ALU.add), bounds_ready if l == DEPTH - 1 else None)
            for _ in range(6):
                next(first_table)
            dve.wait_ge(x_loaded, 64)
            for m in range(KT):
                split_a(0, 0, m, X, m)
            run(first_table)
            dve.wait_ge(const_loaded, 48)
            put(cp(masks[:, :, :], masks_f32))

            for l in range(DEPTH):
                for c in range(N_CHUNKS):
                    split_low(l * N_CHUNKS + c + AHEAD)
                    if c < N_IN:
                        mixer_work(l, c)
                        if c == N_IN - 1:
                            mixer_end(l)
                    elif c < UP_A:
                        if c > OUT0:
                            residual(l, 0, c - 1 - OUT0)
                        if c == UP_A - 1:
                            residual(l, 0, KT - 1)
                            norm(l, 0)
                            table = s5_tables(l + 1) if l + 1 < DEPTH else iter(())
                    elif UP_A < c <= DOWN_A:
                        hidden(l, c - 1 - UP_A)
                        hidden_low(l, c - 1 - UP_A)
                    elif DOWN_A < c < UP_B and (c - DOWN_A) % 2 == 0:
                        half_down(l, (c - DOWN_A) // 2 - 1)
                        next(table, None)
                    elif UP_B <= c <= DOWN_B:
                        if c == UP_B:
                            half_down(l, KT - 1)
                        else:
                            hidden(l, c - 1 - UP_B + FF_HALF)
                            hidden_low(l, c - 1 - UP_B + FF_HALF)
                    elif c > DOWN_B:
                        if (c - DOWN_B) % 2 == 0:
                            residual(l, 1, (c - DOWN_B) // 2 - 1)
                        elif c < N_CHUNKS - 1:
                            next(table, None)
                        if c == N_CHUNKS - 1:
                            run(table)
                            residual(l, 1, KT - 1)
                norm(l, 1)


def _pack_weights(w_in, w_out, w_up, w_down):
    a = 384
    seg = {"hq": 0, "hf": a, "hi": 2 * a, "hg": 3 * a, "rq": 4 * a, "rk": 4 * a + 192, "rv": 4 * a + 384, "rg": 5 * a + 384, "su": 6 * a + 384}
    pad = np.zeros((DEPTH, D_MODEL, 64), w_in.dtype)

    def cut(name, n):
        return w_in[:, :, seg[name]:seg[name] + n]

    cols = np.concatenate([cut("su", 256), cut("hf", a), cut("hq", a), cut("hi", a), cut("rq", 192), pad, cut("rk", 192), pad,
                           cut("rv", a), cut("hg", a), cut("rg", a)], axis=2)
    def by_tiles(w):
        m = w.shape[2] // 128
        return w.reshape(DEPTH, KT, 128, m, 128).transpose(0, 3, 2, 1, 4).reshape(DEPTH, m, 128, CHUNK)

    up = by_tiles(w_up)
    down = w_down.reshape(DEPTH, 2, 2, 8, 128, KT, 128).transpose(0, 1, 5, 2, 4, 3, 6).reshape(DEPTH, 2, 2 * KT, 128, CHUNK)
    out = (by_tiles(cols), by_tiles(w_out), up[:, :FF_HALF], down[:, 0], up[:, FF_HALF:], down[:, 1])
    return np.ascontiguousarray(np.concatenate(out, axis=1))


def _columns(x, tiles):
    return x.reshape(DEPTH, tiles, 128).transpose(2, 0, 1)


def _constants():
    c = np.zeros((128, N_CV), np.float32)

    def put(name, value):
        a, n = CV[name]
        c[:, a:a + n] = value

    put("ident", np.eye(128))
    put("head_mean", np.kron(np.eye(2), np.ones((64, 64))) / 64)
    put("model_mean", 1.0 / D_MODEL)
    half = RET_DK // 2
    inv = np.float32(ROPE_BASE) ** (-np.arange(half, dtype=np.float32) / np.float32(half))
    pos = np.concatenate([np.arange(SEQ), np.full(NSAMP, PAST_LEN)]).astype(np.float32)
    ang = (inv[:, None] * pos[None, :]).astype(np.float32).astype(np.float64)
    p = np.arange(128) % 32
    cos, sin = np.cos(ang)[p % half], np.sin(ang)[p % half] * np.where(p < half, -1.0, 1.0)[:, None]
    put("cos", cos), put("sin", sin)
    log_gamma = np.log1p(-np.exp2(-5.0 - np.arange(HEADS))).astype(np.float32).astype(np.float64)
    s, t = np.arange(128)[:, None], np.arange(256)[None, :]
    dec = np.where(t >= s, np.exp(log_gamma[:, None, None] * np.maximum(t - s, 0)), 0.0)
    put("decay", dec.transpose(1, 0, 2).reshape(128, -1))
    left = 255 - np.arange(256)
    kd = np.zeros((2, 128, 256))
    kd[:, :, :192] = np.exp(left[:, None] * np.repeat(log_gamma, RET_DK)[None, :]).reshape(2, 128, 192)
    put("k_decay", kd.transpose(1, 0, 2).reshape(128, 512))
    g = np.zeros((128, 2))
    g[:, 0] = np.repeat(np.exp(log_gamma[:4]), 32)
    g[:64, 1] = np.repeat(np.exp(log_gamma[4:]), 32)
    put("gamma", g)
    put("eps", EPS)
    put("pair_sum", np.kron(np.eye(2), np.ones((64, 1))))
    put("quad_sum", np.kron(np.eye(4), np.ones((32, 1))))
    masks = np.zeros((128, 7, 128), np.float32)
    s, t = np.arange(128)[:, None], np.arange(128)[None, :]
    masks[:, 0, :] = (s >> 1 == t >> 1) & (s <= t)
    for L in range(1, 7):
        masks[:, L, :] = (s >> (L + 1) == t >> (L + 1)) & ((s >> L) & 1 == 0) & ((t >> L) & 1 == 1)
    return c, masks


def kernel(**inputs):
    import concourse.bacc as bacc
    from concourse.bass_utils import run_bass_kernel_spmd

    a = {k: np.asarray(v) for k, v in inputs.items()}
    f = np.float32
    x = np.concatenate([a["x_prompt"].reshape(SEQ, D_MODEL), a["x_sample"].reshape(NSAMP, D_MODEL)])
    arrays = {}
    arrays["xT"] = np.ascontiguousarray(x.reshape(T, KT, 128).transpose(2, 1, 0))
    arrays["weights"] = _pack_weights(a["w_in"], a["w_out"], a["w_up"], a["w_down"])
    vec = np.zeros((128, DEPTH, N_PV), f)

    def put(name, value):
        at, n = PV[name]
        vec[:, :, at:at + n] = value

    put("log_dt", _columns(np.repeat(a["s5_log_dt"], 64, axis=1), 8))
    put("a_re", _columns(a["s5_a_re"], 8))
    put("a_im", _columns(a["s5_a_im"], 8))
    put("d", _columns(a["s5_d"], 2))
    put("glu_b", _columns(a["s5_glu_b"], 2))
    put("hg_norm", _columns(np.tile(a["hgrn_norm_w"], (1, 2)), 1))
    put("ret_norm", _columns(a["ret_norm_w"], 3))
    for n in ("ln1_w", "ln1_b", "ln2_w", "ln2_b"):
        put(n, _columns(a[n], KT))
    put("logits", _columns(a["hgrn_lb_logits"], 3))
    arrays["vectors"] = vec
    mats = np.zeros((DEPTH, 128, MATS), f)
    Bm = np.zeros((DEPTH, 128, 2, 2, 128), f)
    Cm = np.zeros((DEPTH, 128, 8, 2, 32), f)
    for g in range(16):
        s, j, o = g // 8, g // 2, g % 2
        for r, n in enumerate(("re", "im")):
            Bm[:, 16 * (g % 8):16 * (g % 8) + 16, s, r, 64 * o:64 * o + 64] = a[f"s5_b_{n}"][:, g].transpose(0, 2, 1)
            Cm[:, 64 * o:64 * o + 64, j, r, 16 * o:16 * o + 16] = a[f"s5_c_{n}"][:, g].transpose(0, 2, 1)
    mats[:, :, 0:512] = Bm.reshape(DEPTH, 128, 512)
    mats[:, :, 512:1024] = Cm.reshape(DEPTH, 128, 512)
    mats[:, :, 1024:1536] = a["s5_glu_w"].reshape(DEPTH, 2, 128, 256).transpose(0, 2, 1, 3).reshape(DEPTH, 128, 512)
    arrays["matrices"] = mats
    arrays["constants"], arrays["level_masks"] = _constants()
    arrays["state_hg"] = np.ascontiguousarray(a["state_hgrn"].reshape(DEPTH, NSAMP, 3, 128, DV).transpose(0, 3, 2, 1, 4))
    rt = np.zeros((DEPTH, NSAMP, 2 * 128, DV), f)
    rt[:, :, :192] = a["state_ret"].reshape(DEPTH, NSAMP, 192, DV)
    arrays["state_rt"] = np.ascontiguousarray(rt.reshape(DEPTH, NSAMP, 2, 128, DV).transpose(0, 3, 2, 1, 4))
    s5 = np.stack([a["state_s5_re"], a["state_s5_im"]])
    arrays["state_s5"] = np.ascontiguousarray(s5.reshape(2, DEPTH, NSAMP, 8, 128).transpose(4, 1, 0, 3, 2))

    nc = bacc.Bacc("TRN2", target_bir_lowering=False, num_devices=1)
    ins = [nc.dram_tensor("in_" + n, v.shape, mybir.dt.from_np(v.dtype), kind="ExternalInput").ap() for n, v in arrays.items()]
    out_shapes = {"y": (128, KT, T), "hg_p": (DEPTH, 128, 3, DV), "rt_p": (DEPTH, 128, 2, DV), "s5_p": (DEPTH, 128, 2, 8),
                  "hg_s": (DEPTH, 128, 3, NSAMP, DV), "rt_s": (DEPTH, 128, 2, NSAMP, DV), "s5_s": (DEPTH, 128, 2, 8, NSAMP)}
    out_aps = [nc.dram_tensor("out_" + n, s, F32, kind="ExternalOutput").ap() for n, s in out_shapes.items()]
    build(nc, *ins, *out_aps)
    r = run_bass_kernel_spmd(nc, [{"in_" + n: v for n, v in arrays.items()}], core_ids=[0]).results[0]
    o = {n: np.asarray(r["out_" + n]) for n in out_shapes}
    y = o["y"].transpose(2, 1, 0).reshape(T, D_MODEL)
    hg_p = o["hg_p"].transpose(0, 2, 1, 3).reshape(DEPTH, 1, HEADS, 64, DV)
    rt_p = o["rt_p"].transpose(0, 2, 1, 3).reshape(DEPTH, 256, DV)[:, :192].reshape(DEPTH, 1, HEADS, RET_DK, DV)
    s5_p = o["s5_p"].transpose(2, 0, 3, 1).reshape(2, DEPTH, 1, 16, 64)
    hg_s = o["hg_s"].transpose(0, 3, 2, 1, 4).reshape(DEPTH, NSAMP, HEADS, 64, DV)
    rt_s = o["rt_s"].transpose(0, 3, 2, 1, 4).reshape(DEPTH, NSAMP, 256, DV)[:, :, :192].reshape(DEPTH, NSAMP, HEADS, RET_DK, DV)
    s5_s = o["s5_s"].transpose(2, 0, 4, 3, 1).reshape(2, DEPTH, NSAMP, 16, 64)
    return tuple(np.ascontiguousarray(v) for v in (
        y[:SEQ].reshape(1, SEQ, D_MODEL), y[SEQ:].reshape(NSAMP, 1, D_MODEL),
        hg_p, rt_p, s5_p[0], s5_p[1], hg_s, rt_s, s5_s[0], s5_s[1]))
```
